# Optimizing a Trainium2 kernel written in Bass

```python
import jax, jax.numpy as jnp
from jax import lax
import numpy as np

D_MODEL = 1024
BATCH = 1
SEQ = 256
DEPTH = 1

GRID_W = 64
CTX_LEN = 256
NA_HEADS = 8
NA_HEAD_DIM = 64
NA_WIDTH = NA_HEADS * NA_HEAD_DIM
WIN_H = 8
WIN_W = 16
NA_KEY_COLS = 2 * WIN_W
ML_HEADS = 4
ML_QK_DIM = 64
ML_V_DIM = 128
ML_QK_WIDTH = ML_HEADS * ML_QK_DIM
ML_WIDTH = ML_HEADS * ML_V_DIM
ML_CHUNK = 64
GATE_SOFTCAP = 15.0
ROPE_BASE = 10000.0
N_EXPERTS = 32
TOP_K = 4
D_EXPERT = D_MODEL
SWIGLU_ALPHA = 1.702
SWIGLU_LIMIT = 7.0
EXPERT_BLOCK = 128
NORM_EPS = 1e-6
NEG_INF = -1e30
CTX_SPLITS = (NA_WIDTH, NA_WIDTH, ML_QK_WIDTH, ML_WIDTH, 4 * ML_HEADS)
LAT_SPLITS = (NA_WIDTH, ML_QK_WIDTH, ML_WIDTH, D_MODEL, D_MODEL)
IN_SPLITS = CTX_SPLITS + LAT_SPLITS
N_CTX_COLS = 2 * NA_WIDTH + ML_QK_WIDTH + ML_WIDTH + 4 * ML_HEADS
N_IN_COLS = N_CTX_COLS + NA_WIDTH + ML_QK_WIDTH + ML_WIDTH + 2 * D_MODEL


def _rmsnorm(x, g):
    xf = x.astype(jnp.float32)
    y = xf * lax.rsqrt(jnp.mean(xf * xf, axis=-1, keepdims=True) + NORM_EPS)
    return (y * g.astype(jnp.float32)).astype(x.dtype)

def _split(a, sizes):
    return jnp.split(a, np.cumsum(sizes)[:-1].tolist(), axis=-1)

def _na_column_tables():
    n_qb = GRID_W // WIN_W
    qcol = np.arange(GRID_W).reshape(n_qb, WIN_W)
    kstart = np.clip(np.arange(n_qb) * WIN_W - WIN_W // 2, 0, GRID_W - NA_KEY_COLS)
    kcol = kstart[:, None] + np.arange(NA_KEY_COLS)
    cs = np.clip(qcol - WIN_W // 2, 0, GRID_W - WIN_W)
    kc = kcol[:, None, :]
    mask = (kc >= cs[:, :, None]) & (kc < cs[:, :, None] + WIN_W)
    dc = np.clip(kc - qcol[:, :, None], -(WIN_W - 1), WIN_W - 1) + (WIN_W - 1)
    return kcol, mask, dc

def _neighbourhood_attention(q, k, v, k_ctx, v_ctx, rpb):
    B, S, _ = q.shape
    rows = S // GRID_W
    wr = min(WIN_H, rows)
    n_qb = GRID_W // WIN_W
    kcol, mask, dc = _na_column_tables()
    grid = (B, rows, GRID_W, NA_HEADS, NA_HEAD_DIM)
    q = q.reshape(grid) * NA_HEAD_DIM ** -0.5
    k = k.reshape(grid)
    v = v.reshape(grid)
    k_ctx = k_ctx.reshape(B, -1, NA_HEADS, NA_HEAD_DIM)
    v_ctx = v_ctx.reshape(B, -1, NA_HEADS, NA_HEAD_DIM)
    n_loc = wr * NA_KEY_COLS

    def one_row(r):
        rs = jnp.clip(r - WIN_H // 2, 0, rows - wr)
        qb = lax.dynamic_index_in_dim(q, r, axis=1, keepdims=False).reshape(B, n_qb, WIN_W, NA_HEADS, NA_HEAD_DIM)
        kb = lax.dynamic_slice_in_dim(k, rs, wr, axis=1)[:, :, kcol]
        vb = lax.dynamic_slice_in_dim(v, rs, wr, axis=1)[:, :, kcol]
        dr = rs + jnp.arange(wr) - r + (WIN_H - 1)
        bias = rpb[:, dr[None, None, :, None], dc[:, :, None, :]].astype(jnp.float32)
        s_loc = jnp.einsum('bjqhd,brjkhd->bhjqrk', qb, kb).astype(jnp.float32) + bias
        s_loc = jnp.where(mask[:, :, None, :], s_loc, NEG_INF).reshape(B, NA_HEADS, n_qb, WIN_W, n_loc)
        s_ctx = jnp.einsum('bjqhd,bchd->bhjqc', qb, k_ctx).astype(jnp.float32)
        p = jax.nn.softmax(jnp.concatenate([s_loc, s_ctx], axis=-1), axis=-1).astype(v.dtype)
        p_loc = p[..., :n_loc].reshape(B, NA_HEADS, n_qb, WIN_W, wr, NA_KEY_COLS)
        o = (jnp.einsum('bhjqrk,brjkhd->bjqhd', p_loc, vb)
             + jnp.einsum('bhjqc,bchd->bjqhd', p[..., n_loc:], v_ctx))
        return o.reshape(B, GRID_W, NA_WIDTH)

    o = lax.map(one_row, jnp.arange(rows, dtype=jnp.int32))
    return jnp.moveaxis(o, 0, 1).reshape(B, S, NA_WIDTH)

def _axial_rope(x, row, col):
    n_freq = ML_QK_DIM // 4
    inv_freq = ROPE_BASE ** (-jnp.arange(n_freq, dtype=jnp.float32) / n_freq)

    def rotate(xh, pos):
        ang = pos[:, None] * inv_freq
        cos = jnp.cos(ang)[:, None, :]
        sin = jnp.sin(ang)[:, None, :]
        x1, x2 = xh[..., :n_freq], xh[..., n_freq:]
        return jnp.concatenate([x1 * cos - x2 * sin, x2 * cos + x1 * sin], axis=-1)

    half = ML_QK_DIM // 2
    return jnp.concatenate([rotate(x[..., :half], row), rotate(x[..., half:], col)], axis=-1)

def _to_chunks(a):
    B, H, T = a.shape[:3]
    a = a.reshape((B, H, T // ML_CHUNK, ML_CHUNK) + a.shape[3:])
    return jnp.moveaxis(a, 2, 0)

def _mlstm_chunkwise(q, k, v, log_i, log_f, state):
    tril = np.tril(np.ones((ML_CHUNK, ML_CHUNK), dtype=bool))
    with_out = q is not None

    def step(carry, inp):
        C, n, m = carry
        if with_out:
            qc, kc, vc, li, lf = inp
        else:
            kc, vc, li, lf = inp
        b = jnp.cumsum(lf, axis=-1)
        bL = b[..., -1]
        dec = bL[..., None] - b + li
        m_new = jnp.maximum(bL + m, jnp.max(dec, axis=-1))
        w_s = jnp.exp(dec - m_new[..., None])
        w_c = jnp.exp(bL + m - m_new)
        C_new = w_c[..., None, None] * C + jnp.einsum('bhs,bhsd,bhse->bhde', w_s, kc, vc)
        n_new = w_c[..., None] * n + jnp.einsum('bhs,bhsd->bhd', w_s, kc)
        if not with_out:
            return (C_new, n_new, m_new), None
        d_mat = jnp.where(tril, b[..., :, None] - b[..., None, :] + li[..., None, :], -jnp.inf)
        m_inter = b + m[..., None]
        m_t = jnp.maximum(m_inter, jnp.max(d_mat, axis=-1))
        w_intra = jnp.exp(d_mat - m_t[..., None])
        w_inter = jnp.exp(m_inter - m_t)
        s = jnp.einsum('bhtd,bhsd->bhts', qc, kc) * w_intra
        num = (w_inter[..., None] * jnp.einsum('bhtd,bhde->bhte', qc, C)
               + jnp.einsum('bhts,bhse->bhte', s, vc))
        den = w_inter * jnp.einsum('bhtd,bhd->bht', qc, n) + jnp.sum(s, axis=-1)
        h = num / jnp.maximum(jnp.abs(den), jnp.exp(-m_t))[..., None]
        return (C_new, n_new, m_new), h

    if with_out:
        xs = (_to_chunks(q), _to_chunks(k), _to_chunks(v), _to_chunks(log_i), _to_chunks(log_f))
    else:
        xs = (_to_chunks(k), _to_chunks(v), _to_chunks(log_i), _to_chunks(log_f))
    final, hs = lax.scan(step, state, xs)
    if not with_out:
        return final
    hs = jnp.moveaxis(hs, 0, 2)
    return hs.reshape(hs.shape[0], hs.shape[1], -1, hs.shape[-1])

def _mlstm_branch(q, k, v, o_pre, gates, k_ctx, v_ctx, gates_ctx, b_gates, g_head, row, col):
    B, S, _ = q.shape
    n_ctx = k_ctx.shape[1]
    f32 = jnp.float32
    qk_scale = ML_QK_DIM ** -0.5

    def heads_first(a):
        return jnp.swapaxes(a, 1, 2)

    def flip(a):
        return jnp.flip(a, axis=2)

    q = heads_first(_axial_rope(q.reshape(B, S, ML_HEADS, ML_QK_DIM).astype(f32), row, col))
    k = heads_first(_axial_rope(k.reshape(B, S, ML_HEADS, ML_QK_DIM).astype(f32), row, col) * qk_scale)
    v = heads_first(v.reshape(B, S, ML_HEADS, ML_V_DIM).astype(f32))
    k_ctx = heads_first(k_ctx.reshape(B, n_ctx, ML_HEADS, ML_QK_DIM).astype(f32) * qk_scale)
    v_ctx = heads_first(v_ctx.reshape(B, n_ctx, ML_HEADS, ML_V_DIM).astype(f32))

    def gate_logs(g):
        t = g.shape[1]
        g = g.reshape(B, t, 4, ML_HEADS).astype(f32) + b_gates.astype(f32)
        g = GATE_SOFTCAP * jnp.tanh(g / GATE_SOFTCAP)
        g = jnp.transpose(g, (2, 0, 3, 1))
        return g[0], jax.nn.log_sigmoid(g[1]), g[2], jax.nn.log_sigmoid(g[3])

    li_f, lf_f, li_b, lf_b = gate_logs(gates)
    lic_f, lfc_f, lic_b, lfc_b = gate_logs(gates_ctx)
    state0 = (jnp.zeros((B, ML_HEADS, ML_QK_DIM, ML_V_DIM), f32),
              jnp.zeros((B, ML_HEADS, ML_QK_DIM), f32),
              jnp.zeros((B, ML_HEADS), f32))
    st_f = _mlstm_chunkwise(None, k_ctx, v_ctx, lic_f, lfc_f, state0)
    h_f = _mlstm_chunkwise(q, k, v, li_f, lf_f, st_f)
    st_b = _mlstm_chunkwise(None, flip(k_ctx), flip(v_ctx), flip(lic_b), flip(lfc_b), state0)
    h_b = flip(_mlstm_chunkwise(flip(q), flip(k), flip(v), flip(li_b), flip(lf_b), st_b))
    h = heads_first(h_f + h_b)
    h = h * lax.rsqrt(jnp.mean(h * h, axis=-1, keepdims=True) + NORM_EPS) * g_head.reshape(ML_HEADS, ML_V_DIM).astype(f32)
    return (jax.nn.sigmoid(o_pre.astype(f32)) * h.reshape(B, S, ML_WIDTH)).astype(o_pre.dtype)

def _clamped_swiglu(g, l):
    g = jnp.minimum(g, SWIGLU_LIMIT)
    l = jnp.clip(l, -SWIGLU_LIMIT, SWIGLU_LIMIT)
    return g * jax.nn.sigmoid(SWIGLU_ALPHA * g) * (l + 1.0)

def _moe_ffn(h, w_router, b_router, w_gate, b_gate, w_lin, b_lin, w_down, b_down):
    B, S, D = h.shape
    n_tok = B * S
    n_assign = n_tok * TOP_K
    xf = h.reshape(n_tok, D)
    logits = (xf @ w_router + b_router).astype(jnp.float32)
    top_logit, top_e = lax.top_k(logits, TOP_K)
    top_w = jax.nn.softmax(top_logit, axis=-1)
    e_flat = top_e.reshape(-1)
    order = jnp.argsort(e_flat)
    e_sorted = e_flat[order]
    counts = jnp.bincount(e_flat, length=N_EXPERTS)
    padded = (counts + EXPERT_BLOCK - 1) // EXPERT_BLOCK * EXPERT_BLOCK
    pad_end = jnp.cumsum(padded)
    pad_start = pad_end - padded
    start = jnp.cumsum(counts) - counts
    dest = pad_start[e_sorted] + jnp.arange(n_assign) - start[e_sorted]
    n_rows = -(-n_assign // EXPERT_BLOCK) * EXPERT_BLOCK + N_EXPERTS * EXPERT_BLOCK
    n_blocks = n_rows // EXPERT_BLOCK
    row_tok = jnp.full((n_rows,), n_tok, jnp.int32).at[dest].set((order // TOP_K).astype(jnp.int32))
    row_w = jnp.zeros((n_rows,), jnp.float32).at[dest].set(top_w.reshape(-1)[order])
    blk_start = jnp.arange(n_blocks) * EXPERT_BLOCK
    blk_e = jnp.minimum(jnp.sum(blk_start[:, None] >= pad_end[None, :], axis=1), N_EXPERTS - 1)
    x_pad = jnp.concatenate([xf, jnp.zeros((1, D), xf.dtype)], axis=0)

    def expert_block(args):
        idx, wts, e = args
        xb = x_pad[idx]
        a = _clamped_swiglu(xb @ w_gate[e] + b_gate[e], xb @ w_lin[e] + b_lin[e])
        y = a @ w_down[e] + b_down[e]
        return (y * wts[:, None]).astype(h.dtype)

    y = lax.map(expert_block, (row_tok.reshape(n_blocks, EXPERT_BLOCK),
                               row_w.reshape(n_blocks, EXPERT_BLOCK), blk_e))
    out = jnp.zeros((n_tok + 1, D), h.dtype).at[row_tok].add(y.reshape(n_rows, D))
    return out[:n_tok].reshape(B, S, D)

def first_inputs(seed: int = 0) -> dict:
    key = jax.random.key(seed)
    ks = jax.random.split(key, 28)
    f32 = jnp.float32
    D, E, F = D_MODEL, N_EXPERTS, D_EXPERT

    def nrm(k, shape, scale):
        return scale * jax.random.normal(k, shape, f32)

    def gain(k, shape):
        return 1.0 + 0.02 * jax.random.normal(k, shape, f32)

    f_bias = 3.0 + 3.0 * jax.random.uniform(ks[11], (DEPTH, 2, ML_HEADS), f32)
    i_bias = nrm(ks[12], (DEPTH, 2, ML_HEADS), 0.1)
    b_mlstm_gates = jnp.stack([i_bias[:, 0], f_bias[:, 0], i_bias[:, 1], f_bias[:, 1]], axis=1)
    return {
        'x': jax.random.normal(ks[0], (BATCH, SEQ, D), f32),
        'c': jax.random.normal(ks[1], (BATCH, D), f32),
        'ctx': jax.random.normal(ks[2], (BATCH, CTX_LEN, D), f32),
        'c_ctx': jax.random.normal(ks[3], (D,), f32),
        'w_ada': nrm(ks[4], (DEPTH, D, 6 * D), 0.5 * D ** -0.5),
        'b_ada': nrm(ks[5], (DEPTH, 6 * D), 0.02),
        'g_mix_pre': gain(ks[6], (DEPTH, D)),
        'g_mix_post': gain(ks[7], (DEPTH, D)),
        'g_ffn_pre': gain(ks[8], (DEPTH, D)),
        'g_ffn_post': gain(ks[9], (DEPTH, D)),
        'w_in': nrm(ks[10], (DEPTH, D, N_IN_COLS), D ** -0.5),
        'b_mlstm_gates': b_mlstm_gates,
        'rpb': nrm(ks[13], (DEPTH, NA_HEADS, 2 * WIN_H - 1, 2 * WIN_W - 1), 0.1),
        'g_mlstm_head': gain(ks[14], (DEPTH, ML_WIDTH)),
        'w_branch_na': nrm(ks[15], (DEPTH, NA_WIDTH, D), NA_WIDTH ** -0.5),
        'w_branch_ml': nrm(ks[16], (DEPTH, ML_WIDTH, D), ML_WIDTH ** -0.5),
        'w_out': nrm(ks[17], (DEPTH, D, D), D ** -0.5),
        'w_router': nrm(ks[18], (DEPTH, D, E), D ** -0.5),
        'b_router': nrm(ks[19], (DEPTH, E), 0.01),
        'w_gate': nrm(ks[20], (DEPTH, E, D, F), D ** -0.5),
        'b_gate': nrm(ks[21], (DEPTH, E, F), 0.01),
        'w_lin': nrm(ks[22], (DEPTH, E, D, F), D ** -0.5),
        'b_lin': nrm(ks[23], (DEPTH, E, F), 0.01),
        'w_down': nrm(ks[24], (DEPTH, E, F, D), F ** -0.5),
        'b_down': nrm(ks[25], (DEPTH, E, D), 0.01),
    }

def first_block(x, c, ctx, c_ctx, w_ada, b_ada, g_mix_pre, g_mix_post, g_ffn_pre, g_ffn_post,
              w_in, b_mlstm_gates, rpb, g_mlstm_head, w_branch_na, w_branch_ml, w_out,
              w_router, b_router, w_gate, b_gate, w_lin, b_lin, w_down, b_down):
    B, S, D = x.shape
    t = jnp.arange(S)
    row = (t // GRID_W).astype(jnp.float32)
    col = (t % GRID_W).astype(jnp.float32)
    silu_c = jax.nn.silu(c)
    silu_cc = jax.nn.silu(c_ctx)
    for layer in range(DEPTH):
        mod = silu_c @ w_ada[layer] + b_ada[layer]
        sh_m, sc_m, gt_m, sh_f, sc_f, gt_f = jnp.split(mod, 6, axis=-1)
        mod_c = silu_cc @ w_ada[layer][:, :2 * D] + b_ada[layer][:2 * D]
        sh_c, sc_c = jnp.split(mod_c, 2, axis=-1)

        h = _rmsnorm(x, g_mix_pre[layer]) * (1.0 + sc_m[:, None]) + sh_m[:, None]
        hc = _rmsnorm(ctx, g_mix_pre[layer]) * (1.0 + sc_c) + sh_c
        (na_k, na_v, ml_k, ml_v, ml_g, na_q, ml_q, ml_o, gate_na, gate_ml) = _split(h @ w_in[layer], IN_SPLITS)
        (na_kc, na_vc, ml_kc, ml_vc, ml_gc) = _split(hc @ w_in[layer][:, :N_CTX_COLS], CTX_SPLITS)
        o_na = _neighbourhood_attention(na_q, na_k, na_v, na_kc, na_vc, rpb[layer])
        o_ml = _mlstm_branch(ml_q, ml_k, ml_v, ml_o, ml_g, ml_kc, ml_vc, ml_gc,
                             b_mlstm_gates[layer], g_mlstm_head[layer], row, col)
        merged = (jax.nn.sigmoid(gate_na) * (o_na @ w_branch_na[layer])
                  + jax.nn.sigmoid(gate_ml) * (o_ml @ w_branch_ml[layer]))
        x = x + gt_m[:, None] * _rmsnorm(merged @ w_out[layer], g_mix_post[layer])

        h2 = _rmsnorm(x, g_ffn_pre[layer]) * (1.0 + sc_f[:, None]) + sh_f[:, None]
        ffn = _moe_ffn(h2, w_router[layer], b_router[layer], w_gate[layer], b_gate[layer],
                       w_lin[layer], b_lin[layer], w_down[layer], b_down[layer])
        x = x + gt_f[:, None] * _rmsnorm(ffn, g_ffn_post[layer])
    return x


DEPTH_2 = 2

CONV_DIM = 512
CONV_WIDTH = 3
RET_HEADS = 4
RET_HEAD_DIM = 128
RET_DIM = RET_HEADS * RET_HEAD_DIM
GLA_HEADS = 4
GLA_KEY_HEAD_DIM = 64
GLA_VAL_HEAD_DIM = 128
GLA_KEY_DIM = GLA_HEADS * GLA_KEY_HEAD_DIM
GLA_VAL_DIM = GLA_HEADS * GLA_VAL_HEAD_DIM
GLA_GATE_RANK = 16
GLA_GATE_TAU = 16.0
N_BRANCHES = 3
CHUNK = 64
D_FF = (((8 * D_MODEL + 2) // 3 + 255) // 256) * 256
EPS = 1e-6
IN_COLS = 3 * CONV_DIM + 4 * RET_DIM + 2 * GLA_KEY_DIM + 2 * GLA_VAL_DIM + GLA_GATE_RANK + N_BRANCHES * D_MODEL


def rms_norm(x, w):
    xf = x.astype(jnp.float32)
    y = xf * lax.rsqrt(jnp.mean(xf * xf, axis=-1, keepdims=True) + EPS)
    return (y * w.astype(jnp.float32)).astype(x.dtype)

def head_norm(y, w, center):
    b, t, h, d = y.shape
    if center:
        y = y - jnp.mean(y, axis=-1, keepdims=True)
    y = y * lax.rsqrt(jnp.mean(y * y, axis=-1, keepdims=True) + EPS)
    return y.reshape(b, t, h * d) * w.astype(jnp.float32)

def rotary(x, positions):
    half = x.shape[-1] // 2
    inv_freq = ROPE_BASE ** (-jnp.arange(half, dtype=jnp.float32) / half)
    ang = positions.astype(jnp.float32)[..., None] * inv_freq
    cos = jnp.cos(ang)[:, :, None, :]
    sin = jnp.sin(ang)[:, :, None, :]
    x1, x2 = x[..., :half], x[..., half:]
    return jnp.concatenate([x1 * cos - x2 * sin, x2 * cos + x1 * sin], axis=-1)

def to_chunks(x):
    b, t, h, d = x.shape
    return x.reshape(b, t // CHUNK, CHUNK, h, d).transpose(1, 0, 3, 2, 4)

def from_chunks(x):
    nc, b, h, c, d = x.shape
    return x.transpose(1, 0, 3, 2, 4).reshape(b, nc * c, h, d)

def short_conv(u, b_gate, c_gate, conv_w):
    z = c_gate * u
    t = z.shape[1]
    zp = jnp.pad(z, ((0, 0), (CONV_WIDTH - 1, 0), (0, 0)))
    y = sum(conv_w[i] * zp[:, i:i + t, :] for i in range(CONV_WIDTH))
    return b_gate * y

def retention(q, k, v):
    b, t, h, dk = q.shape
    dv = v.shape[-1]
    log_g = jnp.log(1.0 - 2.0 ** (-5.0 - jnp.arange(h, dtype=jnp.float32)))
    idx = jnp.arange(CHUNK, dtype=jnp.float32)
    diff = idx[:, None] - idx[None, :]
    causal = diff >= 0
    decay_mask = jnp.where(causal, jnp.exp(log_g[:, None, None] * jnp.maximum(diff, 0.0)), 0.0)
    q_decay = jnp.exp(log_g[:, None] * (idx + 1.0))[None, :, :, None]
    k_decay = jnp.exp(log_g[:, None] * (CHUNK - 1.0 - idx))[None, :, :, None]
    chunk_decay = jnp.exp(log_g * CHUNK)[None, :, None, None]
    q = q * (dk ** -0.5)

    def step(state, inp):
        qi, ki, vi = inp
        s = jnp.einsum('bhid,bhjd->bhij', qi, ki) * decay_mask
        intra = jnp.einsum('bhij,bhjv->bhiv', s, vi)
        inter = jnp.einsum('bhid,bhdv->bhiv', qi * q_decay, state)
        new_state = state * chunk_decay + jnp.einsum('bhjd,bhjv->bhdv', ki * k_decay, vi)
        return new_state, intra + inter

    state0 = jnp.zeros((b, h, dk, dv), jnp.float32)
    _, out = lax.scan(step, state0, (to_chunks(q), to_chunks(k), to_chunks(v)))
    return from_chunks(out)

def gated_linear_attention(q, k, v, log_a):
    b, t, h, dk = q.shape
    dv = v.shape[-1]
    q = q * (dk ** -0.5)
    tril = jnp.tril(jnp.ones((CHUNK, CHUNK), dtype=bool))[None, None, :, :, None]

    def step(state, inp):
        qi, ki, vi, gi = inp
        cum = jnp.cumsum(gi, axis=2)
        rel = cum[:, :, :, None, :] - cum[:, :, None, :, :]
        pair_decay = jnp.where(tril, jnp.exp(jnp.where(tril, rel, 0.0)), 0.0)
        s = jnp.einsum('bhid,bhjd,bhijd->bhij', qi, ki, pair_decay)
        intra = jnp.einsum('bhij,bhjv->bhiv', s, vi)
        inter = jnp.einsum('bhid,bhdv->bhiv', qi * jnp.exp(cum), state)
        last = cum[:, :, -1:, :]
        new_state = state * jnp.exp(last)[:, :, 0, :, None] + jnp.einsum(
            'bhjd,bhjv->bhdv', ki * jnp.exp(last - cum), vi)
        return new_state, intra + inter

    state0 = jnp.zeros((b, h, dk, dv), jnp.float32)
    _, out = lax.scan(step, state0, (to_chunks(q), to_chunks(k), to_chunks(v), to_chunks(log_a)))
    return from_chunks(out)

def split_columns(proj):
    sizes = ([CONV_DIM] * 3 + [RET_DIM] * 4
             + [GLA_KEY_DIM, GLA_KEY_DIM, GLA_VAL_DIM, GLA_VAL_DIM, GLA_GATE_RANK]
             + [D_MODEL] * N_BRANCHES)
    offsets = [int(o) for o in np.cumsum(sizes)[:-1]]
    return jnp.split(proj, offsets, axis=-1)

def mixer_block(h, positions, w_in, conv_w, ret_gn_w, gla_w_a2, gla_b_a, gla_gn_w,
                w_branch_a, w_branch_b, w_branch_c, w_out):
    bsz, t, _ = h.shape
    proj = (h @ w_in).astype(jnp.float32)
    (cu, cb, cc, rq, rk, rv, rg, gq, gk, gv, gr, ga_down,
     gate_a, gate_b, gate_c) = split_columns(proj)

    y_a = short_conv(cu, cb, cc, conv_w.astype(jnp.float32))

    rq = rotary(rq.reshape(bsz, t, RET_HEADS, RET_HEAD_DIM), positions)
    rk = rotary(rk.reshape(bsz, t, RET_HEADS, RET_HEAD_DIM), positions)
    rv = rv.reshape(bsz, t, RET_HEADS, RET_HEAD_DIM)
    y_b = head_norm(retention(rq, rk, rv), ret_gn_w, center=True) * jax.nn.silu(rg)

    gate_logits = ga_down @ gla_w_a2.astype(jnp.float32) + gla_b_a.astype(jnp.float32)
    log_a = (jax.nn.log_sigmoid(gate_logits) / GLA_GATE_TAU).reshape(bsz, t, GLA_HEADS, GLA_KEY_HEAD_DIM)
    gq = gq.reshape(bsz, t, GLA_HEADS, GLA_KEY_HEAD_DIM)
    gk = gk.reshape(bsz, t, GLA_HEADS, GLA_KEY_HEAD_DIM)
    gv = gv.reshape(bsz, t, GLA_HEADS, GLA_VAL_HEAD_DIM)
    y_c = head_norm(gated_linear_attention(gq, gk, gv, log_a), gla_gn_w, center=False) * jax.nn.silu(gr)

    merged = (jax.nn.sigmoid(gate_a) * (y_a @ w_branch_a.astype(jnp.float32))
              + jax.nn.sigmoid(gate_b) * (y_b @ w_branch_b.astype(jnp.float32))
              + jax.nn.sigmoid(gate_c) * (y_c @ w_branch_c.astype(jnp.float32)))
    return (merged @ w_out.astype(jnp.float32)).astype(h.dtype)

def swiglu(h, w_gate, w_up, w_down):
    return (jax.nn.silu(h @ w_gate) * (h @ w_up)) @ w_down

def second_inputs(seed: int = 0) -> dict:
    key = jax.random.key(seed)
    ks = jax.random.split(key, 20)
    f32 = jnp.float32

    def normal(k, shape, scale):
        return jax.random.normal(k, shape, f32) * scale

    def gain(k, shape):
        return 1.0 + 0.1 * jax.random.normal(k, shape, f32)

    return {
        "x": normal(ks[0], (BATCH, SEQ, D_MODEL), 1.0),
        "positions": jnp.broadcast_to(jnp.arange(SEQ, dtype=jnp.int32), (BATCH, SEQ)),
        "norm_mix_pre": gain(ks[1], (DEPTH_2, D_MODEL)),
        "w_in": normal(ks[2], (DEPTH_2, D_MODEL, IN_COLS), D_MODEL ** -0.5),
        "conv_w": normal(ks[3], (DEPTH_2, CONV_WIDTH, CONV_DIM), CONV_WIDTH ** -0.5),
        "ret_gn_w": gain(ks[4], (DEPTH_2, RET_DIM)),
        "gla_w_a2": normal(ks[5], (DEPTH_2, GLA_GATE_RANK, GLA_KEY_DIM), GLA_GATE_RANK ** -0.5),
        "gla_b_a": normal(ks[6], (DEPTH_2, GLA_KEY_DIM), 0.1),
        "gla_gn_w": gain(ks[7], (DEPTH_2, GLA_VAL_DIM)),
        "w_branch_a": normal(ks[8], (DEPTH_2, CONV_DIM, D_MODEL), CONV_DIM ** -0.5),
        "w_branch_b": normal(ks[9], (DEPTH_2, RET_DIM, D_MODEL), RET_DIM ** -0.5),
        "w_branch_c": normal(ks[10], (DEPTH_2, GLA_VAL_DIM, D_MODEL), GLA_VAL_DIM ** -0.5),
        "w_out": normal(ks[11], (DEPTH_2, D_MODEL, D_MODEL), D_MODEL ** -0.5),
        "norm_mix_post": gain(ks[12], (DEPTH_2, D_MODEL)),
        "norm_ffn_pre": gain(ks[13], (DEPTH_2, D_MODEL)),
        "w_ffn_gate": normal(ks[14], (DEPTH_2, D_MODEL, D_FF), D_MODEL ** -0.5),
        "w_ffn_up": normal(ks[15], (DEPTH_2, D_MODEL, D_FF), D_MODEL ** -0.5),
        "w_ffn_down": normal(ks[16], (DEPTH_2, D_FF, D_MODEL), D_FF ** -0.5),
        "norm_ffn_post": gain(ks[17], (DEPTH_2, D_MODEL)),
    }

def second_block(x, positions, norm_mix_pre, w_in, conv_w, ret_gn_w, gla_w_a2, gla_b_a, gla_gn_w,
              w_branch_a, w_branch_b, w_branch_c, w_out, norm_mix_post, norm_ffn_pre,
              w_ffn_gate, w_ffn_up, w_ffn_down, norm_ffn_post):
    for layer in range(DEPTH_2):
        h = rms_norm(x, norm_mix_pre[layer])
        m = mixer_block(h, positions, w_in[layer], conv_w[layer], ret_gn_w[layer], gla_w_a2[layer],
                        gla_b_a[layer], gla_gn_w[layer], w_branch_a[layer], w_branch_b[layer],
                        w_branch_c[layer], w_out[layer])
        x = x + rms_norm(m, norm_mix_post[layer]).astype(x.dtype)
        h = rms_norm(x, norm_ffn_pre[layer])
        f = swiglu(h, w_ffn_gate[layer], w_ffn_up[layer], w_ffn_down[layer])
        x = x + rms_norm(f, norm_ffn_post[layer]).astype(x.dtype)
    return x


def setup_inputs(seed=0):
    out = dict(first_inputs(seed))
    for name, value in second_inputs(seed + 1).items():
        if name != "x":
            out[name + "_2"] = value
    return out


def reference(
    x, c, ctx, c_ctx, w_ada, b_ada, g_mix_pre, g_mix_post, g_ffn_pre, g_ffn_post, w_in,
    b_mlstm_gates, rpb, g_mlstm_head, w_branch_na, w_branch_ml, w_out, w_router, b_router,
    w_gate, b_gate, w_lin, b_lin, w_down, b_down, positions_2, norm_mix_pre_2, w_in_2, conv_w_2,
    ret_gn_w_2, gla_w_a2_2, gla_b_a_2, gla_gn_w_2, w_branch_a_2, w_branch_b_2, w_branch_c_2,
    w_out_2, norm_mix_post_2, norm_ffn_pre_2, w_ffn_gate_2, w_ffn_up_2, w_ffn_down_2,
    norm_ffn_post_2,
):
    x = first_block(
        x, c, ctx, c_ctx, w_ada, b_ada, g_mix_pre, g_mix_post, g_ffn_pre, g_ffn_post, w_in,
        b_mlstm_gates, rpb, g_mlstm_head, w_branch_na, w_branch_ml, w_out, w_router, b_router,
        w_gate, b_gate, w_lin, b_lin, w_down, b_down,
    )
    return second_block(
        x, positions_2, norm_mix_pre_2, w_in_2, conv_w_2, ret_gn_w_2, gla_w_a2_2, gla_b_a_2,
        gla_gn_w_2, w_branch_a_2, w_branch_b_2, w_branch_c_2, w_out_2, norm_mix_post_2,
        norm_ffn_pre_2, w_ffn_gate_2, w_ffn_up_2, w_ffn_down_2, norm_ffn_post_2,
    )


_drawn_inputs = setup_inputs


def setup_inputs(seed=0):
    import zlib

    import numpy as np

    out = dict(_drawn_inputs(seed))
    spreads = {}
    factors = {'g_ffn_post': 3.817, 'b_gate': 8.0, 'b_lin': 8.0, 'b_down': 8.0, 'gla_b_a_2': 3.249}
    for name, (base, spread) in spreads.items():
        noise = np.random.default_rng([zlib.crc32(name.encode()), seed]).standard_normal(out[name].shape)
        drawn = base * np.exp(spread * noise) if base else spread * noise
        out[name] = __import__('jax').numpy.asarray(drawn.astype(out[name].dtype))
    for name, factor in factors.items():
        out[name] = (out[name] * factor).astype(out[name].dtype)
    return out
```

```python
from contextlib import ExitStack

import numpy as np
import concourse.bass as bass
from concourse import mybir

F32 = mybir.dt.float32
I32 = mybir.dt.int32
U32 = mybir.dt.uint32
ALU = mybir.AluOpType
ACT = mybir.ActivationFunctionType
AX = mybir.AxisListType

P = 128
D = 1024
DC = D // P
T = 256
TT = T // P
GRID_W = 64
WIN_W = 16
NA_H, NA_D = 8, 64
ML_H, ML_D, ML_V = 4, 64, 128
E, TOPK = 32, 4
EPS = 1e-6
NEG = -1e30
SOFTCAP = 15.0
ALPHA, LIMIT = 1.702, 7.0
SLOTS = 64
MAXPASS = T // SLOTS
RH, RD = 4, 128
GH, GD, GV, GR = 4, 64, 128, 16
TAU = 16.0
FF = 2816
FC = FF // P
RING = 6
ARENA = 23760
LINKS = 55
MAGIC = 12582912.0
TURN = (6.28125, float(np.float32(2 * np.pi - 6.28125)),
        float(np.float32(2 * np.pi - 6.28125 - float(np.float32(2 * np.pi - 6.28125)))))
PI_IN = 3.1415925
SLAB = DC * 512

VECS1 = {}
_n = 0
for _name, _k in (("c", 8), ("c_ctx", 8), ("b_ada", 48), ("g_mix_pre", 8), ("g_mix_post", 8), ("g_ffn_pre", 8),
                  ("g_ffn_post", 8), ("g_mlstm_head", 4)):
    VECS1[_name] = (_n, _k)
    _n += _k
NV1 = _n
VECS2 = {}
_n = 0
for _name, _k in (("norm_mix_pre_2", 8), ("conv_w_2", 12), ("ret_gn_w_2", 4), ("gla_b_a_2", 2), ("gla_gn_w_2", 4),
                  ("norm_mix_post_2", 8), ("norm_ffn_pre_2", 8), ("norm_ffn_post_2", 8)):
    VECS2[_name] = (_n, _k)
    _n += _k
NV2 = _n

C_NAK, C_NAV, C_MLK, C_MLV, C_MLG = 0, 512, 1024, 1280, 1792
C_NAQ, C_MLQ, C_MLO, C_GNA, C_GML = 1808, 2320, 2576, 3088, 4112
C2 = {"cu": 0, "cb": 512, "cc": 1024, "rq": 1536, "rk": 2048, "rv": 2560, "rg": 3072, "gq": 3584, "gk": 3840,
      "gv": 4096, "gr": 4608, "ga": 5120, "ga0": 5136, "ga1": 5648, "gb0": 6160, "gb1": 6672, "gc0": 7184, "gc1": 7696}


def constants():
    f = np.float32
    i = np.arange(P)
    t = np.arange(T)
    out = {}
    out["ident"] = np.eye(P, dtype=f)
    out["tri"] = (i[:, None] <= t[None, :]).astype(f)
    out["ltri"] = (i[:, None] >= (t[None, :] - P)).astype(f)
    out["maskf"] = np.where(i[:, None] <= i[None, :], 0.0, NEG).astype(f)
    out["maskb"] = np.where(i[:, None] >= i[None, :], 0.0, NEG).astype(f)
    for name, half in (("rot16", 16), ("rot64", 64)):
        m = np.zeros((P, P), f)
        for a in range(P):
            if a % (2 * half) < half:
                m[a + half, a] = -1.0
            else:
                m[a - half, a] = 1.0
        out[name] = m
    nf = ML_D // 4
    inv = (f(10000.0) ** (-np.arange(nf, dtype=f) / f(nf))).astype(f)
    d = i % ML_D
    pos = np.where(d[:, None] < ML_D // 2, (t // GRID_W)[None, :], (t % GRID_W)[None, :]).astype(f)
    ang = (pos * inv[d % nf][:, None]).astype(f)
    out["cos1"] = np.cos(ang).astype(f)
    out["sin1"] = np.sin(ang).astype(f)
    c = np.arange(GRID_W)
    start = np.clip(c - WIN_W // 2, 0, GRID_W - WIN_W)
    inwin = (c[:, None] >= start[None, :]) & (c[:, None] < start[None, :] + WIN_W)
    rel = np.zeros((P, GRID_W, P), f)
    for a in range(2):
        for kc in range(GRID_W):
            for q in range(GRID_W):
                if inwin[kc, q]:
                    rel[31 * a + kc - q + 15, kc, 64 * a + q] = 1.0
                else:
                    rel[62, kc, 64 * a + q] = NEG
    out["rel"] = rel.reshape(P, GRID_W * P)
    out["iota"] = np.tile(np.arange(64, dtype=f), (P, 1))
    h = np.arange(RH, dtype=f)
    log_g = np.log(1.0 - 2.0 ** (-5.0 - h.astype(np.float64)))
    diff = (t[None, :] - i[:, None])[:, None, :]
    dec = np.where(diff >= 0, np.exp(log_g[None, :, None] * np.maximum(diff, 0)), 0.0) * RD ** -0.5
    out["center"] = (np.eye(P) - 1.0 / P).astype(f)
    out["retmask"] = dec.astype(f).reshape(P, RH * T)
    half = RD // 2
    out["invfreq"] = (f(10000.0) ** (-np.arange(half, dtype=f) / f(half))).astype(f)[i % half][:, None].copy()
    return out


CONST_SHAPES = {"ident": P, "tri": T, "ltri": T, "maskf": P, "maskb": P, "rot16": P, "rot64": P, "cos1": T, "sin1": T,
                "iota": 64, "center": P, "retmask": RH * T, "invfreq": 1}


def build(nc, A, out):
    with ExitStack() as ctx:
        def sb(name, shape, dt=F32):
            return ctx.enter_context(nc.sbuf_tensor(name, shape, dt))

        def sem(name):
            return ctx.enter_context(nc.semaphore(name))

        bank = [ctx.enter_context(nc.psum_tensor(f"bank{i}", [P, 512], F32)) for i in range(8)]

        ring = sb("ring", [P, RING * SLAB])
        K = {n: sb("k_" + n, [P, w]) for n, w in CONST_SHAPES.items() if n not in ("retmask", "center", "cos1", "sin1")}
        K["cos1"], K["sin1"] = sb("k_cos1", [P, T]), sb("k_sin1", [P, T])
        ones = sb("ones", [P, T])
        xT = sb("xT", [P, DC, T])
        vT = sb("vT", [P, NV1])
        v2T = sb("v2T", [P, 2 * NV2])
        mod = sb("mod", [P, 48])
        modc = sb("modc", [P, 16])
        gains = sb("gains", [P, 2, DC])
        stage = sb("stage", [P, 64])
        colA = sb("colA", [P, 8])
        scol = sb("scol", [P, DC, 2])
        arenaA = sb("arenaA", [P, ARENA])

        def carve(*shapes):
            at, got = 0, []
            for s in shapes:
                n = int(np.prod(s))
                v = arenaA[:, at:at + n]
                if len(s) == 2:
                    v = v.rearrange("p (a b) -> p a b", a=s[0])
                if len(s) == 3:
                    v = v.rearrange("p (a b c) -> p a b c", a=s[0], b=s[1])
                got.append(v)
                at += n
            assert at <= ARENA, at
            return got

        (hAll, naK, naV, mlK, mlV, naQ, mlQ, mlO, gNA, gML, bias, Pna, PT, gate, small) = carve(
            (DC, 512), (4, 512), (4, 512), (2, 512), (4 * ML_H, 129), (4, T), (2, T), (4, T), (DC, T), (DC, T),
            (48, 64), (2, 512), (4, T), (4, 16), (640,))
        rstd = Pna[:, 0, :]
        ropeT = PT[:, 0:2, :].rearrange("p a b -> p (a b)")
        xin = arenaA[:, 8 * 512:8 * 512 + 4096].rearrange("p (a b) -> p a b", a=4)
        at = 8 * 512 + 4096 + 1024 + 16 * 129 + 1024 + 512 + 1024
        sq = arenaA[:, at:at + 4096].rearrange("p (a b) -> p a b", a=DC)
        wml = arenaA[:, at + 4096:at + 4096 + 2 * 896].rearrange("p (a b) -> p a b", a=2)
        hml = arenaA[:, at + 4096 + 1792:at + 4096 + 1792 + 1024].rearrange("p (a b) -> p a b", a=2)
        oNaT = naQ
        oMlT = naK[:, 0:2, :].rearrange("p a b -> p (a b)").rearrange("p (a b) -> p a b", a=4)
        merged = hAll[:, 0:4, :].rearrange("p a b -> p (a b)").rearrange("p (a b) -> p a b", a=DC)
        mixT = hAll[:, 4:8, :].rearrange("p a b -> p (a b)").rearrange("p (a b) -> p a b", a=DC)
        vin = small[:, 0:128]
        vin2 = small[:, 128:256]
        relrhs = small[:, 256:304]
        lfb = small[:, 304:320]
        keyb = small[:, 320:352].rearrange("p (a b) -> p a b", a=4)
        gt1 = small[:, 352:384].rearrange("p (a b) -> p a b", a=4)
        gt2 = small[:, 384:416].rearrange("p (a b) -> p a b", a=4)
        bg = small[:, 416:432]
        lsg = small[:, 432:464].rearrange("p (a b) -> p a b", a=4)
        nst = small[:, 464:560]

        def at(off, *shape):
            n = int(np.prod(shape))
            v = arenaA[:, off:off + n]
            if len(shape) == 2:
                v = v.rearrange("p (a b) -> p a b", a=shape[0])
            return v

        h2T = at(0, DC, T)
        accT = at(2048, DC, T)
        h2N = at(4096, TT, D)
        braw = at(6144, 2, D)
        bgT, blT = at(8192, DC, E), at(8448, DC, E)
        bdraw = at(8704, D)
        wr = at(9728, DC, E)
        brow = at(9984, E)
        logits = at(10016, TT, E)
        chosen = at(10080, TT, E)
        weight = at(10144, TT, E)
        place0 = at(10208, TT, E)
        place = at(10272, TT, MAXPASS * E)
        weightT = at(10528, T)
        selS = at(10784, 2, TT * SLOTS).rearrange("p a (t s) -> p a t s", t=TT)
        selW = at(11040, TT, 2 * SLOTS)
        selWT = at(11296, T)
        top = at(11552, TT, 8)
        topi = at(11568, TT, 8)
        topf = at(11584, TT, 8)
        topp = at(11600, TT, 8)
        tmpe = at(11616, TT, E)
        rcol = at(11680, 16)
        sq2 = at(13840, DC, T)
        tmpx = at(15888, DC, T)
        xe = at(17936, 2, DC * SLOTS).rearrange("p a (c s) -> p a c s", c=DC)
        eg, el, es, ea = [at(18960 + 512 * k, DC, SLOTS) for k in range(4)]
        yT = at(21008, DC, 2 * SLOTS)
        yN = at(22032, D)
        npass_sb = sb("npass_sb", [P, 1], I32)
        gpost = sb("gpost", [P, DC])
        gpre = sb("gpre", [P, DC])
        ncol = sb("ncol", [P, 2])

        hT = at(0, DC, T)
        mergedC = at(2048, DC, T)
        headY, headSq = at(2048, 4, T), at(3072, 4, T)
        convU, convB, convC = at(4096, 4, T), at(5120, 4, T), at(6144, 4, T)
        yA = convC
        retQ, retK, retV, retG = at(7168, 4, T), at(8192, 4, T), at(9216, TT, 512), at(10240, 4, T)
        yB, yC = retQ, retK
        glaQ, glaK, glaV = at(11264, 2, T), at(11776, 2, T), at(12288, TT, 512)
        glaA = at(13312, T)
        glaEk = at(13568, 2, 64)
        glaNeg = at(13696, 2, 4)
        glaPos = at(13704, 2, 4)
        hcol = at(13712, 8)
        gateA, gateB, gateC = at(13840, DC, T), at(15888, DC, T), at(4096, DC, T)
        mixC = at(9216, DC, T)
        glaR = at(17936, 4, T)
        cos2, sin2 = at(18960, T), at(19216, T)
        retP = at(19472, 2, 384)
        glaCum = at(20240, 2, T)
        glaEq = at(20752, 2, T)
        glaP = at(21264, 2, 384)
        retmask = at(22032, RH, T)
        wa2 = at(23056, T)
        center = at(23312, P)
        lgt = at(2048, 2, T)
        lab = at(2560, 2, T)
        lln = at(3072, 2, T)
        fT = at(4096, FC, T)
        fS = at(9728, 4, 512)
        ffT = at(2048, DC, T)
        posi, posf, ang, kf = [at(2048 + 256 * k, T) for k in range(4)]
        v2c = sb("v2c", [P, NV2])
        V2 = lambda n: v2c[:, VECS2[n][0]:VECS2[n][0] + VECS2[n][1]]
        outN = at(4096, TT, D)

        slabs2 = [(n, ("w_in_2", 8, C2[n], w)) for n, w in (
            ("cu", 512), ("cb", 512), ("cc", 512), ("rq", 512), ("rk", 512), ("rv", 512), ("rg", 512), ("gq", 256),
            ("gk", 256), ("gv", 512), ("gr", 512), ("ga", 16), ("ga0", 512), ("ga1", 512), ("gb0", 512), ("gb1", 512),
            ("gc0", 512), ("gc1", 512))]
        slabs2 += [(f"br{x}", (f"w_branch_{x}_2", 4, 0, 1024)) for x in "abc"]
        slabs2 += [(f"out{i}", ("w_out_2", 8, 512 * i, 512)) for i in range(2)]
        for i in range(6):
            w = min(512, FF - 512 * i)
            slabs2 += [(f"fg{i}", ("w_ffn_gate_2", 8, 512 * i, w)), (f"fu{i}", ("w_ffn_up_2", 8, 512 * i, w))]
        DOWN = [(0, 4)] + [(4 + 3 * k, 3) for k in range(6)]
        slabs2 += [(f"fd{i}", ("w_ffn_down_2", k, c0 * P, 1024)) for i, (c0, k) in enumerate(DOWN)]
        N2 = len(slabs2)
        assert N2 % RING == 0
        S2 = {n: k for k, (n, _) in enumerate(slabs2)}
        groups2 = []
        for n, k in (("cu", 2), ("cb", 2), ("cc", 2), ("rq", 2), ("rk", 2), ("rv", 2), ("rg", 2), ("gq", 1), ("gk", 1),
                     ("gv", 2), ("gr", 2), ("ga", 1)):
            groups2 += [("act", n, f"{n}_{i}") for i in range(k)]
        for x in "abc":
            groups2 += [("act", f"g{x}{i // 2}", f"gate{x}_{i}") for i in range(4)]
        for x in "abc":
            groups2 += [("dve", f"br{x}", f"br{x}_{i}") for i in range(4)]
        groups2 += [("act", f"out{i // 2}", f"out_{i}") for i in range(4)]
        for i in range(6):
            groups2 += [("act", f"fg{i}", f"fg_{2 * i + k}") for k in range(2 if i < 5 else 1)]
            groups2 += [("dve", f"fu{i}", f"fu_{2 * i + k}") for k in range(2 if i < 5 else 1)]
        groups2 += [("none", f"fd{i}", f"fd_{i}") for i in range(len(DOWN))]
        G2 = {n: k for k, (_, _, n) in enumerate(groups2)}
        NG2 = len(groups2)
        NACT2 = sum(b == "act" for b, _, _ in groups2)
        NDVE2 = sum(b == "dve" for b, _, _ in groups2)

        def emptied2(g, L):
            by = groups2[g][0]
            n = sum(b == by for b, _, _ in groups2[:g + 1])
            return (c_act, L * NACT2 + n) if by == "act" else (c_dve, L * NDVE2 + n)

        def made2(name, L):
            return c_lin, L * NG2 + (NG2 + G2[name] + 1)

        c_in = [sem(f"c_in{i}") for i in range(RING)]
        c_lin, c_act, c_dve, c_h, c_vec, c_chain = [sem(n) for n in ("c_lin", "c_act", "c_dve", "c_h", "c_vec", "c_chain")]
        c_const, c_pos, c_sin, c_rot, c_rope, c_conv = [sem(n) for n in ("c_const", "c_pos", "c_sin", "c_rot", "c_rope", "c_conv")]
        c_wa2, c_lg, c_abs, c_exp, c_ln, c_cum = [sem(n) for n in ("c_wa2", "c_lg", "c_abs", "c_exp", "c_ln", "c_cum")]
        r_s, r_p, r_o, r_oc, r_c, r_cc = [sem(n) for n in ("r_s", "r_p", "r_o", "r_oc", "r_c", "r_cc")]
        h_sum, h_ms, h_root, h_col, h_row, h_y = [sem(n) for n in ("h_sum", "h_ms", "h_root", "h_col", "h_row", "h_y")]
        l_e, l_q, l_s, l_p = [sem(n) for n in ("l_e", "l_q", "l_s", "l_p")]
        fin_t, fin_c = sem("fin_t"), sem("fin_c")
        vecs2_turned = sem("vecs2_turned")
        v2_copied = sem("v2_copied")
        n_sq = sem("n_sq")
        n_sum = sem("n_sum")
        n_ms = sem("n_ms")
        n_root = sem("n_root")
        n_col = sem("n_col")
        n_row = sem("n_row")
        n_xn = sem("n_xn")
        x_done = sem("x_done")
        h2_done = sem("h2_done")
        h2_turned = sem("h2_turned")
        h2_copied = sem("h2_copied")
        moe_const = sem("moe_const")
        rt_log = sem("rt_log")
        rt_top = sem("rt_top")
        rt_exp = sem("rt_exp")
        rt_sel = sem("rt_sel")
        rt_cnt = sem("rt_cnt")
        rt_wt = sem("rt_wt")
        rt_wts = sem("rt_wts")
        b_turned = sem("b_turned")
        b_copied = sem("b_copied")
        acc_ps = sem("acc_ps")
        acc_set = sem("acc_set")
        npass_set = sem("npass_set")
        moe_in = [sem(f"moe_in{i}") for i in range(RING)]
        moe_used = sem("moe_used")
        moe_sel = sem("moe_sel")
        moe_x = sem("moe_x")
        moe_xs = sem("moe_xs")
        moe_gr = sem("moe_gr")
        moe_g2 = sem("moe_g2")
        moe_sig = sem("moe_sig")
        moe_lr = sem("moe_lr")
        moe_l2 = sem("moe_l2")
        moe_l3 = sem("moe_l3")
        moe_a = sem("moe_a")
        moe_ys = sem("moe_ys")
        moe_swt = sem("moe_swt")
        moe_swts = sem("moe_swts")
        moe_yt = sem("moe_yt")
        moe_y2 = sem("moe_y2")
        moe_sc = sem("moe_sc")
        moe_add = sem("moe_add")
        consts_in = sem("consts_in")
        x_in = sem("x_in")
        vec_in = sem("vec_in")
        slab_in = [sem(f"slab_in{i}") for i in range(RING)]
        out_done = sem("out_done")
        ones_set = sem("ones_set")
        vecs_turned = sem("vecs_turned")
        vecs_copied = sem("vecs_copied")
        x_turned = sem("x_turned")
        x_copied = sem("x_copied")
        relrhs_in = sem("relrhs_in")
        bg_in = sem("bg_in")
        rel_done = sem("rel_done")
        rel_copied = sem("rel_copied")
        silu_done = sem("silu_done")
        sig_c = sem("sig_c")
        ada_done = sem("ada_done")
        gains_done = sem("gains_done")
        mod_done = sem("mod_done")
        sq_done = sem("sq_done")
        sum_done = sem("sum_done")
        ms_done = sem("ms_done")
        root_done = sem("root_done")
        rstd_done = sem("rstd_done")
        rstd_row = sem("rstd_row")
        xn_done = sem("xn_done")
        h_done = sem("h_done")
        lin_done = sem("lin_done")
        lin_act = sem("lin_act")
        lin_dve = sem("lin_dve")
        act_chain = sem("act_chain")
        dve_chain = sem("dve_chain")
        ml_rot = sem("ml_rot")
        ml_rope = sem("ml_rope")
        g_pre = sem("g_pre")
        g_tanh = sem("g_tanh")
        g_cap = sem("g_cap")
        g_exp = sem("g_exp")
        g_lf = sem("g_lf")
        g_cum = sem("g_cum")
        g_keyb = sem("g_keyb")
        na_s = sem("na_s")
        na_max = sem("na_max")
        na_exp = sem("na_exp")
        na_p = sem("na_p")
        na_pt = sem("na_pt")
        na_pts = sem("na_pts")
        na_o = sem("na_o")
        na_os = sem("na_os")
        ml_s = sem("ml_s")
        ml_b = sem("ml_b")
        ml_bm = sem("ml_bm")
        ml_w = sem("ml_w")
        ml_p = sem("ml_p")
        ml_o = sem("ml_o")
        ml_os = sem("ml_os")
        ml_hn = sem("ml_hn")
        ml_ht = sem("ml_ht")
        ml_hts = sem("ml_hts")

        w_in = A["w_in"][0].rearrange("(c p) n -> p c n", p=P)
        w_ada = A["w_ada"][0].rearrange("(c p) n -> p c n", p=P)
        slabs = [("rel0", A["rel"][:, 0:4096]), ("rel1", A["rel"][:, 4096:8192])]
        slabs += [(f"ada{i}", w_ada[:, :, 512 * i:512 * i + 512]) for i in range(4)]
        slabs += [("na_k", w_in[:, :, C_NAK:C_NAV]), ("na_v", w_in[:, :, C_NAV:C_MLK]),
                  ("ml_k", w_in[:, :, C_MLK:C_MLV]), ("ml_v", w_in[:, :, C_MLV:C_MLG]),
                  ("ml_g", w_in[:, :, C_MLG:C_NAQ]), ("na_q", w_in[:, :, C_NAQ:C_MLQ]),
                  ("ml_q", w_in[:, :, C_MLQ:C_MLO]), ("ml_o", w_in[:, :, C_MLO:C_GNA]),
                  ("gna0", w_in[:, :, C_GNA:C_GNA + 512]), ("gna1", w_in[:, :, C_GNA + 512:C_GML]),
                  ("gml0", w_in[:, :, C_GML:C_GML + 512]), ("gml1", w_in[:, :, C_GML + 512:C_GML + 1024])]
        slabs += [(f"ada{i}", w_ada[:, :, 512 * i:512 * i + 512]) for i in range(4, 12)]
        slabs += [("b_na", A["w_branch_na"][0].rearrange("(c p) n -> p c n", p=P)),
                  ("b_ml", A["w_branch_ml"][0].rearrange("(c p) n -> p c n", p=P))]
        w_out = A["w_out"][0].rearrange("(c p) n -> p c n", p=P)
        slabs += [(f"out{i}", w_out[:, :, 512 * i:512 * i + 512]) for i in range(2)]
        S1 = {n: k for k, (n, _) in enumerate(slabs)}
        N1 = len(slabs)
        assert N1 % RING == 0

        def slab_view(n, c):
            words = int(np.prod(slabs[n][1].shape[1:]))
            v = ring[:, (n % RING) * SLAB:(n % RING) * SLAB + words]
            return v.rearrange("p (c n) -> p c n", c=c)

        groups = [("dve", f"ada{i}") for i in range(4)]
        groups += [("act", f"na_k{m}") for m in range(4)] + [("act", f"na_v{t}") for t in range(4)]
        groups += [("act", f"ml_k{m}") for m in range(2)] + [("act", f"ml_v{t}") for t in range(4)]
        groups += [("dve", "ml_g")] + [("act", f"na_q{m}") for m in range(2)] + [("act", "ml_q0")]
        groups += [("act", f"ml_o{m}") for m in range(2)]
        groups += [("act", f"gna{m}") for m in range(4)] + [("act", f"gml{m}") for m in range(4)]
        groups += [("dve", f"ada{i}") for i in range(4, 12)]
        groups += [("dve", f"b_na{m}") for m in range(4)] + [("dve", f"b_ml{m}") for m in range(4)]
        groups += [("act", f"out{m}") for m in range(4)]
        G1 = {n: k for k, (_, n) in enumerate(groups)}

        def emptied(g):
            by = groups[g][0]
            return (lin_act if by == "act" else lin_dve), sum(b == by for b, _ in groups[:g + 1])

        def freed(n):
            name = slabs[n][0]
            if name.startswith("rel"):
                return rel_done, (4, 7)[int(name[3:])]
            if name.startswith("ada"):
                return lin_done, G1[name] + 1
            if name in ("b_na", "b_ml"):
                return lin_done, G1[name + "3"] + 1
            if name[:3] in ("gna", "gml", "out"):
                return lin_done, G1[f"{name[:3]}{2 * int(name[3:]) + 1}"] + 1
            return lin_done, max(g for nm, g in G1.items() if nm.startswith(name)) + 1

        def slot(j):
            return ring[:, j * SLAB:(j + 1) * SLAB].rearrange("p (c n) -> p c n", c=DC)

        two = lambda b: b.rearrange("p (a b) -> p a b", a=2)
        eight = lambda b: b.rearrange("p (a b) -> p a b", a=DC)
        block = ctx.enter_context(nc.Block())

        @block.sync
        def _(sp):
            for n, (name, src) in enumerate(slabs):
                if n >= RING:
                    sp.wait_ge(*freed(n - RING))
                dst = slab_view(n, src.shape[1]) if len(src.shape) == 3 else ring[:, (n % RING) * SLAB:][:, 0:4096]
                sp.dma_start(dst, src).then_inc(slab_in[n % RING], 16)
            def expert_slab(e, j):
                w = A[("w_gate", "w_lin", "w_down")[j // 2]][0]
                src = w[e, :, 512 * (j % 2):512 * (j % 2) + 512] if isinstance(e, int) else \
                    w[bass.DynSlice(e, 1), :, 512 * (j % 2):512 * (j % 2) + 512].rearrange("a k n -> (a k) n")
                sp.dma_start(slot(j), src.rearrange("(c p) n -> p c n", p=P)).then_inc(moe_in[j], 16)

            for j in range(RING):
                sp.wait_ge(*freed(N1 - RING + j))
                expert_slab(0, j)
            with sp.Fori(1, E) as e:
                for j in range(RING):
                    sp.wait_ge(moe_used, e * RING + (j - RING + 1))
                    expert_slab(e, j)
            sp.wait_ge(npass_set, 1)
            npass = sp.value_load(npass_sb[0:1, 0:1], min_val=1, max_val=MAXPASS)
            with sp.If(npass > 1):
                with sp.Fori(1, npass) as p:
                    with sp.Fori(0, E) as e:
                        for j in range(RING):
                            sp.wait_ge(moe_used, p * (E * RING) + e * RING + (j - RING + 1))
                            expert_slab(e, j)
            def layer_slab(L, n):
                name, (arr, chunks, at0, w) = slabs2[n]
                a = A[arr][bass.DynSlice(L, 1)].rearrange("a k n -> (a k) n")
                src = a[at0:at0 + chunks * P, :] if arr == "w_ffn_down_2" else a[:, at0:at0 + w]
                dst = ring[:, (n % RING) * SLAB:(n % RING) * SLAB + chunks * w].rearrange("p (c n) -> p c n", c=chunks)
                sp.dma_start(dst, src.rearrange("(c p) n -> p c n", p=P)).then_inc(c_in[n % RING], 16)

            with sp.Fori(0, 2) as L:
                for n in range(N2):
                    before = slabs2[(n - RING) % N2][0]
                    g = max(k for k, (_, s, _) in enumerate(groups2) if s == before)
                    sp.wait_ge(c_lin, L * NG2 + (g + 1 + (NG2 if n >= RING else 0)))
                    layer_slab(L, n)
            sp.wait_ge(fin_c, 4)
            for t in range(TT):
                sp.dma_start(out[0, t * P:(t + 1) * P, :], outN[:, t, :]).then_inc(out_done, 16)
            sp.wait_ge(out_done, 16 * TT)

        @block.scalar
        def _(act):
            links = [0]

            def link(ins):
                links[0] += 1
                ins.then_inc(act_chain, 1)
                act.wait_ge(act_chain, links[0])

            for name, (r, k) in VECS1.items():
                src = A[name]
                src = src if len(src.shape) == 1 else src.rearrange("a b -> (a b)")
                act.dma_start(vin[r:r + k, :], src.rearrange("(a b) -> a b", b=P)).then_inc(vec_in, 16)
            for L in range(2):
                for name, (r, k) in VECS2.items():
                    src = A[name][L]
                    src = src if len(src.shape) == 1 else src.rearrange("a b -> (a b)")
                    act.dma_start(vin2[L * NV2 + r:L * NV2 + r + k, :], src.rearrange("(a b) -> a b", b=P)).then_inc(vec_in, 16)
            for t in range(2):
                act.dma_start(xin[:, t, :], A["x"][0, t * P:(t + 1) * P, :]).then_inc(x_in, 16)
                act.dma_start(xin[:, 2 + t, :], A["ctx"][0, t * P:(t + 1) * P, :]).then_inc(x_in, 16)
            for n in K:
                act.dma_start(K[n][:, :], A[n]).then_inc(consts_in, 16)
            act.wait_ge(vecs_turned, 1)
            act.wait_ge(vecs2_turned, 1)
            act.activation(v2T[:, :], bank[6][:, 0:2 * NV2], ACT.Copy).then_inc(v2_copied, 1)
            link(act.activation(vT[:, :], bank[7][:, 0:NV1], ACT.Copy))
            act.activation(stage[:, 0:16], vT[:, 0:16], ACT.Sigmoid).then_inc(sig_c, 1)
            for c in range(DC):
                act.wait_ge(x_copied, 2 * c + 2)
                act.activation(sq[:, c, 0:T], xT[:, c, :], ACT.Square)
                act.activation(sq[:, c, T:512], hAll[:, c, T:512], ACT.Square).then_inc(sq_done, 1)
            act.wait_ge(ms_done, 1)
            act.activation(colA[:, 0:4], colA[:, 0:4], ACT.Sqrt).then_inc(root_done, 1)
            act.wait_ge(gains_done, 1)
            for c in range(DC):
                act.wait_ge(xn_done, c + 1)
                act.activation(hAll[:, c, 0:T], hAll[:, c, 0:T], ACT.Identity, bias=mod[:, c:c + 1],
                               scale=gains[:, 0, c:c + 1])
                act.activation(hAll[:, c, T:512], hAll[:, c, T:512], ACT.Identity, bias=modc[:, c:c + 1],
                               scale=gains[:, 1, c:c + 1]).then_inc(h_done, 1)

            def empty(name, dst, func=ACT.Copy, scale=1.0, src=None):
                g = G1[name]
                act.wait_ge(lin_done, g + 1)
                b = bank[g % 4][:, :]
                act.activation(dst, src(b) if src else b, func, scale=scale).then_inc(lin_act, 1)

            for m in range(4):
                if m == 0:
                    act.wait_ge(x_turned, DC)
                empty(f"na_k{m}", naK[:, m, :])
            for t in range(4):
                empty(f"na_v{t}", naV[:, t, :])
            for m in range(2):
                empty(f"ml_k{m}", mlK[:, m, :])
            for t in range(4):
                empty(f"ml_v{t}", mlV[:, 4 * t:4 * t + 4, 0:128], src=lambda b: b.rearrange("p (a b) -> p a b", a=4))
            for m in range(2):
                empty(f"na_q{m}", naQ[:, 2 * m:2 * m + 2, :], scale=NA_D ** -0.5, src=two)
            empty("ml_q0", mlQ[:, :, :], scale=ML_D ** -0.5, src=two)
            for m in range(2):
                empty(f"ml_o{m}", mlO[:, 2 * m:2 * m + 2, :], ACT.Sigmoid, src=two)
            act.wait_ge(g_pre, 1)
            act.activation(gate[:, :, :], gate[:, :, :], ACT.Tanh, scale=1.0 / SOFTCAP).then_inc(g_tanh, 1)
            act.wait_ge(g_cap, 1)
            link(act.activation(gt2[:, :, :], gt1[:, :, :], ACT.Exp, scale=-1.0))
            act.activation(lsg[:, :, :], gt2[:, :, :], ACT.Ln, bias=1.0).then_inc(g_exp, 1)

            filler = [f"gna{m}" for m in range(4)] + [f"gml{m}" for m in range(4)]
            for i in range(2 * NA_H):
                h, qt = divmod(i, 2)
                act.wait_ge(na_max, i + 1)
                if i >= 2:
                    act.wait_ge(na_pt, i - 1)
                act.activation(Pna[:, i % 2, :], bank[4 + i % 2][:, :], ACT.Exp, bias=nst[:, i:i + 1],
                               accum_out=nst[:, 32 + i:33 + i]).then_inc(na_exp, 1)
                if i < 8:
                    name = filler[i]
                    if i == 0:
                        act.wait_ge(sum_done, 1)
                    dst = (gNA if i < 4 else gML)[:, 2 * (i % 4):2 * (i % 4) + 2, :]
                    empty(name, dst, ACT.Sigmoid, src=two)
                act.wait_ge(na_pt, i + 1)
                if qt == 0 and h >= 1:
                    act.wait_ge(na_o, h)
                act.activation(PT[:, :, qt * P:(qt + 1) * P], bank[6][:, :].rearrange("p (a b) -> p a b", a=4),
                               ACT.Copy).then_inc(na_pts, 1)

            for i in range(2 * ML_H):
                h, dr = divmod(i, 2)
                act.wait_ge(ml_b, h + 1)
                act.wait_ge(ml_bm, 2 * h + 2)
                if i == 0:
                    act.wait_ge(na_max, 2 * NA_H)
                if i >= 2:
                    act.wait_ge(ml_o, i - 1)
                w = wml[:, i % 2, :]
                B = bank[6][:, dr * T:dr * T + T]
                kb = lambda tt: keyb[:, tt, 4 * dr + h:4 * dr + h + 1]
                act.activation(w[:, 0:256], B, ACT.Exp, bias=kb(2))
                act.activation(w[:, 256:512], B, ACT.Exp, bias=kb(3))
                Bm = ropeT[:, dr * T:dr * T + T]
                act.activation(w[:, 512:640], Bm[:, 0:128], ACT.Exp, bias=kb(0))
                act.activation(w[:, 640:768], Bm[:, 128:256], ACT.Exp, bias=kb(1))
                far = B[:, 128:256] if dr == 0 else B[:, 0:128]
                act.activation(w[:, 768:896], far, ACT.Exp, bias=kb(0 if dr == 0 else 1)).then_inc(ml_w, 1)
            act.wait_ge(ms_done, 2)
            act.activation(nst[:, 56:64], nst[:, 56:64], ACT.Sqrt).then_inc(root_done, 1)
            for m in range(4):
                empty(f"out{m}", mixT[:, 2 * m:2 * m + 2, :], src=two)
            def norm(k, src, n0):
                for c in range(DC):
                    act.activation(sq2[:, c, :], src[:, c, :], ACT.Square).then_inc(n_sq, 1)
                act.wait_ge(n_ms, k + 1)
                act.activation(ncol[:, :], ncol[:, :], ACT.Sqrt).then_inc(n_root, 1)

            act.wait_ge(ml_o, 2 * ML_H)
            act.wait_ge(ml_hts, ML_H)
            act.wait_ge(lin_done, G1["b_ml3"] + 1)
            moe_loads = [(braw[0:E, 0, :], A["b_gate"][0]), (braw[0:E, 1, :], A["b_lin"][0]), (bdraw[0:E, :], A["b_down"][0]),
                         (wr, A["w_router"][0].rearrange("(c p) n -> p c n", p=P)),
                         (brow, A["b_router"][0].partition_broadcast(P))]
            for dst, src in moe_loads:
                act.dma_start(dst, src).then_inc(moe_const, 16)
            act.wait_ge(lin_act, emptied(G1["out3"])[1])
            act.wait_ge(lin_dve, emptied(G1["b_ml3"])[1])
            norm(0, mixT, 0)
            act.wait_ge(x_done, DC)
            act.wait_ge(n_row, 1)
            norm(1, xT, DC)
            for c in range(DC):
                act.wait_ge(n_xn, c + 1)
                act.activation(h2T[:, c, :], tmpx[:, c, :], ACT.Identity, bias=mod[:, 24 + c:25 + c],
                               scale=gpre[:, c:c + 1]).then_inc(h2_done, 1)
            for k, dst in enumerate((bgT, blT)):
                act.wait_ge(b_turned, k + 1)
                act.activation(dst, bank[4 + k][:, 0:DC * E].rearrange("p (a b) -> p a b", a=DC), ACT.Copy).then_inc(b_copied, 1)
            for g in range(4):
                act.wait_ge(h2_turned, g + 1)
                act.activation(h2N[:, g // 2, (g % 2) * 512:(g % 2) * 512 + 512], bank[g][:, :], ACT.Copy).then_inc(h2_copied, 1)
            act.wait_ge(rt_top, 1)
            for t in range(TT):
                ins = act.activation(topp[:, t, 0:TOPK], top[:, t, 0:TOPK], ACT.Exp, bias=rcol[:, t:t + 1],
                                     accum_out=rcol[:, 2 + t:3 + t])
            ins.then_inc(rt_exp, 1)
            act.wait_ge(rt_wt, 1)
            act.activation(weightT[0:E, :], bank[6][0:E, 0:T], ACT.Copy).then_inc(rt_wts, 1)

            act.wait_ge(npass_set, 1)
            npass = act.value_load(npass_sb[0:1, 0:1], min_val=1, max_val=MAXPASS)
            with act.Fori(0, npass) as p:
                with act.Fori(0, E // 2) as j:
                    it = act.snap(p * (E // 2) + j)
                    for a in range(2):
                        act.wait_ge(moe_x, it * 2 + (a + 1))
                        act.activation(xe[:, a, :, :], eight(bank[0][:, :]), ACT.Copy).then_inc(moe_xs, 1)
                        if a == 0:
                            act.wait_ge(moe_swt, it + 1)
                            act.wait_ge(moe_sc, it * 4)
                            act.activation(selWT, bank[4][:, 0:T], ACT.Copy).then_inc(moe_swts, 1)
                        act.wait_ge(moe_g2, it * 2 + (a + 1))
                        act.activation(es, eg, ACT.Sigmoid, scale=ALPHA).then_inc(moe_sig, 1)
                        act.wait_ge(moe_used, it * 12 + (6 * a + 6))
                        act.wait_ge(moe_yt, it)
                        act.activation(yT[:, :, a * SLOTS:(a + 1) * SLOTS], eight(bank[3][:, :]), ACT.Copy).then_inc(moe_ys, 1)
                    act.wait_ge(moe_yt, it + 1)
                    act.wait_ge(moe_sc, it * 4)
                    act.activation(yN[:, 0:512], bank[5][:, :], ACT.Copy)
                    act.activation(yN[:, 512:1024], bank[6][:, :], ACT.Copy).then_inc(moe_y2, 1)
            act.wait_ge(moe_add, npass * (4 * E // 2))
            norm(2, accT, 2 * DC)
            act.wait_ge(x_done, 2 * DC)
            act.dma_start(retmask, A["retmask"].rearrange("p (a b) -> p a b", a=RH)).then_inc(c_const, 16)
            act.dma_start(center, A["center"]).then_inc(c_const, 16)
            act.dma_start(posi.bitcast(I32), A["positions_2"][0].partition_broadcast(P)).then_inc(c_const, 16)
            act.wait_ge(c_pos, 1)
            act.activation(sin2, ang, ACT.Sin)
            act.activation(cos2, kf, ACT.Sin).then_inc(c_sin, 1)

            with act.Fori(0, 2) as L:
                act.wait_ge(x_done, L * (2 * DC) + 2 * DC)
                act.wait_ge(n_row, L * 4 + 3)
                norm(L * 4 + 3, xT, 0)

                def empty(name, dst, func=ACT.Copy, scale=1.0, src=None):
                    act.wait_ge(*made2(name, L))
                    b = bank[G2[name] % 4][:, :]
                    act.activation(dst, src(b) if src else b, func, scale=scale).then_inc(c_act, 1)

                for i in range(2):
                    empty(f"cu_{i}", convU[:, 2 * i:2 * i + 2, :], src=two)
                for i in range(2):
                    empty(f"cb_{i}", convB[:, 2 * i:2 * i + 2, :], src=two)
                for i in range(2):
                    empty(f"cc_{i}", convC[:, 2 * i:2 * i + 2, :], src=two)
                for i in range(2):
                    empty(f"rq_{i}", retQ[:, 2 * i:2 * i + 2, :], src=two)
                for i in range(2):
                    empty(f"rk_{i}", retK[:, 2 * i:2 * i + 2, :], src=two)
                for i in range(2):
                    empty(f"rv_{i}", retV[:, i, :])
                for i in range(2):
                    empty(f"rg_{i}", retG[:, 2 * i:2 * i + 2, :], ACT.Silu, src=two)
                empty("gq_0", glaQ, scale=GD ** -0.5, src=two)
                empty("gk_0", glaK, src=two)
                for i in range(2):
                    empty(f"gv_{i}", glaV[:, i, :])
                for i in range(2):
                    empty(f"gr_{i}", glaR[:, 2 * i:2 * i + 2, :], ACT.Silu, src=two)
                act.wait_ge(c_lg, L)
                empty("ga_0", glaA[0:GR, :], src=lambda b: b[0:GR, 0:T])
                act.wait_ge(c_abs, L + 1)
                act.activation(lln, lab, ACT.Exp, scale=-1.0).then_inc(c_exp, 1)
                act.wait_ge(c_exp, L + 1)
                act.activation(lln, lln, ACT.Ln, bias=1.0).then_inc(c_ln, 1)
                gates = {"a": gateA, "b": gateB, "c": gateC}
                order = [(x, i) for x in "abc" for i in range(4)]

                def gate_group(k):
                    x, i = order[k]
                    if k == 8:
                        act.wait_ge(c_conv, L + 1)
                    empty(f"gate{x}_{i}", gates[x][:, 2 * i:2 * i + 2, :], ACT.Sigmoid, src=two)

                act.wait_ge(c_cum, L + 1)
                for h in range(RH):
                    gate_group(2 * h)
                    gate_group(2 * h + 1)
                    act.wait_ge(r_o, L * 8 + (h + 1))
                    act.activation(headY[:, h, :], bank[6][:, 0:T], ACT.Copy).then_inc(r_oc, 1)
                    act.wait_ge(r_c, L * 4 + (h + 1))
                    act.activation(headY[:, h, :], bank[7][:, 0:T], ACT.Copy)
                    act.activation(headSq[:, h, :], bank[7][:, 0:T], ACT.Square).then_inc(r_cc, 1)
                act.wait_ge(h_ms, L * 2 + 1)
                act.activation(hcol, hcol, ACT.Sqrt).then_inc(h_root, 1)
                for m in range(2):
                    for b in range(4):
                        k = 4 * m + b
                        if k >= 2:
                            act.wait_ge(l_s, L * 8 + (k - 1))
                        w = T - 64 * b
                        act.activation(glaEq[:, k % 2, 0:w], glaCum[:, m, 64 * b:T], ACT.Exp, scale=1.0 / TAU, bias=glaNeg[:, m, b:b + 1])
                        act.activation(glaEk[:, k % 2, :], glaCum[:, m, 64 * b:64 * b + 64], ACT.Exp, scale=-1.0 / TAU,
                                       bias=glaPos[:, m, b:b + 1]).then_inc(l_e, 1)
                    for hh in range(2):
                        h = 2 * m + hh
                        gate_group(8 + h)
                        if h == 0:
                            act.wait_ge(h_y, L * 2 + 1)
                        act.wait_ge(r_o, L * 8 + (5 + h))
                        act.activation(headY[:, h, :], bank[6][:, 0:T], ACT.Copy)
                        act.activation(headSq[:, h, :], bank[6][:, 0:T], ACT.Square).then_inc(r_oc, 1)
                act.wait_ge(h_ms, L * 2 + 2)
                act.activation(hcol, hcol, ACT.Sqrt).then_inc(h_root, 1)
                for i in range(4):
                    empty(f"out_{i}", mixC[:, 2 * i:2 * i + 2, :], src=two)
                act.wait_ge(c_dve, L * NDVE2 + 12)
                act.wait_ge(c_act, L * NACT2 + (sum(b == "act" for b, _, _ in groups2[:G2["out_3"] + 1])))
                norm(L * 4 + 4, mixC, 0)
                act.wait_ge(x_done, L * (2 * DC) + 3 * DC)
                act.wait_ge(n_row, L * 4 + 5)
                norm(L * 4 + 5, xT, 0)
                for i in range(11):
                    if i >= 4:
                        act.wait_ge(*emptied2(G2[f"fu_{i - 4}"], L))
                    empty(f"fg_{i}", fS[:, i % 4, :], ACT.Silu)
                act.wait_ge(*made2("fd_6", L))
                for i in range(4):
                    ins = act.activation(ffT[:, 2 * i:2 * i + 2, :], two(bank[i][:, :]), ACT.Copy)
                ins.then_inc(fin_t, 1)
                act.wait_ge(fin_t, L + 1)
                norm(L * 4 + 6, ffT, 0)

        @block.tensor
        def _(pe):
            def slab(name):
                n = S1[name]
                pe.wait_ge(slab_in[n % RING], 16 * (n // RING + 1))
                return slab_view(n, slabs[n][1].shape[1])

            def open_bank(name):
                g = G1[name]
                if g < 4:
                    pe.wait_ge(x_copied, 2 * DC)
                else:
                    pe.wait_ge(*emptied(g - 4))
                return bank[g % 4]

            pe.wait_ge(consts_in, 16 * len(K))
            pe.wait_ge(vec_in, 16 * (len(VECS1) + 2 * len(VECS2)))
            pe.transpose(bank[6][:, 0:2 * NV2], vin2[0:2 * NV2, :], K["ident"][0:2 * NV2, 0:2 * NV2]).then_inc(vecs2_turned, 1)
            pe.transpose(bank[7][:, 0:NV1], vin[0:NV1, :], K["ident"][0:NV1, 0:NV1]).then_inc(vecs_turned, 1)
            pe.wait_ge(x_in, 64)
            for c in range(DC):
                if c >= 4:
                    pe.wait_ge(x_copied, 2 * (c - 4) + 2)
                for t in range(4):
                    last = pe.transpose(bank[c % 4][:, t * P:(t + 1) * P], xin[:, t, c * P:(c + 1) * P], K["ident"][:, :])
                last.then_inc(x_turned, 1)
            pe.wait_ge(relrhs_in, 16 * (2 * NA_H))
            pe.wait_ge(ones_set, 1)
            for b in range(7):
                if b >= 2:
                    pe.wait_ge(rel_copied, b - 1)
                for k in range(10 * b, min(10 * b + 10, 64)):
                    if k in (0, 32):
                        v = slab(f"rel{k // 32}")
                        sl = ring[:, (k // 32) * SLAB:(k // 32) * SLAB + 4096].rearrange("p (k q) -> p k q", k=32)
                    last = pe.matmul(bank[4 + b % 2][:, 48 * (k - 10 * b):48 * (k - 10 * b) + 48], sl[0:63, k % 32, :],
                                     relrhs[0:63, :], start=True, stop=True)
                last.then_inc(rel_done, 1)

            def ada(i):
                w = slab(f"ada{i}")
                b = open_bank(f"ada{i}")
                for m in range(4):
                    for c in range(DC):
                        last = pe.matmul(b[:, 2 * m:2 * m + 2],
                                         w[:, c, m * P:(m + 1) * P], scol[:, c, :], start=(c == 0), stop=(c == DC - 1))
                last.then_inc(lin_done, 1)

            pe.wait_ge(silu_done, 1)
            for i in range(4):
                ada(i)
            pe.wait_ge(sq_done, DC)
            pe.wait_ge(v2_copied, 1)
            for t in range(4):
                for c in range(DC):
                    last = pe.matmul(bank[6][:, t:t + 1], sq[:, c, t * P:(t + 1) * P], ones[:, 0:1], start=(c == 0), stop=(c == DC - 1))
            last.then_inc(sum_done, 1)
            pe.wait_ge(rstd_done, 1)
            for t in range(4):
                last = pe.matmul(bank[5][:, t * P:(t + 1) * P], colA[:, t:t + 1].to_broadcast([P, P]), K["ident"][:, :],
                                 start=True, stop=True)
            last.then_inc(rstd_row, 1)

            def feat(name, w, m, half, rhs, dst, kc=DC, base=0):
                for c in range(kc):
                    last = pe.matmul(dst, w[:, c, base + m * P:base + (m + 1) * P], rhs(c), start=(c == 0), stop=(c == kc - 1))
                return last

            for c in range(DC):
                pe.wait_ge(h_done, c + 1)
            lat = lambda c: hAll[:, c, 0:T]
            both = lambda c: hAll[:, c, :]
            for nm, tiles in (("na_k", 4), ("na_v", 4), ("ml_k", 2), ("ml_v", 4)):
                w = slab(nm)
                for m in range(tiles):
                    b = open_bank(f"{nm}{m}")
                    if nm in ("na_k", "ml_k"):
                        last = feat(nm, w, m, 0, both, b[:, :])
                    else:
                        for c in range(DC):
                            last = pe.matmul(b[:, :], hAll[:, c, m * P:(m + 1) * P], w[:, c, :], start=(c == 0), stop=(c == DC - 1))
                    last.then_inc(lin_done, 1)
            w = slab("ml_g")
            b = open_bank("ml_g")
            for t in range(4):
                for c in range(DC):
                    last = pe.matmul(b[:, 16 * t:16 * t + 16], hAll[:, c, t * P:(t + 1) * P], w[:, c, :], start=(c == 0), stop=(c == DC - 1))
            last.then_inc(lin_done, 1)

            def pair(name, w, i, rhs, kc=DC):
                b = open_bank(name)
                for j in range(2):
                    last = feat(name, w, 2 * i + j, j, rhs, b[:, j * T:(j + 1) * T], kc)
                last.then_inc(lin_done, 1)


            for nm, prs in (("na_q", 2), ("ml_q", 1), ("ml_o", 2)):
                w = slab(nm)
                for i in range(prs):
                    pair(f"{nm}{i}", w, i, lat)
            pe.wait_ge(*emptied(G1["ml_q0"]))
            for m in range(2):
                pe.matmul(bank[4][:, m * T:(m + 1) * T], K["rot16"][:, :], mlQ[:, m, :], start=True, stop=True)
                last = pe.matmul(bank[5][:, m * T:(m + 1) * T], K["rot16"][:, :], mlK[:, m, 0:T], start=True, stop=True)
            last.then_inc(ml_rot, 1)
            pe.wait_ge(g_lf, 1)
            order = {0: [2, 3, 0, 1], 1: [3, 2, 1, 0]}
            for dr in range(2):
                own = K["tri"][:, 0:128] if dr == 0 else K["ltri"][:, 128:256]
                for k, tt in enumerate(order[dr]):
                    dst = bank[6][:, 8 * tt + 4 * dr:8 * tt + 4 * dr + 4]
                    for j in range(k):
                        pe.matmul(dst, ones[:, 0:128], lsg[:, order[dr][j], 4 * dr:4 * dr + 4], start=(j == 0), stop=False)
                    last = pe.matmul(dst, own, lsg[:, tt, 4 * dr:4 * dr + 4], start=(k == 0), stop=True)
            last.then_inc(g_cum, 1)

            fillers = []
            for nm, i in [(a, i) for a in ("gna", "gml") for i in range(4)]:
                def f(nm=nm, i=i):
                    w = slab(f"{nm}{i // 2}")
                    pair(f"{nm}{i}", w, i % 2, lat)
                fillers.append(f)
            for i in range(4, 12):
                fillers.append(lambda i=i: ada(i))

            def scores(i):
                h, qt = divmod(i, 2)
                r = 64 * (h % 2)
                if i >= 2:
                    pe.wait_ge(na_exp, i - 1)
                if i < 2:
                    pe.wait_ge(ml_rope, 1)
                    pe.wait_ge(rel_copied, 7)
                pe.matmul(bank[4 + i % 2][:, :], naQ[r:r + 64, h // 2, qt * P:(qt + 1) * P], naK[r:r + 64, h // 2, :],
                          start=True, stop=True).then_inc(na_s, 1)

            def head_out(h):
                r = 64 * (h % 2)
                pe.wait_ge(na_pts, 2 * h + 2)
                if h >= 1:
                    pe.wait_ge(na_os, h)
                for k in range(4):
                    last = pe.matmul(bank[7][r:r + 64, 0:T][:, :], naV[:, k, h * 64:h * 64 + 64], PT[:, k, :],
                                     start=(k == 0), stop=(k == 3), skip_group_check=True)
                last.then_inc(na_o, 1)

            scores(0)
            for i in range(2 * NA_H):
                if i + 1 < 2 * NA_H:
                    scores(i + 1)
                fillers[i]()
                pe.wait_ge(na_p, i + 1)
                if i >= 1:
                    pe.wait_ge(na_pts, i)
                else:
                    pe.wait_ge(g_keyb, 1)
                for k in range(4):
                    last = pe.transpose(bank[6][:, k * P:(k + 1) * P], Pna[:, i % 2, k * P:(k + 1) * P], K["ident"][:, :])
                last.then_inc(na_pt, 1)
                if i % 2:
                    head_out(i // 2)

            def ml_scores(h):
                r = 64 * (h % 2)
                if h >= 1:
                    pe.wait_ge(ml_p, 2 * h)
                    pe.wait_ge(ml_w, 2 * h)
                else:
                    pe.wait_ge(na_exp, 2 * NA_H)
                    pe.wait_ge(na_pts, 2 * NA_H)
                    pe.wait_ge(ml_rope, 1)
                for tt in range(4):
                    last = pe.matmul(bank[4 + tt // 2][:, (tt % 2) * T:(tt % 2) * T + T],
                                     mlK[r:r + 64, h // 2, tt * P:(tt + 1) * P], mlQ[r:r + 64, h // 2, :],
                                     start=True, stop=True)
                last.then_inc(ml_s, 1)
                for dr in range(2):
                    B = bank[6][:, dr * T:(dr + 1) * T]
                    lf = lambda tt: lsg[:, tt, 4 * dr + h:4 * dr + h + 1].to_broadcast([P, P])
                    pe.matmul(B, lf(2), ones[:, :], start=True, stop=False)
                    if dr == 0:
                        pe.matmul(B[:, 128:256], lf(1), K["tri"][:, 0:128], start=False, stop=False)
                        pe.matmul(B, lf(0), K["tri"][:, :], start=False, stop=False)
                    else:
                        pe.matmul(B[:, 0:128], lf(0), K["ltri"][:, 128:256], start=False, stop=False)
                        pe.matmul(B, lf(1), K["ltri"][:, :], start=False, stop=False)
                    last = pe.matmul(B, lf(3), ones[:, :], start=False, stop=True)
                last.then_inc(ml_b, 1)

            def ml_out(i):
                h, dr = divmod(i, 2)
                pe.wait_ge(ml_p, i + 1)
                if i >= 1:
                    pe.wait_ge(ml_os, i)
                else:
                    pe.wait_ge(na_os, NA_H)
                w = wml[:, i % 2, :]
                for qt in range(2):
                    parts = [(w[:, qt * P:(qt + 1) * P], 2), (w[:, 256 + qt * P:256 + (qt + 1) * P], 3),
                             (w[:, 512 + qt * P:512 + (qt + 1) * P], qt)]
                    if dr == 0 and qt == 1:
                        parts.append((w[:, 768:896], 0))
                    if dr == 1 and qt == 0:
                        parts.append((w[:, 768:896], 1))
                    for k, (lhsT, tt) in enumerate(parts):
                        last = pe.matmul(bank[7][:, 129 * qt:129 * qt + 129], lhsT, mlV[:, 4 * tt + h, :],
                                         start=(k == 0), stop=(k == len(parts) - 1))
                last.then_inc(ml_o, 1)

            def branch(nm, i, o):
                w = slab(nm)
                pair(f"{nm}{i}", w, i, lambda c: o[:, c, :], 4)

            pe.wait_ge(na_os, NA_H)
            for h in range(ML_H):
                ml_scores(h)
                branch("b_na", h, oNaT)
                ml_out(2 * h)
                ml_out(2 * h + 1)
            for h in range(ML_H):
                pe.wait_ge(ml_hn, h + 1)
                for qt in range(2):
                    last = pe.transpose(bank[4 + h % 2][:, qt * P:(qt + 1) * P], hml[:, qt, h * P:(h + 1) * P], K["ident"][:, :])
                    if h >= 2 and qt == 0:
                        pass
                last.then_inc(ml_ht, 1)
                if h + 1 >= 2 and h + 1 < ML_H:
                    pe.wait_ge(ml_hts, h)
            pe.wait_ge(ml_hts, ML_H)
            for i in range(4):
                branch("b_ml", i, oMlT)
            pe.wait_ge(*emptied(G1["b_ml3"]))
            for i in range(4):
                w = slab(f"out{i // 2}")
                pair(f"out{i}", w, i % 2, lambda c: merged[:, c, :])
            def norm(k, n0):
                pe.wait_ge(n_sq, n0 + DC)
                for t in range(TT):
                    for c in range(DC):
                        last = pe.matmul(bank[6][:, t:t + 1], sq2[:, c, t * P:(t + 1) * P], ones[:, 0:1],
                                         start=(c == 0), stop=(c == DC - 1))
                last.then_inc(n_sum, 1)
                pe.wait_ge(n_col, k + 1)
                for t in range(TT):
                    last = pe.matmul(bank[7][:, t * P:(t + 1) * P], ncol[:, t:t + 1].to_broadcast([P, P]), K["ident"][:, :],
                                     start=True, stop=True)
                last.then_inc(n_row, 1)

            norm(0, DC * 0)
            pe.wait_ge(moe_const, 16 * 5)
            for k in range(2):
                for c in range(DC):
                    last = pe.transpose(bank[4 + k][:, c * E:(c + 1) * E], braw[0:E, k, c * P:(c + 1) * P], K["ident"][0:E, 0:E])
                last.then_inc(b_turned, 1)
            norm(1, DC)
            pe.wait_ge(h2_done, DC)
            pe.wait_ge(n_xn, DC)
            for t in range(TT):
                for c in range(DC):
                    last = pe.matmul(bank[7][:, t * E:(t + 1) * E], h2T[:, c, t * P:(t + 1) * P], wr[:, c, :],
                                     start=(c == 0), stop=(c == DC - 1))
            last.then_inc(rt_log, 1)
            for g in range(4):
                pe.wait_ge(lin_act, emptied(G1["out3"])[1])
                for k in range(4):
                    c = 4 * (g % 2) + k
                    last = pe.transpose(bank[g][:, k * P:(k + 1) * P], h2T[:, c, (g // 2) * P:(g // 2 + 1) * P], K["ident"][:, :])
                last.then_inc(h2_turned, 1)
            pe.wait_ge(rt_sel, 1)
            pe.wait_ge(b_copied, 2)
            pe.matmul(bank[5][:, 0:E], K["tri"][:, 0:P], chosen[:, 0, :], start=True, stop=True)
            pe.matmul(bank[5][:, E:2 * E], ones[:, 0:P], chosen[:, 0, :], start=True, stop=False)
            pe.matmul(bank[5][:, E:2 * E], K["tri"][:, 0:P], chosen[:, 1, :], start=False, stop=True)
            pe.matmul(bank[5][:, 2 * E:3 * E], ones[:, 0:P], chosen[:, 0, :], start=True, stop=False)
            pe.matmul(bank[5][:, 2 * E:3 * E], ones[:, 0:P], chosen[:, 1, :], start=False, stop=True).then_inc(rt_cnt, 1)
            pe.wait_ge(rt_sel, 2)
            for t in range(TT):
                last = pe.transpose(bank[6][0:E, t * P:(t + 1) * P], weight[:, t, :], K["ident"][:, :])
            last.then_inc(rt_wt, 1)
            pe.wait_ge(rt_wts, 1)
            for g in range(4):
                pe.wait_ge(h2_copied, g + 1)
                for k in range(2):
                    last = pe.matmul(bank[g][:, k * T:(k + 1) * T], bdraw[0:E, (2 * g + k) * P:(2 * g + k + 1) * P],
                                     weightT[0:E, :], start=True, stop=True)
                last.then_inc(acc_ps, 1)
            pe.wait_ge(acc_set, 4)

            pe.wait_ge(npass_set, 1)
            npass = pe.value_load(npass_sb[0:1, 0:1], min_val=1, max_val=MAXPASS)
            with pe.Fori(0, npass) as p:
                with pe.Fori(0, E // 2) as j:
                    it = pe.snap(p * (E // 2) + j)
                    pe.wait_ge(moe_sel, it + 1)
                    for a in range(2):
                        pe.wait_ge(moe_xs, it * 2 + a)
                        for c in range(DC):
                            for t in range(TT):
                                last = pe.matmul(bank[0][:, c * SLOTS:(c + 1) * SLOTS], h2N[:, t, c * P:(c + 1) * P],
                                                 selS[:, a, t, :], start=(t == 0), stop=(t == TT - 1))
                        last.then_inc(moe_x, 1)
                        if a == 0:
                            pe.wait_ge(moe_add, it * 4)
                            for t in range(TT):
                                last = pe.transpose(bank[4][:, t * P:(t + 1) * P], selW[:, t, :], K["ident"][:, :])
                            last.then_inc(moe_swt, 1)
                        pe.wait_ge(moe_xs, it * 2 + (a + 1))
                        for k, b, read in ((0, 1, moe_gr), (1, 2, moe_lr), (2, 3, moe_ys)):
                            pe.wait_ge(read, it * 2 + a)
                            if k == 2:
                                pe.wait_ge(moe_a, it * 2 + (a + 1))
                            for s in (2 * k, 2 * k + 1):
                                pe.wait_ge(moe_in[s], it * 32 + (16 * a + 16))
                                for m in range(4):
                                    mm = 4 * (s % 2) + m
                                    for c in range(DC):
                                        rhs = xe[:, a, c, :] if k < 2 else ea[:, c, :]
                                        last = pe.matmul(bank[b][:, mm * SLOTS:(mm + 1) * SLOTS],
                                                         slot(s)[:, c, m * P:(m + 1) * P], rhs,
                                                         start=(c == 0), stop=(c == DC - 1))
                                last.then_inc(moe_used, 1)
                    pe.wait_ge(moe_ys, it * 2 + 2)
                    pe.wait_ge(moe_y2, it)
                    for c in range(DC):
                        last = pe.transpose(bank[5 + c // 4][:, (c % 4) * P:(c % 4 + 1) * P], yT[:, c, :], K["ident"][:, :])
                    last.then_inc(moe_yt, 1)
                    pe.wait_ge(moe_y2, it + 1)
                    pe.wait_ge(moe_swts, it + 1)
                    for g in range(4):
                        pe.wait_ge(moe_add, it * 4 + (g - 1 if g >= 2 else 0))
                        for k in range(2):
                            c = 2 * g + k
                            last = pe.matmul(bank[7 if g % 2 == 0 else 4][:, k * T:(k + 1) * T], yN[:, c * P:(c + 1) * P],
                                             selWT, start=True, stop=True)
                        last.then_inc(moe_sc, 1)
            pe.wait_ge(moe_add, npass * (4 * E // 2))
            norm(2, 2 * DC)
            pe.matmul(bank[5][:, 0:1], K["ident"][:, :], ones[:, 0:1], start=True, stop=True).then_inc(c_lin, NG2)
            with pe.Fori(0, 2) as L:
                def slab2(name):
                    n = S2[name]
                    _, (arr, chunks, _, w) = slabs2[n]
                    pe.wait_ge(c_in[n % RING], L * (16 * (N2 // RING)) + 16 * (n // RING + 1))
                    return ring[:, (n % RING) * SLAB:(n % RING) * SLAB + chunks * w].rearrange("p (c n) -> p c n", c=chunks)

                def open2(name):
                    g = G2[name]
                    if g >= 4:
                        pe.wait_ge(*emptied2(g - 4, L))
                    return bank[g % 4]

                def pair2(w, name, i, rhs, kc=DC):
                    b = open2(name)
                    for j in range(2):
                        last = feat(name, w, 2 * i + j, j, rhs, b[:, j * T:(j + 1) * T], kc)
                    last.then_inc(c_lin, 1)

                def rows2(w, name, t):
                    b = open2(name)
                    for c in range(DC):
                        last = pe.matmul(b[:, :], hT[:, c, t * P:(t + 1) * P], w[:, c, :], start=(c == 0), stop=(c == DC - 1))
                    last.then_inc(c_lin, 1)

                norm(L * 4 + 3, (L * 4 + 3) * DC)
                pe.wait_ge(c_h, L * (2 * DC) + DC)
                lat2 = lambda c: hT[:, c, :]
                for nm in ("cu", "cb", "cc", "rq", "rk"):
                    w = slab2(nm)
                    for i in range(2):
                        pair2(w, f"{nm}_{i}", i, lat2)
                w = slab2("rv")
                rows2(w, "rv_0", 0)
                pe.wait_ge(*emptied2(G2["rk_1"], L))
                for h in range(RH):
                    pe.matmul(bank[4 + h // 2][:, (h % 2) * T:(h % 2 + 1) * T], K["rot64"][:, :], retQ[:, h, :], start=True, stop=True)
                for h in range(RH):
                    last = pe.matmul(bank[6 + h // 2][:, (h % 2) * T:(h % 2 + 1) * T], K["rot64"][:, :], retK[:, h, :], start=True, stop=True)
                last.then_inc(c_rot, 1)
                rows2(w, "rv_1", 1)
                w = slab2("rg")
                for i in range(2):
                    pair2(w, f"rg_{i}", i, lat2)
                for nm in ("gq", "gk"):
                    pair2(slab2(nm), f"{nm}_0", 0, lat2)
                w = slab2("gv")
                for t in range(2):
                    rows2(w, f"gv_{t}", t)
                w = slab2("gr")
                for i in range(2):
                    pair2(w, f"gr_{i}", i, lat2)
                w = slab2("ga")
                b = open2("ga_0")
                for c in range(DC):
                    last = pe.matmul(b[0:GR, 0:T], w[:, c, :], hT[:, c, :], start=(c == 0), stop=(c == DC - 1))
                last.then_inc(c_lin, 1)
                pe.wait_ge(*emptied2(G2["ga_0"], L))
                pe.wait_ge(c_wa2, L * 16 + 16)
                pe.wait_ge(c_rope, L + 1)
                for m in range(2):
                    last = pe.matmul(bank[4][:, m * T:(m + 1) * T], wa2[0:GR, m * P:(m + 1) * P], glaA[0:GR, :], start=True, stop=True)
                last.then_inc(c_lg, 1)

                order = [(x, i) for x in "abc" for i in range(4)]

                def gate_group(k):
                    x, i = order[k]
                    pair2(slab2(f"g{x}{i // 2}"), f"gate{x}_{i}", i % 2, lat2)

                def attend(v, h, p):
                    d = bank[6]
                    val = lambda t: v[:, t, h * P:(h + 1) * P]
                    pe.matmul(d[:, 0:P], val(0), p[:, 0:128], start=True, stop=True)
                    pe.matmul(d[:, P:T], val(0), p[:, 128:256], start=True, stop=False)
                    pe.matmul(d[:, P:T], val(1), p[:, 256:384], start=False, stop=True).then_inc(r_o, 1)

                def ret_scores(h):
                    b = bank[4 + h % 2]
                    if h == 0:
                        pe.wait_ge(c_abs, L + 1)
                        pe.wait_ge(c_const, 48)
                    if h >= 2:
                        pe.wait_ge(r_p, L * 4 + (h - 1))
                    pe.matmul(b[:, 0:T], retK[:, h, 0:P], retQ[:, h, :], start=True, stop=True)
                    pe.matmul(b[:, T:T + P], retK[:, h, P:T], retQ[:, h, P:T], start=True, stop=True).then_inc(r_s, 1)

                ret_scores(0)
                for h in range(RH):
                    gate_group(2 * h)
                    if h + 1 < RH:
                        ret_scores(h + 1)
                    pe.wait_ge(r_p, L * 4 + (h + 1))
                    if h >= 1:
                        pe.wait_ge(r_oc, L * 8 + h)
                    attend(retV, h, retP[:, h % 2, :])
                    gate_group(2 * h + 1)
                    pe.wait_ge(r_oc, L * 8 + (h + 1))
                    if h >= 1:
                        pe.wait_ge(r_cc, L * 4 + h)
                    pe.matmul(bank[7][:, 0:T], center, headY[:, h, :], start=True, stop=True).then_inc(r_c, 1)

                def head_sums(k):
                    for h in range(4):
                        for t in range(TT):
                            last = pe.matmul(bank[7][:, 256 + 2 * h + t:257 + 2 * h + t], headSq[:, h, t * P:(t + 1) * P], ones[:, 0:1],
                                             start=True, stop=True)
                    last.then_inc(h_sum, 1)

                def head_rows(k):
                    pe.wait_ge(h_col, L * 2 + (k + 1))
                    for h in range(4):
                        for t in range(TT):
                            last = pe.matmul(bank[4 + h // 2][:, (h % 2) * T + t * P:(h % 2) * T + (t + 1) * P],
                                             hcol[:, 2 * h + t:2 * h + t + 1].to_broadcast([P, P]), K["ident"][:, :],
                                             start=True, stop=True)
                    last.then_inc(h_row, 1)

                pe.wait_ge(r_cc, L * 4 + 4)
                head_sums(0)
                head_rows(0)
                for m in range(2):
                    for b in range(4):
                        k = 4 * m + b
                        pe.wait_ge(l_q, L * 8 + (k + 1))
                        if b == 0:
                            if m == 0:
                                pe.wait_ge(h_y, L * 2 + 1)
                            else:
                                pe.wait_ge(l_p, L * 4 + 2)
                        pe.nop(nofuse=True)
                        w = T - 64 * b
                        col = 64 * b if b < 2 else T + 64 * (b - 2)
                        r = 64 * (b % 2)
                        for hh in range(2):
                            s = 64 * hh
                            last = pe.matmul(bank[4 + hh][r:r + 64, col:col + w], glaEk[s:s + 64, k % 2, :], glaEq[s:s + 64, k % 2, 0:w],
                                             start=True, stop=True, skip_group_check=True)
                        last.then_inc(l_s, 1)
                    for hh in range(2):
                        h = 2 * m + hh
                        gate_group(8 + h)
                        pe.wait_ge(l_p, L * 4 + (h + 1))
                        if h == 0:
                            pe.wait_ge(r_oc, L * 8 + 4)
                        else:
                            pe.wait_ge(r_oc, L * 8 + 4 + h)
                        attend(glaV, h, glaP[:, hh, :])
                pe.wait_ge(r_oc, L * 8 + 8)
                head_sums(1)
                head_rows(1)
                pe.wait_ge(h_y, L * 2 + 2)
                for x, y in (("a", yA), ("b", yB), ("c", yC)):
                    w = slab2(f"br{x}")
                    for i in range(4):
                        pair2(w, f"br{x}_{i}", i, lambda c, y=y: y[:, c, :], 4)
                pe.wait_ge(c_dve, L * NDVE2 + 12)
                for i in range(4):
                    pair2(slab2(f"out{i // 2}"), f"out_{i}", i % 2, lambda c: mergedC[:, c, :])
                norm(L * 4 + 4, (L * 4 + 4) * DC)
                norm(L * 4 + 5, (L * 4 + 5) * DC)
                pe.wait_ge(c_h, L * (2 * DC) + 2 * DC)
                for i in range(6):
                    for nm in ("fg", "fu"):
                        w = slab2(f"{nm}{i}")
                        for k in range(2 if i < 5 else 1):
                            pair2(w, f"{nm}_{2 * i + k}", k, lat2)
                pe.wait_ge(c_dve, L * NDVE2 + NDVE2)
                for i, (c0, kc) in enumerate(DOWN):
                    w = slab2(f"fd{i}")
                    for k in range(kc):
                        for m in range(DC):
                            last = pe.matmul(bank[m // 2][:, (m % 2) * T:(m % 2 + 1) * T], w[:, k, m * P:(m + 1) * P], fT[:, c0 + k, :],
                                             start=(c0 + k == 0 and m % 2 == 0), stop=(c0 + k == FC - 1), skip_group_check=True)
                    last.then_inc(c_lin, 1)
                norm(L * 4 + 6, (L * 4 + 6) * DC)
            pe.wait_ge(x_done, 6 * DC)
            for g in range(4):
                for k in range(4):
                    c = 4 * (g % 2) + k
                    last = pe.transpose(bank[g][:, k * P:(k + 1) * P], xT[:, c, (g // 2) * P:(g // 2 + 1) * P], K["ident"][:, :])
                last.then_inc(fin_t, 1)

        @block.vector
        def _(dve):
            links = [0]

            def link(ins):
                links[0] += 1
                ins.then_inc(dve_chain, 1)
                dve.wait_ge(dve_chain, links[0])

            dve.memset(relrhs[:, :], 1.0).then_inc(ones_set, 1)
            dve.memset(ones[:, :], 1.0)
            dve.wait_ge(sig_c, 1)
            vcol = lambda n: vT[:, VECS1[n][0]:VECS1[n][0] + VECS1[n][1]]
            dve.tensor_tensor(scol[:, :, 0], vT[:, 0:8], stage[:, 0:8], ALU.mult)
            dve.tensor_tensor(scol[:, :, 1], vT[:, 8:16], stage[:, 8:16], ALU.mult).then_inc(silu_done, 1)
            for c in range(DC):
                dve.wait_ge(x_turned, c + 1)
                dve.tensor_copy(xT[:, c, :], bank[c % 4][:, 0:T]).then_inc(x_copied, 1)
                dve.tensor_copy(hAll[:, c, T:512], bank[c % 4][:, T:512]).then_inc(x_copied, 1)
            for b in range(7):
                n = min(10, 64 - 10 * b)
                dve.wait_ge(rel_done, b + 1)
                dve.tensor_copy(bias[:, :, 10 * b:10 * b + n],
                                bank[4 + b % 2][:, 0:48 * n].rearrange("p (k x) -> p x k", k=n)).then_inc(rel_copied, 1)
            ba = VECS1["b_ada"][0]

            def modulation(i):
                g = G1[f"ada{i}"]
                ps = bank[g % 4][:, 0:8].rearrange("p (m a) -> p m a", a=2)
                vb = vT[:, ba + 4 * i:ba + 4 * i + 4]
                dve.wait_ge(lin_done, g + 1)
                if i < 4:
                    dve.tensor_tensor(modc[:, 4 * i:4 * i + 4], ps[:, :, 1], vb, ALU.add)
                dve.tensor_tensor(mod[:, 4 * i:4 * i + 4], ps[:, :, 0], vb, ALU.add).then_inc(lin_dve, 1)

            for i in range(4):
                modulation(i)
            dve.wait_ge(*emptied(G1["ada3"]))
            dve.scalar_tensor_tensor(out=gains[:, 0, :], in0=mod[:, 8:16], scalar=1.0, in1=vcol("g_mix_pre"),
                                     op0=ALU.add, op1=ALU.mult)
            dve.scalar_tensor_tensor(out=gains[:, 1, :], in0=modc[:, 8:16], scalar=1.0, in1=vcol("g_mix_pre"),
                                     op0=ALU.add, op1=ALU.mult).then_inc(gains_done, 1)
            dve.wait_ge(sum_done, 1)
            dve.tensor_scalar(colA[:, 0:4], bank[6][:, 0:4], 1.0 / D, EPS, ALU.mult, ALU.add).then_inc(ms_done, 1)
            dve.wait_ge(root_done, 1)
            dve.reciprocal(colA[:, 0:4], colA[:, 0:4]).then_inc(rstd_done, 1)
            dve.wait_ge(rstd_row, 1)
            for c in range(DC):
                dve.tensor_tensor(hAll[:, c, 0:T], xT[:, c, :], bank[5][:, 0:T], ALU.mult)
                dve.tensor_tensor(hAll[:, c, T:512], hAll[:, c, T:512], bank[5][:, T:512], ALU.mult).then_inc(xn_done, 1)
            dve.memset(mlV[:, :, 128:129], 1.0).then_inc(ones_set, 1)
            dve.wait_ge(lin_done, G1["ml_g"] + 1)
            dve.wait_ge(bg_in, 16)
            dve.tensor_tensor(gate[:, :, :], bank[G1["ml_g"] % 4][:, 0:64].rearrange("p (a b) -> p a b", a=4),
                              bg[:, None, :].to_broadcast([P, 4, 16]), ALU.add).then_inc(lin_dve, 1)
            dve.wait_ge(*emptied(G1["ml_g"]))
            dve.memset(stage[:, 61:62], 0.0).then_inc(g_pre, 1)
            dve.wait_ge(g_tanh, 1)
            link(dve.tensor_scalar(gate[:, :, :], gate[:, :, :], SOFTCAP, None, ALU.mult))
            gf = gate[:, :, :].rearrange("p t (d k h) -> p t d k h", d=2, k=2)
            for dr in range(2):
                ins = dve.scalar_tensor_tensor(out=gt1[:, :, 4 * dr:4 * dr + 4], in0=gf[:, :, dr, 1, :], scalar=-1.0,
                                               in1=gf[:, :, dr, 1, :], op0=ALU.mult, op1=ALU.max)
            ins.then_inc(g_cap, 1)
            dve.wait_ge(g_exp, 1)
            for dr in range(2):
                link(dve.scalar_tensor_tensor(out=lsg[:, :, 4 * dr:4 * dr + 4], in0=gf[:, :, dr, 1, :], scalar=0.0,
                                              in1=lsg[:, :, 4 * dr:4 * dr + 4], op0=ALU.min, op1=ALU.subtract))
            dve.memset(stage[:, 61:62], 0.0).then_inc(g_lf, 1)
            dve.wait_ge(ml_rot, 1)
            rot = lambda b: b[:, :].rearrange("p (a b) -> p a b", a=2)
            bc = lambda k: K[k][:, None, :].to_broadcast([P, 2, T])
            rt = ropeT[:, :].rearrange("p (a b) -> p a b", a=2)
            for buf, b in ((mlQ[:, :, :], bank[4]), (mlK[:, :, 0:T], bank[5])):
                link(dve.tensor_tensor(rt, rot(b), bc("sin1"), ALU.mult))
                link(dve.tensor_tensor(buf, buf, bc("cos1"), ALU.mult))
                link(dve.tensor_tensor(buf, buf, rt, ALU.add))
            dve.memset(stage[:, 61:62], 0.0).then_inc(ml_rope, 1)
            dve.wait_ge(g_cum, 1)
            cum = bank[6][:, 0:32].rearrange("p (t d h) -> p t d h", t=4, d=2)
            for dr in range(2):
                ins = dve.tensor_tensor(keyb[:, :, 4 * dr:4 * dr + 4], gf[:, :, dr, 0, :], cum[:, :, dr, :], ALU.subtract)
            link(ins)
            dve.memset(stage[:, 61:62], 0.0).then_inc(g_keyb, 1)

            def front(i):
                h, qt = divmod(i, 2)
                e0 = 2 - 2 * qt
                dve.wait_ge(na_s, i + 1)
                b = bank[4 + i % 2]
                loc = b[:, 0:T].rearrange("p (a b) -> p a b", a=4)
                link(dve.tensor_tensor(loc, loc, bias[:, 6 * h + e0:6 * h + e0 + 4, :], ALU.add))
                link(dve.tensor_reduce(nst[:, 16 + i:17 + i], b[:, :], AX.X, ALU.max))
                dve.tensor_scalar(nst[:, i:i + 1], nst[:, 16 + i:17 + i], -1.0, None, ALU.mult).then_inc(na_max, 1)

            front(0)
            for i in range(2 * NA_H):
                h, qt = divmod(i, 2)
                if i + 1 < 2 * NA_H:
                    front(i + 1)
                if i >= 8:
                    modulation(i - 4)
                dve.wait_ge(na_exp, i + 1)
                link(dve.reciprocal(nst[:, 32 + i:33 + i], nst[:, 32 + i:33 + i]))
                dve.tensor_scalar(Pna[:, i % 2, :], Pna[:, i % 2, :], nst[:, 32 + i:33 + i], None, ALU.mult).then_inc(na_p, 1)
                if qt:
                    r = 64 * (h % 2)
                    dve.wait_ge(na_o, h + 1)
                    dve.tensor_copy(oNaT[r:r + 64, h // 2, :], bank[7][r:r + 64, 0:T]).then_inc(na_os, 1)

            for h in range(ML_H):
                for dr in range(2):
                    i = 2 * h + dr
                    dve.wait_ge(ml_b, h + 1)
                    if i >= 2:
                        dve.wait_ge(ml_w, i - 1)
                    mask = K["maskf" if dr == 0 else "maskb"][:, None, :].to_broadcast([P, 2, P])
                    dve.tensor_tensor(ropeT[:, dr * T:dr * T + T].rearrange("p (a b) -> p a b", a=2),
                                      bank[6][:, dr * T:dr * T + T].rearrange("p (a b) -> p a b", a=2),
                                      mask, ALU.add).then_inc(ml_bm, 1)
                g = G1[f"b_na{h}"]
                dve.wait_ge(lin_done, g + 1)
                if h == 0:
                    dve.wait_ge(lin_act, emptied(G1["gml3"])[1])
                dve.tensor_tensor(merged[:, 2 * h:2 * h + 2, :], bank[g % 4][:, :].rearrange("p (a b) -> p a b", a=2),
                                  gNA[:, 2 * h:2 * h + 2, :], ALU.mult).then_inc(lin_dve, 1)
                for dr in range(2):
                    i = 2 * h + dr
                    w = wml[:, i % 2, :]
                    dve.wait_ge(ml_w, i + 1)
                    dve.wait_ge(ml_s, h + 1)
                    S = lambda tt, a, b: bank[4 + tt // 2][:, (tt % 2) * T + a:(tt % 2) * T + b]
                    dve.tensor_tensor(w[:, 0:256], w[:, 0:256], S(2, 0, T), ALU.mult)
                    dve.tensor_tensor(w[:, 256:512], w[:, 256:512], S(3, 0, T), ALU.mult)
                    dve.tensor_tensor(w[:, 512:640], w[:, 512:640], S(0, 0, 128), ALU.mult)
                    dve.tensor_tensor(w[:, 640:768], w[:, 640:768], S(1, 128, 256), ALU.mult)
                    far = S(0, 128, 256) if dr == 0 else S(1, 0, 128)
                    dve.tensor_tensor(w[:, 768:896], w[:, 768:896], far, ALU.mult).then_inc(ml_p, 1)
                for dr in range(2):
                    i = 2 * h + dr
                    dve.wait_ge(ml_o, i + 1)
                    for qt in range(2):
                        dst = hml[:, qt, h * P:(h + 1) * P]
                        num = bank[7][:, 129 * qt:129 * qt + 128]
                        den = bank[7][:, 129 * qt + 128:129 * qt + 129]
                        q = nst[:, 48 + qt:49 + qt]
                        link(dve.tensor_scalar(q, den, 1.0, None, ALU.max))
                        link(dve.scalar_tensor_tensor(out=q, in0=den, scalar=-1.0, in1=q, op0=ALU.mult, op1=ALU.max))
                        link(dve.reciprocal(q, q))
                        if dr == 0:
                            link(dve.tensor_scalar(dst, num, q, None, ALU.mult))
                        else:
                            link(dve.scalar_tensor_tensor(out=dst, in0=num, scalar=q, in1=dst, op0=ALU.mult, op1=ALU.add))
                    dve.memset(stage[:, 61:62], 0.0).then_inc(ml_os, 1)
                for qt in range(2):
                    dst = hml[:, qt, h * P:(h + 1) * P]
                    link(dve.tensor_tensor(rstd[:, 0:P], dst, dst, ALU.mult))
                    link(dve.tensor_reduce(nst[:, 56 + 2 * h + qt:57 + 2 * h + qt], rstd[:, 0:P], AX.X, ALU.add))
            ms = nst[:, 56:64]
            dve.tensor_scalar(ms, ms, 1.0 / ML_V, EPS, ALU.mult, ALU.add).then_inc(ms_done, 1)
            dve.wait_ge(root_done, 2)
            link(dve.reciprocal(ms, ms))
            for h in range(ML_H):
                for qt in range(2):
                    dst = hml[:, qt, h * P:(h + 1) * P]
                    ins = dve.tensor_scalar(dst, dst, ms[:, 2 * h + qt:2 * h + qt + 1], None, ALU.mult)
                ins.then_inc(ml_hn, 1)
            gh = VECS1["g_mlstm_head"][0]
            for h in range(ML_H):
                dve.wait_ge(ml_ht, h + 1)
                dve.scalar_tensor_tensor(out=oMlT[:, h, :], in0=bank[4 + h % 2][:, 0:T], scalar=vT[:, gh + h:gh + h + 1],
                                         in1=mlO[:, h, :], op0=ALU.mult, op1=ALU.mult).then_inc(ml_hts, 1)
            for m in range(4):
                g = G1[f"b_ml{m}"]
                dve.wait_ge(lin_done, g + 1)
                gm = gML[:, 2 * m:2 * m + 2, :]
                link(dve.tensor_tensor(gm, bank[g % 4][:, :].rearrange("p (a b) -> p a b", a=2), gm, ALU.mult))
                dve.tensor_tensor(merged[:, 2 * m:2 * m + 2, :], merged[:, 2 * m:2 * m + 2, :], gm, ALU.add).then_inc(lin_dve, 1)
            def norm(k):
                dve.wait_ge(n_sum, k + 1)
                dve.tensor_scalar(ncol[:, :], bank[6][:, 0:2], 1.0 / D, EPS, ALU.mult, ALU.add).then_inc(n_ms, 1)
                dve.wait_ge(n_root, k + 1)
                dve.reciprocal(ncol[:, :], ncol[:, :]).then_inc(n_col, 1)
                dve.wait_ge(n_row, k + 1)

            row = bank[7][:, 0:T]

            def residual(src):
                for c in range(DC):
                    link(dve.tensor_tensor(tmpx[:, c, :], src[:, c, :], row, ALU.mult))
                    dve.scalar_tensor_tensor(out=xT[:, c, :], in0=tmpx[:, c, :], scalar=gpost[:, c:c + 1], in1=xT[:, c, :],
                                             op0=ALU.mult, op1=ALU.add).then_inc(x_done, 1)

            dve.tensor_tensor(gpost[:, :], mod[:, 16:24], vcol("g_mix_post"), ALU.mult)
            dve.scalar_tensor_tensor(out=gpre[:, :], in0=mod[:, 32:40], scalar=1.0, in1=vcol("g_ffn_pre"), op0=ALU.add, op1=ALU.mult)
            norm(0)
            residual(mixT)
            norm(1)
            dve.wait_ge(x_done, DC)
            for c in range(DC):
                dve.tensor_tensor(tmpx[:, c, :], xT[:, c, :], row, ALU.mult).then_inc(n_xn, 1)
            dve.wait_ge(rt_log, 1)
            dve.wait_ge(moe_const, 16 * 5)
            link(dve.tensor_tensor(logits, bank[7][:, 0:TT * E].rearrange("p (a b) -> p a b", a=TT),
                                   brow[:, None, :].to_broadcast([P, TT, E]), ALU.add))
            for t in range(TT):
                link(dve.max(top[:, t, :], logits[:, t, :]))
            for t in range(TT):
                ins = dve.tensor_scalar(rcol[:, t:t + 1], top[:, t, 0:1], -1.0, None, ALU.mult)
            ins.then_inc(rt_top, 1)
            for t in range(TT):
                link(dve.max_index(topi[:, t, :].bitcast(U32), top[:, t, :], logits[:, t, :]))
                link(dve.tensor_copy(topf[:, t, :], topi[:, t, :].bitcast(U32)))
            io = K["iota"][:, 0:E]
            for t in range(TT):
                link(dve.tensor_scalar(chosen[:, t, :], io, topf[:, t, 0:1], None, ALU.is_equal))
                for k in range(1, TOPK):
                    link(dve.scalar_tensor_tensor(out=chosen[:, t, :], in0=io, scalar=topf[:, t, k:k + 1], in1=chosen[:, t, :],
                                                  op0=ALU.is_equal, op1=ALU.add))
            dve.memset(stage[:, 61:62], 0.0).then_inc(rt_sel, 1)
            dve.wait_ge(rt_exp, 1)
            link(dve.reciprocal(rcol[:, 4:6], rcol[:, 2:4]))
            for t in range(TT):
                link(dve.tensor_scalar(topp[:, t, 0:TOPK], topp[:, t, 0:TOPK], rcol[:, 4 + t:5 + t], None, ALU.mult))
                link(dve.tensor_scalar(weight[:, t, :], io, topf[:, t, 0:1], topp[:, t, 0:1], ALU.is_equal, ALU.mult))
                for k in range(1, TOPK):
                    link(dve.tensor_scalar(tmpe[:, t, :], io, topf[:, t, k:k + 1], topp[:, t, k:k + 1], ALU.is_equal, ALU.mult))
                    link(dve.tensor_tensor(weight[:, t, :], weight[:, t, :], tmpe[:, t, :], ALU.add))
            dve.memset(stage[:, 61:62], 0.0).then_inc(rt_sel, 1)
            dve.wait_ge(rt_cnt, 1)
            cnt = bank[5][:, 0:2 * E].rearrange("p (a b) -> p a b", a=TT)
            link(dve.tensor_tensor(place0, cnt, chosen, ALU.mult))
            for p in range(MAXPASS):
                link(dve.tensor_scalar(place[:, :, p * E:(p + 1) * E], place0, float(-1 - SLOTS * p), None, ALU.add))
            link(dve.tensor_reduce(rcol[:, 8:9], bank[5][:, 2 * E:3 * E], AX.X, ALU.max))
            link(dve.tensor_scalar(rcol[:, 9:10], rcol[:, 8:9], SLOTS + 0.5, 1.0, ALU.is_ge, ALU.add))
            for p in range(2, MAXPASS):
                link(dve.tensor_scalar(rcol[:, 10:11], rcol[:, 8:9], SLOTS * p + 0.5, None, ALU.is_ge))
                link(dve.tensor_tensor(rcol[:, 9:10], rcol[:, 9:10], rcol[:, 10:11], ALU.add))
            dve.tensor_copy(npass_sb[:, :], rcol[:, 9:10]).then_inc(npass_set, 1)
            for g in range(4):
                dve.wait_ge(acc_ps, g + 1)
                dve.tensor_copy(accT[:, 2 * g:2 * g + 2, :], two(bank[g][:, :])).then_inc(acc_set, 1)

            dve.wait_ge(npass_set, 1)
            npass = dve.value_load(npass_sb[0:1, 0:1], min_val=1, max_val=MAXPASS)
            with dve.Fori(0, npass) as p:
                with dve.Fori(0, E // 2) as j:
                    it = dve.snap(p * (E // 2) + j)
                    e2 = dve.snap(j * 2)
                    pe2 = dve.snap(p * E + j * 2)
                    for a in range(2):
                        for t in range(TT):
                            pl = place[:, t, bass.DynSlice(pe2 + a, 1)]
                            dve.tensor_scalar(selS[:, a, t, :], K["iota"][:, 0:SLOTS], pl, None, ALU.is_equal)
                            ins = dve.tensor_scalar(selW[:, t, a * SLOTS:(a + 1) * SLOTS], K["iota"][:, 0:SLOTS], pl,
                                                    weight[:, t, bass.DynSlice(e2 + a, 1)], ALU.is_equal, ALU.mult)
                    ins.then_inc(moe_sel, 1)
                    for a in range(2):
                        col = lambda b: b[:, :, bass.DynSlice(e2 + a, 1)].to_broadcast([P, DC, SLOTS])
                        n1 = lambda: it * 2 + (a + 1)
                        dve.wait_ge(moe_used, it * 12 + (6 * a + 2))
                        dve.tensor_tensor(eg, eight(bank[1][:, :]), col(bgT), ALU.add).then_inc(moe_gr, 1)
                        dve.wait_ge(moe_gr, n1())
                        dve.tensor_scalar(eg, eg, LIMIT, None, ALU.min).then_inc(moe_g2, 1)
                        dve.wait_ge(moe_used, it * 12 + (6 * a + 4))
                        dve.tensor_tensor(el, eight(bank[2][:, :]), col(blT), ALU.add).then_inc(moe_lr, 1)
                        dve.wait_ge(moe_lr, n1())
                        dve.tensor_scalar(el, el, LIMIT, -LIMIT, ALU.min, ALU.max).then_inc(moe_l2, 1)
                        dve.wait_ge(moe_l2, n1())
                        dve.scalar_tensor_tensor(out=el, in0=el, scalar=1.0, in1=eg, op0=ALU.add, op1=ALU.mult).then_inc(moe_l3, 1)
                        dve.wait_ge(moe_l3, n1())
                        dve.wait_ge(moe_sig, n1())
                        dve.tensor_tensor(ea, el, es, ALU.mult).then_inc(moe_a, 1)
                    dve.wait_ge(moe_add, it * 4)
                    for g in range(4):
                        dve.wait_ge(moe_sc, it * 4 + (g + 1))
                        dve.tensor_tensor(accT[:, 2 * g:2 * g + 2, :], accT[:, 2 * g:2 * g + 2, :],
                                          two(bank[7 if g % 2 == 0 else 4][:, :]), ALU.add).then_inc(moe_add, 1)
            dve.tensor_tensor(gpost[:, :], mod[:, 40:48], vcol("g_ffn_post"), ALU.mult)
            norm(2)
            residual(accT)
            dve.wait_ge(c_const, 48)
            dve.wait_ge(x_done, 2 * DC)
            link(dve.tensor_copy(posf, posi.bitcast(I32)))
            link(dve.tensor_scalar(ang, posf, K["invfreq"][:, 0:1], None, ALU.mult))
            link(dve.tensor_scalar(kf, ang, float(1 / (2 * np.pi)), MAGIC, ALU.mult, ALU.add))
            link(dve.tensor_scalar(kf, kf, -MAGIC, None, ALU.add))
            for part in TURN:
                link(dve.scalar_tensor_tensor(out=ang, in0=kf, scalar=-part, in1=ang, op0=ALU.mult, op1=ALU.add))
            link(dve.tensor_scalar(ang, ang, PI_IN, -PI_IN, ALU.min, ALU.max))
            link(dve.tensor_scalar(kf, ang, float(np.pi / 2), None, ALU.add))
            link(dve.tensor_scalar(posf, kf, PI_IN, float(-2 * np.pi), ALU.is_gt, ALU.mult))
            link(dve.tensor_tensor(kf, kf, posf, ALU.add))
            dve.tensor_scalar(kf, kf, PI_IN, -PI_IN, ALU.min, ALU.max).then_inc(c_pos, 1)
            dve.memset(glaP[64:128, :, :], 0.0)
            dve.wait_ge(c_sin, 1)

            with dve.Fori(0, 2) as L:
                steps = [0]

                def link(ins):
                    steps[0] += 1
                    ins.then_inc(c_chain, 1)
                    dve.wait_ge(c_chain, L * LINKS + steps[0])

                def residual(src, n):
                    for c in range(DC):
                        link(dve.tensor_tensor(tmpx[:, c, :], src[:, c, :], row, ALU.mult))
                        dve.scalar_tensor_tensor(out=xT[:, c, :], in0=tmpx[:, c, :], scalar=gpost[:, c:c + 1], in1=xT[:, c, :],
                                                 op0=ALU.mult, op1=ALU.add).then_inc(x_done, 1)

                link(dve.tensor_copy(v2c[:, :], v2T[:, :].rearrange("p (l n) -> p l n", l=2)[:, bass.DynSlice(L, 1), :]
                                     .rearrange("p l n -> p (l n)")))
                norm(L * 4 + 3)
                dve.wait_ge(x_done, L * (2 * DC) + 2 * DC)
                for c in range(DC):
                    dve.scalar_tensor_tensor(out=hT[:, c, :], in0=xT[:, c, :], scalar=V2("norm_mix_pre_2")[:, c:c + 1], in1=row,
                                             op0=ALU.mult, op1=ALU.mult).then_inc(c_h, 1)
                dve.wait_ge(*emptied2(G2["cc_1"], L))
                cw = V2("conv_w_2")
                link(dve.tensor_tensor(convU, convU, convC, ALU.mult))
                for c in range(4):
                    link(dve.tensor_scalar(yA[:, c, :], convU[:, c, :], cw[:, 8 + c:9 + c], None, ALU.mult))
                    link(dve.scalar_tensor_tensor(out=yA[:, c, 1:T], in0=convU[:, c, 0:T - 1], scalar=cw[:, 4 + c:5 + c],
                                                  in1=yA[:, c, 1:T], op0=ALU.mult, op1=ALU.add))
                    link(dve.scalar_tensor_tensor(out=yA[:, c, 2:T], in0=convU[:, c, 0:T - 2], scalar=cw[:, c:c + 1],
                                                  in1=yA[:, c, 2:T], op0=ALU.mult, op1=ALU.add))
                dve.tensor_tensor(yA, yA, convB, ALU.mult).then_inc(c_conv, 1)
                dve.wait_ge(c_rot, L + 1)
                tr = at(13840, 4, T)
                for buf, b0 in ((retQ, 4), (retK, 6)):
                    for k in range(2):
                        link(dve.tensor_tensor(tr[:, 2 * k:2 * k + 2, :], two(bank[b0 + k][:, :]), sin2[:, None, :].to_broadcast([P, 2, T]), ALU.mult))
                    link(dve.tensor_tensor(buf, buf, cos2[:, None, :].to_broadcast([P, 4, T]), ALU.mult))
                    ins = dve.tensor_tensor(buf, buf, tr, ALU.add)
                    if b0 == 4:
                        link(ins)
                ins.then_inc(c_rope, 1)
                dve.wait_ge(c_lg, L + 1)
                for m in range(2):
                    ins = dve.tensor_scalar(lgt[:, m, :], bank[4][:, m * T:(m + 1) * T], V2("gla_b_a_2")[:, m:m + 1], None, ALU.add)
                link(ins)
                dve.scalar_tensor_tensor(out=lab, in0=lgt, scalar=-1.0, in1=lgt, op0=ALU.mult, op1=ALU.max).then_inc(c_abs, 1)
                dve.wait_ge(c_ln, L + 1)
                link(dve.scalar_tensor_tensor(out=lgt, in0=lgt, scalar=0.0, in1=lln, op0=ALU.min, op1=ALU.subtract))
                for m in range(2):
                    link(dve.tensor_tensor_scan(glaCum[:, m, :], ones[:, :], lgt[:, m, :], 0.0, ALU.mult, ALU.add))
                mid = glaCum.rearrange("p m (b k) -> p m b k", k=64)[:, :, :, 31]
                dve.tensor_scalar(glaNeg, mid, -1.0 / TAU, None, ALU.mult)
                dve.tensor_scalar(glaPos, mid, 1.0 / TAU, None, ALU.mult).then_inc(c_cum, 1)
                for h in range(RH):
                    dve.wait_ge(r_s, L * 4 + (h + 1))
                    if h >= 2:
                        dve.wait_ge(r_o, L * 8 + (h - 1))
                    b = bank[4 + h % 2]
                    dve.tensor_tensor(retP[:, h % 2, 0:T], b[:, 0:T], retmask[:, h, :], ALU.mult)
                    dve.tensor_tensor(retP[:, h % 2, T:T + P], b[:, T:T + P], retmask[:, h, 0:P], ALU.mult).then_inc(r_p, 1)

                def heads(k, y, gain, gate_):
                    dve.wait_ge(h_sum, L * 2 + (k + 1))
                    dve.tensor_scalar(hcol, bank[7][:, 256:264], 1.0 / P, EPS, ALU.mult, ALU.add).then_inc(h_ms, 1)
                    dve.wait_ge(h_root, L * 2 + (k + 1))
                    dve.reciprocal(hcol, hcol).then_inc(h_col, 1)
                    dve.wait_ge(h_row, L * 2 + (k + 1))
                    for m in range(2):
                        link(dve.tensor_tensor(headY[:, 2 * m:2 * m + 2, :], headY[:, 2 * m:2 * m + 2, :], two(bank[4 + m][:, :]), ALU.mult))
                    for h in range(4):
                        ins = dve.scalar_tensor_tensor(out=y[:, h, :], in0=headY[:, h, :], scalar=gain[:, h:h + 1], in1=gate_[:, h, :],
                                                       op0=ALU.mult, op1=ALU.mult)
                    ins.then_inc(h_y, 1)

                heads(0, yB, V2("ret_gn_w_2"), retG)
                for m in range(2):
                    for b in range(4):
                        k = 4 * m + b
                        w = T - 64 * b
                        dve.wait_ge(l_e, L * 8 + (k + 1))
                        dve.tensor_tensor(glaEq[:, k % 2, 0:w], glaEq[:, k % 2, 0:w], glaQ[:, m, 64 * b:T], ALU.mult)
                        dve.tensor_tensor(glaEk[:, k % 2, :], glaEk[:, k % 2, :], glaK[:, m, 64 * b:64 * b + 64], ALU.mult).then_inc(l_q, 1)
                    dve.wait_ge(l_s, L * 8 + (4 * m + 4))
                    for hh in range(2):
                        if m:
                            dve.wait_ge(r_o, L * 8 + (5 + hh))
                        for b in range(4):
                            w = T - 64 * b
                            col = 64 * b if b < 2 else T + 64 * (b - 2)
                            r = 64 * (b % 2)
                            c0 = 64 * (b % 2)
                            ins = dve.tensor_tensor(glaP[r:r + 64, hh, col:col + w], bank[4 + hh][r:r + 64, col:col + w],
                                                    K["tri"][r:r + 64, c0:c0 + w], ALU.mult)
                        ins.then_inc(l_p, 1)
                heads(1, yC, V2("gla_gn_w_2"), glaR)
                for x, g_ in (("a", gateA), ("b", gateB), ("c", gateC)):
                    for i in range(4):
                        g = G2[f"br{x}_{i}"]
                        dve.wait_ge(*made2(f"br{x}_{i}", L))
                        mg = mergedC[:, 2 * i:2 * i + 2, :]
                        gg = g_[:, 2 * i:2 * i + 2, :]
                        if x == "a":
                            if i == 0:
                                dve.wait_ge(*emptied2(G2["gatec_3"], L))
                            dve.tensor_tensor(mg, two(bank[g % 4][:, :]), gg, ALU.mult).then_inc(c_dve, 1)
                        else:
                            link(dve.tensor_tensor(gg, two(bank[g % 4][:, :]), gg, ALU.mult))
                            dve.tensor_tensor(mg, mg, gg, ALU.add).then_inc(c_dve, 1)
                link(dve.tensor_copy(gpost[:, :], V2("norm_mix_post_2")))
                norm(L * 4 + 4)
                residual(mixC, 0)
                norm(L * 4 + 5)
                dve.wait_ge(x_done, L * (2 * DC) + 3 * DC)
                for c in range(DC):
                    dve.scalar_tensor_tensor(out=hT[:, c, :], in0=xT[:, c, :], scalar=V2("norm_ffn_pre_2")[:, c:c + 1], in1=row,
                                             op0=ALU.mult, op1=ALU.mult).then_inc(c_h, 1)
                for i in range(11):
                    g = G2[f"fu_{i}"]
                    dve.wait_ge(*made2(f"fu_{i}", L))
                    dve.wait_ge(*emptied2(G2[f"fg_{i}"], L))
                    dve.tensor_tensor(fT[:, 2 * i:2 * i + 2, :], two(bank[g % 4][:, :]), two(fS[:, i % 4, :]), ALU.mult).then_inc(c_dve, 1)
                link(dve.tensor_copy(gpost[:, :], V2("norm_ffn_post_2")))
                norm(L * 4 + 6)
                residual(ffT, 0)
                assert steps[0] == LINKS, steps[0]
            for g in range(4):
                dve.wait_ge(fin_t, 2 + g + 1)
                dve.tensor_copy(outN[:, g // 2, (g % 2) * 512:(g % 2 + 1) * 512], bank[g][:, :]).then_inc(fin_c, 1)

        @block.gpsimd
        def _(pool):
            pool.wait_ge(ones_set, 1)
            src = A["rpb"][0].rearrange("h r d -> d h r")
            with nc.allow_non_contiguous_dma(reason="a small table turned"):
                for a in range(2):
                    for h in range(NA_H):
                        pool.dma_start(relrhs[31 * a:31 * a + 31, 6 * h:6 * h + 6], src[:, h, 5 - a:11 - a])\
                            .then_inc(relrhs_in, 16)
                pool.dma_start(bg[:, :], A["b_mlstm_gates"][0].rearrange("a b -> (a b)").partition_broadcast(P)).then_inc(bg_in, 16)
            pool.wait_ge(x_done, 2 * DC)
            with pool.Fori(0, 2) as L:
                pool.wait_ge(c_lg, L)
                pool.dma_start(wa2[0:GR, :], A["gla_w_a2_2"][bass.DynSlice(L, 1)].rearrange("a r n -> (a r) n")).then_inc(c_wa2, 16)


def kernel(**inputs):
    import numpy as _np
    import concourse.bacc as _bacc
    from concourse.bass_utils import run_bass_kernel_spmd as _run

    nc = _bacc.Bacc("TRN2", target_bir_lowering=False, num_devices=1)
    arrays, aps = {}, {}
    for name, a in list(inputs.items()) + list(constants().items()):
        a = _np.ascontiguousarray(a)
        arrays[f"in_{name}"] = a
        aps[name] = nc.dram_tensor(f"in_{name}", a.shape, mybir.dt.from_np(a.dtype), kind="ExternalInput").ap()
    out = nc.dram_tensor("out_0", (1, T, D), F32, kind="ExternalOutput").ap()
    build(nc, aps, out)
    r = _run(nc, [arrays], core_ids=[0])
    return r.results[0]["out_0"]
```

```python
from contextlib import ExitStack

import numpy as np
import concourse.bass as bass
from concourse import mybir

F32 = mybir.dt.float32
F32R = mybir.dt.float32r
I32 = mybir.dt.int32
U32 = mybir.dt.uint32
ALU = mybir.AluOpType
ACT = mybir.ActivationFunctionType
AX = mybir.AxisListType

P = 128
D = 1024
DC = D // P
T = 256
TT = T // P
GRID_W = 64
WIN_W = 16
NA_H, NA_D = 8, 64
ML_H, ML_D, ML_V = 4, 64, 128
E, TOPK = 32, 4
EPS = 1e-6
NEG = -1e30
SOFTCAP = 15.0
ALPHA, LIMIT = 1.702, 7.0
SLOTS = 64
MAXPASS = T // SLOTS
RH, RD = 4, 128
GH, GD, GV, GR = 4, 64, 128, 16
TAU = 16.0
FF = 2816
FC = FF // P
RING = 6
ARENA = 23760
LINKS = 43
MAGIC = 12582912.0
TURN = (6.28125, float(np.float32(2 * np.pi - 6.28125)),
        float(np.float32(2 * np.pi - 6.28125 - float(np.float32(2 * np.pi - 6.28125)))))
PI_IN = 3.1415925
SLAB = DC * 512

VECS1 = {}
_n = 0
for _name, _k in (("c", 8), ("c_ctx", 8), ("b_ada", 48), ("g_mix_pre", 8), ("g_mix_post", 8), ("g_ffn_pre", 8),
                  ("g_ffn_post", 8), ("g_mlstm_head", 4)):
    VECS1[_name] = (_n, _k)
    _n += _k
NV1 = _n
VECS2 = {}
_n = 0
for _name, _k in (("norm_mix_pre_2", 8), ("conv_w_2", 12), ("ret_gn_w_2", 4), ("gla_b_a_2", 2), ("gla_gn_w_2", 4),
                  ("norm_mix_post_2", 8), ("norm_ffn_pre_2", 8), ("norm_ffn_post_2", 8)):
    VECS2[_name] = (_n, _k)
    _n += _k
NV2 = _n

C_NAK, C_NAV, C_MLK, C_MLV, C_MLG = 0, 512, 1024, 1280, 1792
C_NAQ, C_MLQ, C_MLO, C_GNA, C_GML = 1808, 2320, 2576, 3088, 4112
C2 = {"cu": 0, "cb": 512, "cc": 1024, "rq": 1536, "rk": 2048, "rv": 2560, "rg": 3072, "gq": 3584, "gk": 3840,
      "gv": 4096, "gr": 4608, "ga": 5120, "ga0": 5136, "ga1": 5648, "gb0": 6160, "gb1": 6672, "gc0": 7184, "gc1": 7696}


def constants():
    f = np.float32
    i = np.arange(P)
    t = np.arange(T)
    out = {}
    out["ident"] = np.eye(P, dtype=f)
    out["tri"] = (i[:, None] <= t[None, :]).astype(f)
    out["ltri"] = (i[:, None] >= (t[None, :] - P)).astype(f)
    out["maskf"] = np.where(i[:, None] <= i[None, :], 0.0, NEG).astype(f)
    out["maskb"] = np.where(i[:, None] >= i[None, :], 0.0, NEG).astype(f)
    for name, half in (("rot16", 16), ("rot64", 64)):
        m = np.zeros((P, P), f)
        for a in range(P):
            if a % (2 * half) < half:
                m[a + half, a] = -1.0
            else:
                m[a - half, a] = 1.0
        out[name] = m
    nf = ML_D // 4
    inv = (f(10000.0) ** (-np.arange(nf, dtype=f) / f(nf))).astype(f)
    d = i % ML_D
    pos = np.where(d[:, None] < ML_D // 2, (t // GRID_W)[None, :], (t % GRID_W)[None, :]).astype(f)
    ang = (pos * inv[d % nf][:, None]).astype(f)
    out["cos1"] = np.cos(ang).astype(f)
    out["sin1"] = np.sin(ang).astype(f)
    c = np.arange(GRID_W)
    start = np.clip(c - WIN_W // 2, 0, GRID_W - WIN_W)
    inwin = (c[:, None] >= start[None, :]) & (c[:, None] < start[None, :] + WIN_W)
    rel = np.zeros((P, GRID_W, P), f)
    for a in range(2):
        for kc in range(GRID_W):
            for q in range(GRID_W):
                if inwin[kc, q]:
                    rel[31 * a + kc - q + 15, kc, 64 * a + q] = 1.0
                else:
                    rel[62, kc, 64 * a + q] = NEG
    out["rel"] = rel.reshape(P, GRID_W * P)
    out["pick"] = np.stack([(i % 32 == r) for r in range(2)], axis=1).astype(f)
    out["iota"] = np.tile(np.arange(64, dtype=f), (P, 1))
    h = np.arange(RH, dtype=f)
    log_g = np.log(1.0 - 2.0 ** (-5.0 - h.astype(np.float64)))
    diff = (t[None, :] - i[:, None])[:, None, :]
    dec = np.where(diff >= 0, np.exp(log_g[None, :, None] * np.maximum(diff, 0)), 0.0) * RD ** -0.5
    out["center"] = (np.eye(P) - 1.0 / P).astype(f)
    out["retmask"] = dec.astype(f).reshape(P, RH * T)
    half = RD // 2
    out["invfreq"] = (f(10000.0) ** (-np.arange(half, dtype=f) / f(half))).astype(f)[i % half][:, None].copy()
    return out


CONST_SHAPES = {"ident": P, "tri": T, "ltri": T, "maskf": P, "maskb": P, "rot16": P, "rot64": P, "cos1": T, "sin1": T,
                "iota": 64, "pick": 2, "center": P, "retmask": RH * T, "invfreq": 1}


def build(nc, A, out):
    with ExitStack() as ctx:
        def sb(name, shape, dt=F32):
            return ctx.enter_context(nc.sbuf_tensor(name, shape, dt))

        def sem(name):
            return ctx.enter_context(nc.semaphore(name))

        bank = [ctx.enter_context(nc.psum_tensor(f"bank{i}", [P, 512], F32)) for i in range(8)]

        ring_at = -(-nc.sbuf_base // 32) * 32
        ring = sb("ring", [P, RING * SLAB])
        ringR = nc.alloc_sbuf_tensor_at("ring_rounded", [P, RING * SLAB], F32R, offset=ring_at)
        K = {n: sb("k_" + n, [P, w]) for n, w in CONST_SHAPES.items() if n not in ("retmask", "center", "cos1", "sin1")}
        cossin = sb("cossin", [P, 2 * T])
        K["cos1"], K["sin1"] = cossin[:, 0:T], cossin[:, T:2 * T]
        ones = sb("ones", [P, T])
        xT = sb("xT", [P, DC, T])
        vT = sb("vT", [P, NV1])
        v2T = sb("v2T", [P, 2 * NV2])
        mod = sb("mod", [P, 48])
        modc = sb("modc", [P, 16])
        gains = sb("gains", [P, 2, DC])
        stage = sb("stage", [P, 64])
        colA = sb("colA", [P, 8])
        scol = sb("scol", [P, DC, 32])
        arena_at = -(-nc.sbuf_base // 32) * 32
        arenaA = sb("arenaA", [P, ARENA])
        arenaR = nc.alloc_sbuf_tensor_at("arena_rounded", [P, ARENA], F32R, offset=arena_at)

        def carve(*shapes):
            at, got = 0, []
            for s in shapes:
                n = int(np.prod(s))
                v = arenaA[:, at:at + n]
                if len(s) == 2:
                    v = v.rearrange("p (a b) -> p a b", a=s[0])
                if len(s) == 3:
                    v = v.rearrange("p (a b c) -> p a b c", a=s[0], b=s[1])
                got.append(v)
                at += n
            assert at <= ARENA, at
            return got

        (hAll, naK, naV, mlK, mlV, naQ, mlQ, mlO, gNA, gML, bias, Pna, PT, gate, small) = carve(
            (DC, 512), (4, 512), (4, 512), (2, 512), (4 * ML_H, 129), (4, T), (2, T), (4, T), (DC, T), (DC, T),
            (48, 64), (2, 512), (4, T), (4, 16), (640,))
        rstd = Pna[:, 0, :]
        adaRow = [Pna[:, 1, :] if i < 4 else cossin[:, :] for i in range(12)]
        ropeT = PT[:, 0:2, :].rearrange("p a b -> p (a b)")
        xin = arenaA[:, 8 * 512:8 * 512 + 4096].rearrange("p (a b) -> p a b", a=4)
        at = 8 * 512 + 4096 + 1024 + 16 * 129 + 1024 + 512 + 1024
        sq = arenaA[:, at:at + 4096].rearrange("p (a b) -> p a b", a=DC)
        wml = arenaA[:, at + 4096:at + 4096 + 2 * 896].rearrange("p (a b) -> p a b", a=2)
        hml = arenaA[:, at + 4096 + 1792:at + 4096 + 1792 + 1024].rearrange("p (a b) -> p a b", a=2)
        oNaT = naQ
        oMlT = naK[:, 0:2, :].rearrange("p a b -> p (a b)").rearrange("p (a b) -> p a b", a=4)
        merged = hAll[:, 0:4, :].rearrange("p a b -> p (a b)").rearrange("p (a b) -> p a b", a=DC)
        mixT = hAll[:, 4:8, :].rearrange("p a b -> p (a b)").rearrange("p (a b) -> p a b", a=DC)
        vin = small[:, 0:128]
        vin2 = small[:, 128:256]
        relrhs = small[:, 256:304]
        lfb = small[:, 304:320]
        keyb = small[:, 320:352].rearrange("p (a b) -> p a b", a=4)
        gt1 = small[:, 352:384].rearrange("p (a b) -> p a b", a=4)
        gt2 = small[:, 384:416].rearrange("p (a b) -> p a b", a=4)
        bg = small[:, 416:432]
        lsg = small[:, 432:464].rearrange("p (a b) -> p a b", a=4)
        nst = small[:, 464:560]

        def at(off, *shape, buf=arenaA):
            n = int(np.prod(shape))
            v = buf[:, off:off + n]
            if len(shape) == 2:
                v = v.rearrange("p (a b) -> p a b", a=shape[0])
            return v

        h2T = at(0, DC, T)
        accT = at(2048, DC, T)
        h2N = at(4096, TT, D)
        braw = at(6144, 2, D)
        bdraw = at(8704, D)
        wr = at(9728, DC, E)
        brow = at(9984, E)
        logits = at(10016, TT, E)
        chosen = at(10080, TT, E)
        weight = at(10144, TT, E)
        place0 = at(10208, TT, E)
        place = at(10272, TT, MAXPASS * E + 2)
        weightT = at(10532, T)
        selS = at(10788, 2, TT * SLOTS).rearrange("p a (t s) -> p a t s", t=TT)
        selW = at(11044, TT, 2 * SLOTS)
        selWT = at(11300, T)
        top = at(11556, TT, 8)
        topi = at(11572, TT, 8)
        topf = at(11588, TT, 8)
        topp = at(11604, TT, 8)
        tmpe = at(11620, TT, E)
        rcol = at(11684, 16)
        expertSel = at(11700, 2, SLOTS)
        sq2 = at(13840, DC, T)
        tmpx = at(15888, DC, T)
        xg = at(17936, 512)
        xeT = at(18448, 2, 512)
        eg, el, es, ea = [at(19472 + 512 * k, 512) for k in range(4)]
        aT = at(21520, 512)
        yN = at(22032, 2, 512)
        npass_sb = sb("npass_sb", [P, 1], I32)
        gpost = sb("gpost", [P, DC])
        gpre = sb("gpre", [P, DC])
        ncol = sb("ncol", [P, 2])
        nrow = at(23504, T)

        hT = at(0, DC, T)
        mergedC = at(2048, DC, T)
        headY, headSq = at(2048, 4, T), at(3072, 4, T)
        convU, convB, convC = at(4096, 4, T), at(5120, 4, T), at(6144, 4, T)
        yA = convC
        retQ, retK, retV, retG = at(7168, 4, T), at(8192, 4, T), at(9216, TT, 512), at(10240, 4, T)
        yB, yC = retQ, retK
        glaQ, glaK, glaV = at(11264, 2, T), at(11776, 2, T), at(12288, TT, 512)
        glaA = at(13312, T)
        glaEk = at(13568, 2, 64)
        glaNeg = at(13696, 2, 4)
        glaPos = at(13704, 2, 4)
        hcol = at(13712, 8)
        gateA, gateB, gateC = at(13840, DC, T), at(15888, DC, T), at(4096, DC, T)
        mixC = at(9216, DC, T)
        glaR = at(17936, 4, T)
        cos2, sin2 = K["cos1"][:, :], K["sin1"][:, :]
        retP = at(19472, 2, 384)
        glaCum = at(20240, 2, T)
        glaEq = at(20752, 2, T)
        glaP = at(21264, 2, 384)
        retmask = at(22032, RH, T)
        wa2 = at(23056, T)
        center = at(23312, P)
        lgt = at(2048, 2, T)
        lab = at(2560, 2, T)
        lln = at(3072, 2, T)
        fT = at(4096, FC, T)
        fLo = at(11776, FC, T)
        hLo = at(17936, DC, T)
        fH, fL = at(4096, FC, T, buf=arenaR), at(11776, FC, T, buf=arenaR)
        hH, hL = at(0, DC, T, buf=arenaR), at(17936, DC, T, buf=arenaR)
        fS = at(9728, 4, 512)
        ffT = at(2048, DC, T)
        posi, posf, ang, kf = [at(11792 + 256 * k, T) for k in range(4)]
        v2c = sb("v2c", [P, NV2])
        V2 = lambda n: v2c[:, VECS2[n][0]:VECS2[n][0] + VECS2[n][1]]
        outN = at(4096, TT, D)

        slabs2 = [(n, ("w_in_2", 8, C2[n], w)) for n, w in (
            ("cu", 512), ("cb", 512), ("cc", 512), ("rq", 512), ("rk", 512), ("rv", 512), ("rg", 512), ("gq", 256),
            ("gk", 256), ("gv", 512), ("gr", 512), ("ga", 16), ("ga0", 512), ("ga1", 512), ("gb0", 512), ("gb1", 512),
            ("gc0", 512), ("gc1", 512))]
        slabs2 += [(f"br{x}", (f"w_branch_{x}_2", 4, 0, 1024)) for x in "abc"]
        slabs2 += [(f"out{i}", ("w_out_2", 8, 512 * i, 512)) for i in range(2)]
        for i in range(6):
            w = min(512, FF - 512 * i)
            slabs2 += [(f"fg{i}", ("w_ffn_gate_2", 8, 512 * i, w)), (f"fu{i}", ("w_ffn_up_2", 8, 512 * i, w))]
        DOWN = [(0, 4)] + [(4 + 3 * k, 3) for k in range(6)]
        slabs2 += [(f"fd{i}", ("w_ffn_down_2", k, c0 * P, 1024)) for i, (c0, k) in enumerate(DOWN)]
        load2 = dict(slabs2)
        SPLIT = [n for n, _ in slabs2 if n.startswith(("fg", "fu", "fd"))]
        slots2 = []
        for n, _ in slabs2:
            slots2 += [n, n + "_hi"] if n in SPLIT else [n]
        slots2 += [None] * (-len(slots2) % RING)
        N2 = len(slots2)
        S2 = {n: k for k, n in enumerate(slots2) if n}
        groups2 = []
        for n, k in (("cu", 2), ("cb", 2), ("cc", 2), ("rq", 2), ("rk", 2), ("rv", 2), ("rg", 2), ("gq", 1), ("gk", 1),
                     ("gv", 2), ("gr", 2), ("ga", 1)):
            groups2 += [("act", n, f"{n}_{i}") for i in range(k)]
        for x in "abc":
            groups2 += [("act", f"g{x}{i // 2}", f"gate{x}_{i}") for i in range(4)]
        for x in "abc":
            groups2 += [("dve", f"br{x}", f"br{x}_{i}") for i in range(4)]
        groups2 += [("act", f"out{i // 2}", f"out_{i}") for i in range(4)]
        for i in range(6):
            groups2 += [("act", f"fg{i}", f"fg_{2 * i + k}") for k in range(2 if i < 5 else 1)]
            groups2 += [("dve", f"fu{i}", f"fu_{2 * i + k}") for k in range(2 if i < 5 else 1)]
        groups2 += [("none", f"fd{i}", f"fd_{i}") for i in range(len(DOWN))]
        G2 = {n: k for k, (_, _, n) in enumerate(groups2)}
        NG2 = len(groups2)
        NACT2 = sum(b == "act" for b, _, _ in groups2)
        NDVE2 = sum(b == "dve" for b, _, _ in groups2)

        def emptied2(g, L):
            by = groups2[g][0]
            n = sum(b == by for b, _, _ in groups2[:g + 1])
            return (c_act, L * NACT2 + n) if by == "act" else (c_dve, L * NDVE2 + n)

        def cleared2(n, L):
            k = n - RING
            while slots2[k % N2] is None:
                k -= RING
            g = max(g for g, (_, s, _) in enumerate(groups2) if s == slots2[k % N2].removesuffix("_hi"))
            return c_lin, L * NG2 + (g + 1 + (NG2 if k >= 0 else 0))

        def loaded2(name, L):
            n = S2[name]
            mine = [k for k in range(n % RING, N2, RING) if slots2[k] in load2]
            return slab_in[n % RING], L * (16 * len(mine)) + 16 * (N1 // RING + mine.index(n) + 1)

        def place2(name, buf=ring):
            _, chunks, _, w = load2[name.removesuffix("_hi")]
            at0 = (S2[name] % RING) * SLAB
            return buf[:, at0:at0 + chunks * w].rearrange("p (c n) -> p c n", c=chunks)

        def made2(name, L):
            return c_lin, L * NG2 + (NG2 + G2[name] + 1)

        c_lin, c_act, c_dve, c_h, c_chain = [sem(n) for n in ("c_lin", "c_act", "c_dve", "c_h", "c_chain")]
        c_const, c_pos, c_sin, c_rot, c_rope, c_conv = [sem(n) for n in ("c_const", "c_pos", "c_sin", "c_rot", "c_rope", "c_conv")]
        c_wa2, c_lg, c_abs, c_exp, c_ln, c_cum = [sem(n) for n in ("c_wa2", "c_lg", "c_abs", "c_exp", "c_ln", "c_cum")]
        r_s, r_p, r_o, r_oc, r_c, r_cc = [sem(n) for n in ("r_s", "r_p", "r_o", "r_oc", "r_c", "r_cc")]
        h_sum, h_ms, h_root, h_col, h_row, h_y = [sem(n) for n in ("h_sum", "h_ms", "h_root", "h_col", "h_row", "h_y")]
        l_e, l_q, l_s, l_p = [sem(n) for n in ("l_e", "l_q", "l_s", "l_p")]
        fin_t, fin_c = sem("fin_t"), sem("fin_c")
        w_hi, w_lo, f_hi, f_lo = [sem(n) for n in ("w_hi", "w_lo", "f_hi", "f_lo")]
        NSPLIT = len(SPLIT)
        NHID = FC // 2
        pos_in = sem("pos_in")
        vecs2_turned = sem("vecs2_turned")
        v2_copied = sem("v2_copied")
        n_sq = sem("n_sq")
        n_sum = sem("n_sum")
        n_par = sem("n_par")
        n_parc = sem("n_parc")
        par_done = sem("par_done")
        par_copied = sem("par_copied")
        ada_rows = sem("ada_rows")
        ada_copied = sem("ada_copied")
        n_ms = sem("n_ms")
        n_root = sem("n_root")
        n_col = sem("n_col")
        n_row = sem("n_row")
        n_xn = sem("n_xn")
        x_done = sem("x_done")
        h2_done = sem("h2_done")
        h2_turned = sem("h2_turned")
        h2_copied = sem("h2_copied")
        moe_const = sem("moe_const")
        rt_log = sem("rt_log")
        rt_top = sem("rt_top")
        rt_exp = sem("rt_exp")
        rt_sel = sem("rt_sel")
        rt_cnt = sem("rt_cnt")
        rt_wt = sem("rt_wt")
        rt_wts = sem("rt_wts")
        acc_ps = sem("acc_ps")
        npass_set = sem("npass_set")
        moe_in = [sem(f"moe_in{i}") for i in range(RING)]
        moe_used = sem("moe_used")
        moe_sel = sem("moe_sel")
        moe_x = sem("moe_x")
        moe_xs = sem("moe_xs")
        moe_xt = sem("moe_xt")
        moe_xts = sem("moe_xts")
        moe_at = sem("moe_at")
        moe_ats = sem("moe_ats")
        moe_g2 = sem("moe_g2")
        moe_sig = sem("moe_sig")
        moe_l2 = sem("moe_l2")
        moe_l3 = sem("moe_l3")
        moe_a = sem("moe_a")
        moe_ys = sem("moe_ys")
        moe_swt = sem("moe_swt")
        moe_swts = sem("moe_swts")
        moe_sc = sem("moe_sc")
        moe_add = sem("moe_add")
        consts_in = sem("consts_in")
        x_in = sem("x_in")
        first_in = sem("first_in")
        FIRST = ("ident", "pick")
        vec_in = sem("vec_in")
        vec2_in = sem("vec2_in")
        slab_in = [sem(f"slab_in{i}") for i in range(RING)]
        out_done = sem("out_done")
        ones_set = sem("ones_set")
        vecs_turned = sem("vecs_turned")
        x_turned = sem("x_turned")
        x_copied = sem("x_copied")
        relrhs_in = sem("relrhs_in")
        bg_in = sem("bg_in")
        rel_done = sem("rel_done")
        rel_copied = sem("rel_copied")
        silu_done = sem("silu_done")
        sig_c = sem("sig_c")
        gains_done = sem("gains_done")
        sq_done = sem("sq_done")
        sum_done = sem("sum_done")
        ms_done = sem("ms_done")
        root_done = sem("root_done")
        rstd_done = sem("rstd_done")
        rstd_row = sem("rstd_row")
        xn_done = sem("xn_done")
        h_done = sem("h_done")
        lin_done = sem("lin_done")
        lin_act = sem("lin_act")
        lin_dve = sem("lin_dve")
        act_chain = sem("act_chain")
        dve_chain = sem("dve_chain")
        ml_rot = sem("ml_rot")
        ml_rope = sem("ml_rope")
        g_pre = sem("g_pre")
        g_tanh = sem("g_tanh")
        g_cap = sem("g_cap")
        g_exp = sem("g_exp")
        g_lf = sem("g_lf")
        g_cum = sem("g_cum")
        g_keyb = sem("g_keyb")
        na_s = sem("na_s")
        na_max = sem("na_max")
        na_exp = sem("na_exp")
        na_p = sem("na_p")
        na_pt = sem("na_pt")
        na_pts = sem("na_pts")
        na_o = sem("na_o")
        na_os = sem("na_os")
        ml_s = sem("ml_s")
        ml_b = sem("ml_b")
        ml_bm = sem("ml_bm")
        ml_w = sem("ml_w")
        ml_p = sem("ml_p")
        ml_o = sem("ml_o")
        ml_os = sem("ml_os")
        ml_hn = sem("ml_hn")
        ml_ht = sem("ml_ht")
        ml_hts = sem("ml_hts")

        w_in = A["w_in"][0].rearrange("(c p) n -> p c n", p=P)
        w_ada = A["w_ada"][0].rearrange("(c p) n -> p c n", p=P)
        slabs = [(f"ada{i}", w_ada[:, :, 512 * i:512 * i + 512]) for i in range(4)]
        slabs += [("na_k", w_in[:, :, C_NAK:C_NAV]), ("na_v", w_in[:, :, C_NAV:C_MLK]),
                  ("ml_k", w_in[:, :, C_MLK:C_MLV]), ("ml_v", w_in[:, :, C_MLV:C_MLG]),
                  ("ml_g", w_in[:, :, C_MLG:C_NAQ]), ("na_q", w_in[:, :, C_NAQ:C_MLQ]),
                  ("ml_q", w_in[:, :, C_MLQ:C_MLO]), ("ml_o", w_in[:, :, C_MLO:C_GNA]),
                  ("rel0", A["rel"][:, 0:4096]), ("rel1", A["rel"][:, 4096:8192]),
                  ("gna0", w_in[:, :, C_GNA:C_GNA + 512]), ("gna1", w_in[:, :, C_GNA + 512:C_GML]),
                  ("gml0", w_in[:, :, C_GML:C_GML + 512]), ("gml1", w_in[:, :, C_GML + 512:C_GML + 1024])]
        slabs += [(f"ada{i}", w_ada[:, :, 512 * i:512 * i + 512]) for i in range(4, 12)]
        slabs += [("b_na", A["w_branch_na"][0].rearrange("(c p) n -> p c n", p=P)),
                  ("b_ml", A["w_branch_ml"][0].rearrange("(c p) n -> p c n", p=P))]
        w_out = A["w_out"][0].rearrange("(c p) n -> p c n", p=P)
        slabs += [(f"out{i}", w_out[:, :, 512 * i:512 * i + 512]) for i in range(2)]
        S1 = {n: k for k, (n, _) in enumerate(slabs)}
        N1 = len(slabs)
        assert N1 % RING == 0

        def slab_view(n, c):
            words = int(np.prod(slabs[n][1].shape[1:]))
            v = ring[:, (n % RING) * SLAB:(n % RING) * SLAB + words]
            return v.rearrange("p (c n) -> p c n", c=c)

        groups = [("dve", f"ada{i}") for i in range(4)]
        groups += [("act", f"na_k{m}") for m in range(4)] + [("act", f"na_v{t}") for t in range(4)]
        groups += [("act", f"ml_k{m}") for m in range(2)] + [("act", f"ml_v{t}") for t in range(4)]
        groups += [("dve", "ml_g")] + [("act", f"na_q{m}") for m in range(2)] + [("act", "ml_q0")]
        groups += [("act", f"ml_o{m}") for m in range(2)]
        groups += [("act", f"gna{m}") for m in range(4)] + [("act", f"gml{m}") for m in range(4)]
        groups += [("dve", f"ada{i}") for i in range(4, 12)]
        groups += [("dve", f"b_na{m}") for m in range(4)] + [("dve", f"b_ml{m}") for m in range(4)]
        groups += [("act", f"out{m}") for m in range(4)]
        G1 = {n: k for k, (_, n) in enumerate(groups)}

        def emptied(g):
            by = groups[g][0]
            return (lin_act if by == "act" else lin_dve), sum(b == by for b, _ in groups[:g + 1])

        def freed(n):
            name = slabs[n][0]
            if name.startswith("rel"):
                return rel_done, (4, 7)[int(name[3:])]
            if name.startswith("ada"):
                return lin_done, G1[name] + 1
            if name in ("b_na", "b_ml"):
                return lin_done, G1[name + "3"] + 1
            if name[:3] in ("gna", "gml", "out"):
                return lin_done, G1[f"{name[:3]}{2 * int(name[3:]) + 1}"] + 1
            return lin_done, max(g for nm, g in G1.items() if nm.startswith(name)) + 1

        def slot(j):
            return ring[:, j * SLAB:(j + 1) * SLAB].rearrange("p (c n) -> p c n", c=DC)

        two = lambda b: b.rearrange("p (a b) -> p a b", a=2)
        eight = lambda b: b.rearrange("p (a b) -> p a b", a=DC)
        block = ctx.enter_context(nc.Block())

        @block.sync
        def _(sp):
            for t in range(2):
                sp.dma_start(xin[:, t, :], A["x"][0, t * P:(t + 1) * P, :]).then_inc(x_in, 16)
                sp.dma_start(xin[:, 2 + t, :], A["ctx"][0, t * P:(t + 1) * P, :]).then_inc(x_in, 16)
            for n, (name, src) in enumerate(slabs):
                if n == 1:
                    sp.wait_ge(vec_in, 16 * len(VECS1))
                if n >= RING:
                    sp.wait_ge(*freed(n - RING))
                dst = slab_view(n, src.shape[1]) if len(src.shape) == 3 else ring[:, (n % RING) * SLAB:][:, 0:4096]
                sp.dma_start(dst, src).then_inc(slab_in[n % RING], 16)
            def expert_slab(e, j):
                w = A[("w_gate", "w_lin", "w_down")[j // 2]][0]
                src = w[e, :, 512 * (j % 2):512 * (j % 2) + 512] if isinstance(e, int) else \
                    w[bass.DynSlice(e, 1), :, 512 * (j % 2):512 * (j % 2) + 512].rearrange("a k n -> (a k) n")
                sp.dma_start(slot(j), src.rearrange("(c p) n -> p c n", p=P)).then_inc(moe_in[j], 16)

            for j in range(RING):
                sp.wait_ge(*freed(N1 - RING + j))
                expert_slab(0, j)
            with sp.Fori(1, E) as e:
                for j in range(RING):
                    sp.wait_ge(moe_used, e * RING + (j - RING + 1))
                    expert_slab(e, j)
            sp.wait_ge(npass_set, 1)
            npass = sp.value_load(npass_sb[0:1, 0:1], min_val=1, max_val=MAXPASS)
            with sp.If(npass > 1):
                with sp.Fori(1, npass) as p:
                    with sp.Fori(0, E) as e:
                        for j in range(RING):
                            sp.wait_ge(moe_used, p * (E * RING) + e * RING + (j - RING + 1))
                            expert_slab(e, j)
            with sp.Fori(0, 2) as L:
                for n, name in enumerate(slots2):
                    if name not in load2:
                        continue
                    arr, chunks, at0, w = load2[name]
                    sp.wait_ge(*cleared2(n, L))
                    a = A[arr][bass.DynSlice(L, 1)].rearrange("a k n -> (a k) n")
                    src = a[at0:at0 + chunks * P, :] if arr == "w_ffn_down_2" else a[:, at0:at0 + w]
                    sp.dma_start(place2(name), src.rearrange("(c p) n -> p c n", p=P)).then_inc(slab_in[n % RING], 16)
            sp.wait_ge(fin_c, 4)
            for t in range(TT):
                sp.dma_start(out[0, t * P:(t + 1) * P, :], outN[:, t, :]).then_inc(out_done, 16)
            sp.wait_ge(out_done, 16 * TT)

        @block.scalar
        def _(act):
            links = [0]

            def link(ins):
                links[0] += 1
                ins.then_inc(act_chain, 1)
                act.wait_ge(act_chain, links[0])

            for n in FIRST:
                act.dma_start(K[n][:, :], A[n]).then_inc(first_in, 16)
            for name, (r, k) in VECS1.items():
                src = A[name]
                src = src if len(src.shape) == 1 else src.rearrange("a b -> (a b)")
                act.dma_start(vin[r:r + k, :], src.rearrange("(a b) -> a b", b=P)).then_inc(vec_in, 16)
            for L in range(2):
                for name, (r, k) in VECS2.items():
                    src = A[name][L]
                    src = src if len(src.shape) == 1 else src.rearrange("a b -> (a b)")
                    act.dma_start(vin2[L * NV2 + r:L * NV2 + r + k, :], src.rearrange("(a b) -> a b", b=P)).then_inc(vec2_in, 16)
            for n in K:
                if n not in FIRST:
                    act.dma_start(K[n][:, :], A[n]).then_inc(consts_in, 16)
            act.wait_ge(vecs_turned, 1)
            link(act.activation(vT[:, :], bank[7][:, 0:NV1], ACT.Copy))
            act.activation(stage[:, 0:16], vT[:, 0:16], ACT.Sigmoid).then_inc(sig_c, 1)
            def ada_copy(i):
                act.wait_ge(ada_rows, i + 1)
                if i:
                    act.wait_ge(lin_done, G1[f"ada{i - 1}"] + 1)
                act.activation(adaRow[i], bank[G1[f"ada{i}"] % 4][:, :], ACT.Copy).then_inc(ada_copied, 1)

            for c in range(DC):
                act.wait_ge(x_copied, 2 * c + 2)
                act.activation(sq[:, c, 0:T], xT[:, c, :], ACT.Square)
                act.activation(sq[:, c, T:512], hAll[:, c, T:512], ACT.Square).then_inc(sq_done, 1)
            act.wait_ge(vecs2_turned, 1)
            act.activation(v2T[:, :], bank[6][:, 0:2 * NV2], ACT.Copy).then_inc(v2_copied, 1)
            for i in range(4):
                ada_copy(i)
            act.wait_ge(par_done, 1)
            act.activation(rstd, bank[6][:, :], ACT.Copy).then_inc(par_copied, 1)
            act.wait_ge(ms_done, 1)
            act.activation(colA[:, 0:4], colA[:, 0:4], ACT.Sqrt).then_inc(root_done, 1)
            act.wait_ge(gains_done, 1)
            for c in range(DC):
                act.wait_ge(xn_done, c + 1)
                act.activation(hAll[:, c, 0:T], hAll[:, c, 0:T], ACT.Identity, bias=mod[:, c:c + 1],
                               scale=gains[:, 0, c:c + 1])
                act.activation(hAll[:, c, T:512], hAll[:, c, T:512], ACT.Identity, bias=modc[:, c:c + 1],
                               scale=gains[:, 1, c:c + 1]).then_inc(h_done, 1)

            def empty(name, dst, func=ACT.Copy, scale=1.0, src=None):
                g = G1[name]
                act.wait_ge(lin_done, g + 1)
                b = bank[g % 4][:, :]
                act.activation(dst, src(b) if src else b, func, scale=scale).then_inc(lin_act, 1)

            for m in range(4):
                if m == 0:
                    act.wait_ge(x_turned, DC)
                empty(f"na_k{m}", naK[:, m, :])
            for t in range(4):
                empty(f"na_v{t}", naV[:, t, :])
            for m in range(2):
                empty(f"ml_k{m}", mlK[:, m, :])
            for t in range(4):
                empty(f"ml_v{t}", mlV[:, 4 * t:4 * t + 4, 0:128], src=lambda b: b.rearrange("p (a b) -> p a b", a=4))
            for m in range(2):
                empty(f"na_q{m}", naQ[:, 2 * m:2 * m + 2, :], scale=NA_D ** -0.5, src=two)
            empty("ml_q0", mlQ[:, :, :], scale=ML_D ** -0.5, src=two)
            for m in range(2):
                empty(f"ml_o{m}", mlO[:, 2 * m:2 * m + 2, :], ACT.Sigmoid, src=two)
            act.wait_ge(g_pre, 1)
            act.activation(gate[:, :, :], gate[:, :, :], ACT.Tanh, scale=1.0 / SOFTCAP).then_inc(g_tanh, 1)
            act.wait_ge(g_cap, 1)
            link(act.activation(gt2[:, :, :], gt1[:, :, :], ACT.Exp, scale=-1.0))
            act.activation(lsg[:, :, :], gt2[:, :, :], ACT.Ln, bias=1.0).then_inc(g_exp, 1)

            filler = [f"gna{m}" for m in range(4)] + [f"gml{m}" for m in range(4)]
            for i in range(2 * NA_H):
                h, qt = divmod(i, 2)
                act.wait_ge(na_max, i + 1)
                if i >= 2:
                    act.wait_ge(na_pt, i - 1)
                act.activation(Pna[:, i % 2, :], bank[4 + i % 2][:, :], ACT.Exp, bias=nst[:, i:i + 1],
                               accum_out=nst[:, 32 + i:33 + i]).then_inc(na_exp, 1)
                if i >= 8:
                    ada_copy(i - 4)
                if i < 8:
                    name = filler[i]
                    if i == 0:
                        act.wait_ge(sum_done, 1)
                    dst = (gNA if i < 4 else gML)[:, 2 * (i % 4):2 * (i % 4) + 2, :]
                    empty(name, dst, ACT.Sigmoid, src=two)
                act.wait_ge(na_pt, i + 1)
                if qt == 0 and h >= 1:
                    act.wait_ge(na_o, h)
                act.activation(PT[:, :, qt * P:(qt + 1) * P], bank[6][:, :].rearrange("p (a b) -> p a b", a=4),
                               ACT.Copy).then_inc(na_pts, 1)

            for i in range(2 * ML_H):
                h, dr = divmod(i, 2)
                act.wait_ge(ml_b, h + 1)
                act.wait_ge(ml_bm, 2 * h + 2)
                if i == 0:
                    act.wait_ge(na_max, 2 * NA_H)
                if i >= 2:
                    act.wait_ge(ml_o, i - 1)
                w = wml[:, i % 2, :]
                B = bank[6][:, dr * T:dr * T + T]
                kb = lambda tt: keyb[:, tt, 4 * dr + h:4 * dr + h + 1]
                act.activation(w[:, 0:256], B, ACT.Exp, bias=kb(2))
                act.activation(w[:, 256:512], B, ACT.Exp, bias=kb(3))
                Bm = ropeT[:, dr * T:dr * T + T]
                act.activation(w[:, 512:640], Bm[:, 0:128], ACT.Exp, bias=kb(0))
                act.activation(w[:, 640:768], Bm[:, 128:256], ACT.Exp, bias=kb(1))
                far = B[:, 128:256] if dr == 0 else B[:, 0:128]
                act.activation(w[:, 768:896], far, ACT.Exp, bias=kb(0 if dr == 0 else 1)).then_inc(ml_w, 1)
            act.wait_ge(ms_done, 2)
            act.activation(nst[:, 56:64], nst[:, 56:64], ACT.Sqrt).then_inc(root_done, 1)
            def norm(k, src, before=None):
                for c in (0, 4):
                    if before is not None:
                        act.wait_ge(x_done, before + c + 4)
                    act.activation(sq2[:, c:c + 4, :], src[:, c:c + 4, :], ACT.Square).then_inc(n_sq, 1)
                act.wait_ge(n_par, k + 1)
                act.activation(nrow, bank[6][:, 0:T], ACT.Copy).then_inc(n_parc, 1)
                act.wait_ge(n_ms, k + 1)
                act.activation(ncol[:, :], ncol[:, :], ACT.Sqrt).then_inc(n_root, 1)

            act.wait_ge(ml_o, 2 * ML_H)
            act.wait_ge(ml_hts, ML_H)
            act.wait_ge(lin_done, G1["b_ml3"] + 1)
            moe_loads = [(braw[0:E, 0, :], A["b_gate"][0]), (braw[0:E, 1, :], A["b_lin"][0]), (bdraw[0:E, :], A["b_down"][0]),
                         (wr, A["w_router"][0].rearrange("(c p) n -> p c n", p=P)),
                         (brow, A["b_router"][0].partition_broadcast(P))]
            act.dma_start(posi.bitcast(I32), A["positions_2"][0].partition_broadcast(P)).then_inc(pos_in, 16)
            for dst, src in moe_loads:
                act.dma_start(dst, src).then_inc(moe_const, 16)
            for m in range(4):
                empty(f"out{m}", mixT[:, 2 * m:2 * m + 2, :], src=two)
            act.wait_ge(lin_act, emptied(G1["out3"])[1])
            act.wait_ge(lin_dve, emptied(G1["b_ml3"])[1])
            act.wait_ge(c_pos, 1)
            act.activation(sin2, ang, ACT.Sin)
            act.activation(cos2, kf, ACT.Sin).then_inc(c_sin, 1)
            norm(0, mixT)
            act.wait_ge(n_row, 1)
            norm(1, xT, 0)
            for c in range(DC):
                act.wait_ge(n_xn, c + 1)
                act.activation(h2T[:, c, :], tmpx[:, c, :], ACT.Identity, bias=mod[:, 24 + c:25 + c],
                               scale=gpre[:, c:c + 1]).then_inc(h2_done, 1)
            for g in range(4):
                act.wait_ge(h2_turned, g + 1)
                act.activation(h2N[:, g // 2, (g % 2) * 512:(g % 2) * 512 + 512], bank[g][:, :], ACT.Copy).then_inc(h2_copied, 1)
            act.wait_ge(rt_top, 1)
            for t in range(TT):
                ins = act.activation(topp[:, t, 0:TOPK], top[:, t, 0:TOPK], ACT.Exp, bias=rcol[:, t:t + 1],
                                     accum_out=rcol[:, 2 + t:3 + t])
            ins.then_inc(rt_exp, 1)
            act.wait_ge(rt_wt, 1)
            act.activation(weightT[0:E, :], bank[6][0:E, 0:T], ACT.Copy).then_inc(rt_wts, 1)

            act.wait_ge(npass_set, 1)
            npass = act.value_load(npass_sb[0:1, 0:1], min_val=1, max_val=MAXPASS)

            def gathered(n, a):
                act.wait_ge(moe_x, n + 1)
                act.activation(xg, bank[0][:, :], ACT.Copy).then_inc(moe_xs, 1)

            def turned(n, a):
                act.wait_ge(moe_xt, n + 1)
                act.activation(xeT[:, a, :], bank[1][:, :], ACT.Copy).then_inc(moe_xts, 1)

            gathered(0, 0)
            turned(0, 0)
            with act.Fori(0, npass) as p:
                with act.Fori(0, E // 2) as j:
                    it = act.snap(p * (E // 2) + j)
                    act.wait_ge(moe_swt, it + 1)
                    act.activation(selWT, bank[7][:, 0:T], ACT.Copy).then_inc(moe_swts, 1)
                    for a in range(2):
                        n = it * 2 + a
                        act.wait_ge(moe_g2, n + 1)
                        act.activation(es, eg, ACT.Sigmoid, scale=ALPHA).then_inc(moe_sig, 1)
                        gathered(n + 1, 1 - a)
                        act.wait_ge(moe_at, n + 1)
                        act.activation(aT, bank[2][:, :], ACT.Copy).then_inc(moe_ats, 1)
                        turned(n + 1, 1 - a)
                        act.wait_ge(moe_used, n * 6 + 6)
                        for k in range(2):
                            ins = act.activation(yN[a * SLOTS:(a + 1) * SLOTS, k, :], bank[5][k * SLOTS:(k + 1) * SLOTS, :], ACT.Copy)
                        ins.then_inc(moe_ys, 1)
            act.wait_ge(moe_add, npass * (4 * E // 2) + 4)
            norm(2, accT)
            act.wait_ge(x_done, 2 * DC)
            act.dma_start(retmask, A["retmask"].rearrange("p (a b) -> p a b", a=RH)).then_inc(c_const, 16)
            act.dma_start(center, A["center"]).then_inc(c_const, 16)

            with act.Fori(0, 2) as L:
                act.wait_ge(n_row, L * 4 + 3)
                norm(L * 4 + 3, xT, L * (2 * DC) + DC)

                def empty(name, dst, func=ACT.Copy, scale=1.0, src=None):
                    act.wait_ge(*made2(name, L))
                    b = bank[G2[name] % 4][:, :]
                    act.activation(dst, src(b) if src else b, func, scale=scale).then_inc(c_act, 1)

                for i in range(2):
                    empty(f"cu_{i}", convU[:, 2 * i:2 * i + 2, :], src=two)
                for i in range(2):
                    empty(f"cb_{i}", convB[:, 2 * i:2 * i + 2, :], src=two)
                for i in range(2):
                    empty(f"cc_{i}", convC[:, 2 * i:2 * i + 2, :], src=two)
                for i in range(2):
                    empty(f"rq_{i}", retQ[:, 2 * i:2 * i + 2, :], src=two)
                for i in range(2):
                    empty(f"rk_{i}", retK[:, 2 * i:2 * i + 2, :], src=two)
                for i in range(2):
                    empty(f"rv_{i}", retV[:, i, :])
                for i in range(2):
                    empty(f"rg_{i}", retG[:, 2 * i:2 * i + 2, :], ACT.Silu, src=two)
                empty("gq_0", glaQ, scale=GD ** -0.5, src=two)
                empty("gk_0", glaK, src=two)
                for i in range(2):
                    empty(f"gv_{i}", glaV[:, i, :])
                for i in range(2):
                    empty(f"gr_{i}", glaR[:, 2 * i:2 * i + 2, :], ACT.Silu, src=two)
                empty("ga_0", glaA[0:GR, :], src=lambda b: b[0:GR, 0:T])
                act.wait_ge(c_abs, L + 1)
                act.activation(lln, lab, ACT.Exp, scale=-1.0).then_inc(c_exp, 1)
                act.wait_ge(c_exp, L + 1)
                act.activation(lln, lln, ACT.Ln, bias=1.0).then_inc(c_ln, 1)
                gates = {"a": gateA, "b": gateB, "c": gateC}
                order = [(x, i) for x in "abc" for i in range(4)]

                def gate_group(k):
                    x, i = order[k]
                    if k == 8:
                        act.wait_ge(c_conv, L + 1)
                    empty(f"gate{x}_{i}", gates[x][:, 2 * i:2 * i + 2, :], ACT.Sigmoid, src=two)

                act.wait_ge(c_cum, L + 1)
                for h in range(RH):
                    gate_group(2 * h)
                    gate_group(2 * h + 1)
                    act.wait_ge(r_o, L * 8 + (h + 1))
                    act.activation(headY[:, h, :], bank[6][:, 0:T], ACT.Copy).then_inc(r_oc, 1)
                    act.wait_ge(r_c, L * 4 + (h + 1))
                    act.activation(headY[:, h, :], bank[7][:, 0:T], ACT.Copy)
                    act.activation(headSq[:, h, :], bank[7][:, 0:T], ACT.Square).then_inc(r_cc, 1)
                act.wait_ge(h_ms, L * 2 + 1)
                act.activation(hcol, hcol, ACT.Sqrt).then_inc(h_root, 1)
                for m in range(2):
                    for b in range(4):
                        k = 4 * m + b
                        if k >= 2:
                            act.wait_ge(l_s, L * 8 + (k - 1))
                        w = T - 64 * b
                        act.activation(glaEq[:, k % 2, 0:w], glaCum[:, m, 64 * b:T], ACT.Exp, scale=1.0 / TAU, bias=glaNeg[:, m, b:b + 1])
                        act.activation(glaEk[:, k % 2, :], glaCum[:, m, 64 * b:64 * b + 64], ACT.Exp, scale=-1.0 / TAU,
                                       bias=glaPos[:, m, b:b + 1]).then_inc(l_e, 1)
                    for hh in range(2):
                        h = 2 * m + hh
                        gate_group(8 + h)
                        if h == 0:
                            act.wait_ge(h_y, L * 2 + 1)
                        act.wait_ge(r_o, L * 8 + (5 + h))
                        act.activation(headY[:, h, :], bank[6][:, 0:T], ACT.Copy)
                        act.activation(headSq[:, h, :], bank[6][:, 0:T], ACT.Square).then_inc(r_oc, 1)
                act.wait_ge(h_ms, L * 2 + 2)
                act.activation(hcol, hcol, ACT.Sqrt).then_inc(h_root, 1)
                def rounded(k):
                    name = SPLIT[k]
                    act.wait_ge(*loaded2(name, L))
                    act.wait_ge(*cleared2(S2[name + "_hi"], L))
                    n = place2(name).shape[1]
                    for a, b in ((0, n // 2), (n // 2, n)):
                        act.activation(place2(name + "_hi", ringR)[:, a:b, :], place2(name)[:, a:b, :], ACT.Copy).then_inc(w_hi, 1)

                rounded(0)
                rounded(1)
                for i in range(4):
                    empty(f"out_{i}", mixC[:, 2 * i:2 * i + 2, :], src=two)
                act.wait_ge(c_dve, L * NDVE2 + 12)
                act.wait_ge(c_act, L * NACT2 + (sum(b == "act" for b, _, _ in groups2[:G2["out_3"] + 1])))
                norm(L * 4 + 4, mixC)
                act.wait_ge(n_row, L * 4 + 5)
                norm(L * 4 + 5, xT, L * (2 * DC) + 2 * DC)
                for c in range(DC):
                    act.wait_ge(c_h, L * (2 * DC) + (DC + c + 1))
                    act.activation(hH[:, c, :], hLo[:, c, :], ACT.Copy).then_inc(f_hi, 1)

                def hidden(i):
                    act.wait_ge(*emptied2(G2[f"fu_{i}"], L))
                    act.activation(fH[:, 2 * i:2 * i + 2, :], fLo[:, 2 * i:2 * i + 2, :], ACT.Copy).then_inc(f_hi, 1)

                for i in range(11):
                    if i >= 4:
                        act.wait_ge(*emptied2(G2[f"fu_{i - 4}"], L))
                    empty(f"fg_{i}", fS[:, i % 4, :], ACT.Silu)
                    rounded(i + 2)
                    if i >= 2:
                        hidden(i - 2)
                hidden(9)
                hidden(10)
                for k in range(13, NSPLIT):
                    rounded(k)
                act.wait_ge(*made2("fd_6", L))
                for i in range(4):
                    ins = act.activation(ffT[:, 2 * i:2 * i + 2, :], two(bank[i][:, :]), ACT.Copy)
                ins.then_inc(fin_t, 1)
                act.wait_ge(fin_t, L + 1)
                norm(L * 4 + 6, ffT)

        @block.tensor
        def _(pe):
            def slab(name):
                n = S1[name]
                pe.wait_ge(slab_in[n % RING], 16 * (n // RING + 1))
                return slab_view(n, slabs[n][1].shape[1])

            def open_bank(name):
                g = G1[name]
                if g < 4:
                    pe.wait_ge(x_copied, 2 * DC)
                else:
                    pe.wait_ge(*emptied(g - 4))
                return bank[g % 4]

            pe.wait_ge(first_in, 16 * len(FIRST))
            pe.wait_ge(vec_in, 16 * len(VECS1))
            pe.transpose(bank[7][:, 0:NV1], vin[0:NV1, :], K["ident"][0:NV1, 0:NV1]).then_inc(vecs_turned, 1)
            pe.wait_ge(x_in, 64)
            for c in range(DC):
                if c >= 4:
                    pe.wait_ge(x_copied, 2 * (c - 4) + 2)
                for t in range(4):
                    last = pe.transpose(bank[c % 4][:, t * P:(t + 1) * P], xin[:, t, c * P:(c + 1) * P], K["ident"][:, :])
                last.then_inc(x_turned, 1)
            pe.wait_ge(vec2_in, 16 * 2 * len(VECS2))
            pe.transpose(bank[6][:, 0:2 * NV2], vin2[0:2 * NV2, :], K["ident"][0:2 * NV2, 0:2 * NV2]).then_inc(vecs2_turned, 1)

            def ada(i):
                w = slab(f"ada{i}")
                b = open_bank(f"ada{i}")
                for c in range(DC):
                    r = 32 * (c % 4)
                    last = pe.matmul(b[r:r + 32, :], scol[:, c, :], w[:, c, :], start=(c < 4), stop=(c >= 4), skip_group_check=True)
                last.then_inc(ada_rows, 1)

            def ada_turn(i):
                pe.wait_ge(ada_copied, i + 1)
                b = bank[G1[f"ada{i}"] % 4]
                for m in range(4):
                    last = pe.matmul(b[:, 2 * m:2 * m + 2], adaRow[i][:, m * P:(m + 1) * P], K["pick"][:, :], start=True, stop=True)
                last.then_inc(lin_done, 1)

            pe.wait_ge(silu_done, 1)
            for i in range(4):
                ada(i)
                if i:
                    ada_turn(i - 1)
            ada_turn(3)
            pe.wait_ge(sq_done, DC)
            pe.wait_ge(v2_copied, 1)
            for c in range(DC):
                r = 32 * (c % 4)
                last = pe.matmul(bank[6][r:r + 32, :], ones[:, 0:32], sq[:, c, :], start=(c < 4), stop=(c >= 4), skip_group_check=True)
            last.then_inc(par_done, 1)
            pe.wait_ge(par_copied, 1)
            for t in range(4):
                last = pe.matmul(bank[6][:, t:t + 1], rstd[:, t * P:(t + 1) * P], K["pick"][:, 0:1], start=True, stop=True)
            last.then_inc(sum_done, 1)
            pe.wait_ge(rstd_done, 1)
            for t in range(4):
                last = pe.matmul(bank[5][:, t * P:(t + 1) * P], colA[:, t:t + 1].to_broadcast([P, P]), K["ident"][:, :],
                                 start=True, stop=True)
            last.then_inc(rstd_row, 1)

            def feat(name, w, m, half, rhs, dst, kc=DC, base=0):
                for c in range(kc):
                    last = pe.matmul(dst, w[:, c, base + m * P:base + (m + 1) * P], rhs(c), start=(c == 0), stop=(c == kc - 1))
                return last

            for c in range(DC):
                pe.wait_ge(h_done, c + 1)
            lat = lambda c: hAll[:, c, 0:T]
            both = lambda c: hAll[:, c, :]
            for nm, tiles in (("na_k", 4), ("na_v", 4), ("ml_k", 2), ("ml_v", 4)):
                w = slab(nm)
                for m in range(tiles):
                    b = open_bank(f"{nm}{m}")
                    if nm in ("na_k", "ml_k"):
                        last = feat(nm, w, m, 0, both, b[:, :])
                    else:
                        for c in range(DC):
                            last = pe.matmul(b[:, :], hAll[:, c, m * P:(m + 1) * P], w[:, c, :], start=(c == 0), stop=(c == DC - 1))
                    last.then_inc(lin_done, 1)
            w = slab("ml_g")
            b = open_bank("ml_g")
            for t in range(4):
                for c in range(DC):
                    last = pe.matmul(b[:, 16 * t:16 * t + 16], hAll[:, c, t * P:(t + 1) * P], w[:, c, :], start=(c == 0), stop=(c == DC - 1))
            last.then_inc(lin_done, 1)

            def pair(name, w, i, rhs, kc=DC):
                b = open_bank(name)
                for j in range(2):
                    last = feat(name, w, 2 * i + j, j, rhs, b[:, j * T:(j + 1) * T], kc)
                last.then_inc(lin_done, 1)


            for nm, prs in (("na_q", 2), ("ml_q", 1), ("ml_o", 2)):
                w = slab(nm)
                for i in range(prs):
                    pair(f"{nm}{i}", w, i, lat)
            pe.wait_ge(consts_in, 16 * (len(K) - len(FIRST)))
            pe.wait_ge(*emptied(G1["ml_q0"]))
            for m in range(2):
                pe.matmul(bank[4][:, m * T:(m + 1) * T], K["rot16"][:, :], mlQ[:, m, :], start=True, stop=True)
                last = pe.matmul(bank[5][:, m * T:(m + 1) * T], K["rot16"][:, :], mlK[:, m, 0:T], start=True, stop=True)
            last.then_inc(ml_rot, 1)
            pe.wait_ge(consts_in, 16 * (len(K) - len(FIRST)))
            pe.wait_ge(g_lf, 1)
            order = {0: [2, 3, 0, 1], 1: [3, 2, 1, 0]}
            for dr in range(2):
                own = K["tri"][:, 0:128] if dr == 0 else K["ltri"][:, 128:256]
                for k, tt in enumerate(order[dr]):
                    dst = bank[6][:, 8 * tt + 4 * dr:8 * tt + 4 * dr + 4]
                    for j in range(k):
                        pe.matmul(dst, ones[:, 0:128], lsg[:, order[dr][j], 4 * dr:4 * dr + 4], start=(j == 0), stop=False)
                    last = pe.matmul(dst, own, lsg[:, tt, 4 * dr:4 * dr + 4], start=(k == 0), stop=True)
            last.then_inc(g_cum, 1)

            pe.wait_ge(relrhs_in, 16 * (2 * NA_H))
            pe.wait_ge(ml_rope, 1)
            for b in range(7):
                if b >= 2:
                    pe.wait_ge(rel_copied, b - 1)
                for k in range(10 * b, min(10 * b + 10, 64)):
                    if k in (0, 32):
                        slab(f"rel{k // 32}")
                        sl = ring[:, (S1[f"rel{k // 32}"] % RING) * SLAB:][:, 0:4096].rearrange("p (k q) -> p k q", k=32)
                    last = pe.matmul(bank[4 + b % 2][:, 48 * (k - 10 * b):48 * (k - 10 * b) + 48], sl[0:63, k % 32, :],
                                     relrhs[0:63, :], start=True, stop=True)
                last.then_inc(rel_done, 1)

            fillers = []
            for nm, i in [(a, i) for a in ("gna", "gml") for i in range(4)]:
                def f(nm=nm, i=i):
                    w = slab(f"{nm}{i // 2}")
                    pair(f"{nm}{i}", w, i % 2, lat)
                fillers.append(f)
            for i in range(4, 12):
                fillers.append(lambda i=i: (ada(i), ada_turn(i)))

            def scores(i):
                h, qt = divmod(i, 2)
                r = 64 * (h % 2)
                if i >= 2:
                    pe.wait_ge(na_exp, i - 1)
                if i < 2:
                    pe.wait_ge(ml_rope, 1)
                    pe.wait_ge(rel_copied, 7)
                pe.matmul(bank[4 + i % 2][:, :], naQ[r:r + 64, h // 2, qt * P:(qt + 1) * P], naK[r:r + 64, h // 2, :],
                          start=True, stop=True).then_inc(na_s, 1)

            def head_out(h):
                r = 64 * (h % 2)
                pe.wait_ge(na_pts, 2 * h + 2)
                if h >= 1:
                    pe.wait_ge(na_os, h)
                for k in range(4):
                    last = pe.matmul(bank[7][r:r + 64, 0:T][:, :], naV[:, k, h * 64:h * 64 + 64], PT[:, k, :],
                                     start=(k == 0), stop=(k == 3), skip_group_check=True)
                last.then_inc(na_o, 1)

            scores(0)
            for i in range(2 * NA_H):
                if i + 1 < 2 * NA_H:
                    scores(i + 1)
                fillers[i]()
                pe.wait_ge(na_p, i + 1)
                if i >= 1:
                    pe.wait_ge(na_pts, i)
                else:
                    pe.wait_ge(g_keyb, 1)
                for k in range(4):
                    last = pe.transpose(bank[6][:, k * P:(k + 1) * P], Pna[:, i % 2, k * P:(k + 1) * P], K["ident"][:, :])
                last.then_inc(na_pt, 1)
                if i % 2:
                    head_out(i // 2)

            def ml_scores(h):
                r = 64 * (h % 2)
                if h >= 1:
                    pe.wait_ge(ml_p, 2 * h)
                    pe.wait_ge(ml_w, 2 * h)
                else:
                    pe.wait_ge(na_exp, 2 * NA_H)
                    pe.wait_ge(na_pts, 2 * NA_H)
                    pe.wait_ge(ml_rope, 1)
                for tt in range(4):
                    last = pe.matmul(bank[4 + tt // 2][:, (tt % 2) * T:(tt % 2) * T + T],
                                     mlK[r:r + 64, h // 2, tt * P:(tt + 1) * P], mlQ[r:r + 64, h // 2, :],
                                     start=True, stop=True)
                last.then_inc(ml_s, 1)
                for dr in range(2):
                    B = bank[6][:, dr * T:(dr + 1) * T]
                    lf = lambda tt: lsg[:, tt, 4 * dr + h:4 * dr + h + 1].to_broadcast([P, P])
                    pe.matmul(B, lf(2), ones[:, :], start=True, stop=False)
                    if dr == 0:
                        pe.matmul(B[:, 128:256], lf(1), K["tri"][:, 0:128], start=False, stop=False)
                        pe.matmul(B, lf(0), K["tri"][:, :], start=False, stop=False)
                    else:
                        pe.matmul(B[:, 0:128], lf(0), K["ltri"][:, 128:256], start=False, stop=False)
                        pe.matmul(B, lf(1), K["ltri"][:, :], start=False, stop=False)
                    last = pe.matmul(B, lf(3), ones[:, :], start=False, stop=True)
                last.then_inc(ml_b, 1)

            def ml_out(i):
                h, dr = divmod(i, 2)
                pe.wait_ge(ml_p, i + 1)
                if i >= 1:
                    pe.wait_ge(ml_os, i)
                else:
                    pe.wait_ge(na_os, NA_H)
                w = wml[:, i % 2, :]
                for qt in range(2):
                    parts = [(w[:, qt * P:(qt + 1) * P], 2), (w[:, 256 + qt * P:256 + (qt + 1) * P], 3),
                             (w[:, 512 + qt * P:512 + (qt + 1) * P], qt)]
                    if dr == 0 and qt == 1:
                        parts.append((w[:, 768:896], 0))
                    if dr == 1 and qt == 0:
                        parts.append((w[:, 768:896], 1))
                    for k, (lhsT, tt) in enumerate(parts):
                        last = pe.matmul(bank[7][:, 129 * qt:129 * qt + 129], lhsT, mlV[:, 4 * tt + h, :],
                                         start=(k == 0), stop=(k == len(parts) - 1))
                last.then_inc(ml_o, 1)

            def branch(nm, i, o):
                w = slab(nm)
                pair(f"{nm}{i}", w, i, lambda c: o[:, c, :], 4)

            pe.wait_ge(na_os, NA_H)
            for h in range(ML_H):
                ml_scores(h)
                branch("b_na", h, oNaT)
                ml_out(2 * h)
                ml_out(2 * h + 1)
            for h in range(ML_H):
                pe.wait_ge(ml_hn, h + 1)
                for qt in range(2):
                    last = pe.transpose(bank[4 + h % 2][:, qt * P:(qt + 1) * P], hml[:, qt, h * P:(h + 1) * P], K["ident"][:, :])
                    if h >= 2 and qt == 0:
                        pass
                last.then_inc(ml_ht, 1)
                if h + 1 >= 2 and h + 1 < ML_H:
                    pe.wait_ge(ml_hts, h)
            pe.wait_ge(ml_hts, ML_H)
            for i in range(4):
                branch("b_ml", i, oMlT)
            pe.wait_ge(*emptied(G1["b_ml3"]))
            for i in range(4):
                w = slab(f"out{i // 2}")
                pair(f"out{i}", w, i % 2, lambda c: merged[:, c, :])
            def norm(k, n0):
                for c in range(DC):
                    if c % 4 == 0:
                        pe.wait_ge(n_sq, k * 2 + (c // 4 + 1))
                    r = 32 * (c % 4)
                    last = pe.matmul(bank[6][r:r + 32, 0:T], ones[:, 0:32], sq2[:, c, :], start=(c < 4), stop=(c >= 4),
                                     skip_group_check=True)
                last.then_inc(n_par, 1)
                pe.wait_ge(n_parc, k + 1)
                for t in range(TT):
                    last = pe.matmul(bank[6][:, t:t + 1], nrow[:, t * P:(t + 1) * P], K["pick"][:, 0:1], start=True, stop=True)
                last.then_inc(n_sum, 1)
                pe.wait_ge(n_col, k + 1)
                for t in range(TT):
                    last = pe.matmul(bank[7][:, t * P:(t + 1) * P], ncol[:, t:t + 1].to_broadcast([P, P]), K["ident"][:, :],
                                     start=True, stop=True)
                last.then_inc(n_row, 1)

            norm(0, DC * 0)
            pe.wait_ge(moe_const, 16 * 5)
            norm(1, DC)
            pe.wait_ge(h2_done, DC)
            pe.wait_ge(n_xn, DC)
            for t in range(TT):
                for c in range(DC):
                    last = pe.matmul(bank[7][:, t * E:(t + 1) * E], h2T[:, c, t * P:(t + 1) * P], wr[:, c, :],
                                     start=(c == 0), stop=(c == DC - 1))
            last.then_inc(rt_log, 1)
            for g in range(4):
                pe.wait_ge(lin_act, emptied(G1["out3"])[1])
                for k in range(4):
                    c = 4 * (g % 2) + k
                    last = pe.transpose(bank[g][:, k * P:(k + 1) * P], h2T[:, c, (g // 2) * P:(g // 2 + 1) * P], K["ident"][:, :])
                last.then_inc(h2_turned, 1)
            pe.wait_ge(rt_sel, 1)
            pe.matmul(bank[5][:, 0:E], K["tri"][:, 0:P], chosen[:, 0, :], start=True, stop=True)
            pe.matmul(bank[5][:, E:2 * E], ones[:, 0:P], chosen[:, 0, :], start=True, stop=False)
            pe.matmul(bank[5][:, E:2 * E], K["tri"][:, 0:P], chosen[:, 1, :], start=False, stop=True)
            pe.matmul(bank[5][:, 2 * E:3 * E], ones[:, 0:P], chosen[:, 0, :], start=True, stop=False)
            pe.matmul(bank[5][:, 2 * E:3 * E], ones[:, 0:P], chosen[:, 1, :], start=False, stop=True).then_inc(rt_cnt, 1)
            pe.wait_ge(rt_sel, 2)
            for t in range(TT):
                last = pe.transpose(bank[6][0:E, t * P:(t + 1) * P], weight[:, t, :], K["ident"][:, :])
            last.then_inc(rt_wt, 1)
            pe.wait_ge(rt_wts, 1)
            for g in range(4):
                pe.wait_ge(h2_copied, g + 1)
                for k in range(2):
                    last = pe.matmul(bank[g][:, k * T:(k + 1) * T], bdraw[0:E, (2 * g + k) * P:(2 * g + k + 1) * P],
                                     weightT[0:E, :], start=True, stop=True)
                last.then_inc(acc_ps, 1)
            pe.wait_ge(moe_add, 4)

            pe.wait_ge(npass_set, 1)
            npass = pe.value_load(npass_sb[0:1, 0:1], min_val=1, max_val=MAXPASS)

            def gather(n, a):
                for t in range(TT):
                    for k in range(2):
                        last = pe.matmul(bank[0][k * SLOTS:(k + 1) * SLOTS, :], selS[:, a, t, :], h2N[:, t, k * 512:(k + 1) * 512],
                                         start=(t == 0), stop=(t == TT - 1), skip_group_check=True)
                last.then_inc(moe_x, 1)

            def turn(n):
                pe.wait_ge(moe_xs, n + 1)
                for q in range(4):
                    last = pe.transpose(bank[1][:, q * P:(q + 1) * P], xg[:, q * P:(q + 1) * P], K["ident"][:, :])
                last.then_inc(moe_xt, 1)

            def products(n, w, b, lhsT, bias):
                for k in range(2):
                    pe.wait_ge(moe_in[2 * w + k], n * 16 + 16)
                if bias is not None:
                    for k in range(2):
                        pe.matmul(bank[b][k * SLOTS:(k + 1) * SLOTS, :], bias, braw[0:E, w, k * 512:(k + 1) * 512],
                                  start=True, stop=False, skip_group_check=True)
                for c in range(DC):
                    for k in range(2):
                        last = pe.matmul(bank[b][k * SLOTS:(k + 1) * SLOTS, :], lhsT(c), slot(2 * w + k)[:, c, :],
                                         start=(c == 0 and bias is None), stop=(c == DC - 1), skip_group_check=True)
                last.then_inc(moe_used, 2)

            def experts_in(n, a, w, b):
                products(n, w, b, lambda c: xeT[:, a, (c % 4) * P + (c // 4) * SLOTS:][:, 0:SLOTS], expertSel[0:E, a, :])

            pe.wait_ge(moe_sel, 1)
            gather(0, 0)
            turn(0)
            with pe.Fori(0, npass) as p:
                with pe.Fori(0, E // 2) as j:
                    it = pe.snap(p * (E // 2) + j)
                    pe.wait_ge(moe_sel, it + 2)
                    for t in range(TT):
                        last = pe.transpose(bank[7][:, t * P:(t + 1) * P], selW[:, t, :], K["ident"][:, :])
                    last.then_inc(moe_swt, 1)
                    for a in range(2):
                        n = it * 2 + a
                        pe.wait_ge(moe_xts, n + 1)
                        experts_in(n, a, 0, 3)
                        experts_in(n, a, 1, 4)
                        gather(n + 1, 1 - a)
                        pe.wait_ge(moe_a, n + 1)
                        for q in range(4):
                            last = pe.transpose(bank[2][:, q * P:(q + 1) * P], ea[:, q * P:(q + 1) * P], K["ident"][:, :])
                        last.then_inc(moe_at, 1)
                        turn(n + 1)
                        pe.wait_ge(moe_ats, n + 1)
                        if a == 1:
                            pe.wait_ge(moe_ys, n)
                        products(n, 2, 5, lambda c: aT[:, (c % 4) * P + (c // 4) * SLOTS:][:, 0:SLOTS], None)
                    pe.wait_ge(moe_ys, it * 2 + 2)
                    pe.wait_ge(moe_swts, it + 1)
                    for g in range(4):
                        if g >= 2:
                            pe.wait_ge(moe_add, it * 4 + (g + 3))
                        for k in range(2):
                            c = 2 * g + k
                            last = pe.matmul(bank[6 + g % 2][:, k * T:(k + 1) * T], yN[:, c // 4, (c % 4) * P:(c % 4 + 1) * P],
                                             selWT, start=True, stop=True)
                        last.then_inc(moe_sc, 1)
            pe.matmul(bank[5][:, 0:1], K["ident"][:, :], ones[:, 0:1], start=True, stop=True).then_inc(c_lin, NG2)
            pe.wait_ge(moe_add, npass * (4 * E // 2) + 4)
            norm(2, 2 * DC)
            with pe.Fori(0, 2) as L:
                def slab2(name):
                    pe.wait_ge(*loaded2(name, L))
                    return place2(name)

                def open2(name):
                    g = G2[name]
                    if g >= 4:
                        pe.wait_ge(*emptied2(g - 4, L))
                    return bank[g % 4]

                def pair2(w, name, i, rhs, kc=DC):
                    b = open2(name)
                    for j in range(2):
                        last = feat(name, w, 2 * i + j, j, rhs, b[:, j * T:(j + 1) * T], kc)
                    last.then_inc(c_lin, 1)

                def rows2(w, name, t):
                    b = open2(name)
                    for c in range(DC):
                        last = pe.matmul(b[:, :], hT[:, c, t * P:(t + 1) * P], w[:, c, :], start=(c == 0), stop=(c == DC - 1))
                    last.then_inc(c_lin, 1)

                norm(L * 4 + 3, (L * 4 + 3) * DC)
                pe.wait_ge(c_h, L * (2 * DC) + DC)
                lat2 = lambda c: hT[:, c, :]
                for nm in ("cu", "cb", "cc", "rq", "rk"):
                    w = slab2(nm)
                    for i in range(2):
                        pair2(w, f"{nm}_{i}", i, lat2)
                w = slab2("rv")
                rows2(w, "rv_0", 0)
                pe.wait_ge(*emptied2(G2["rk_1"], L))
                for h in range(RH):
                    pe.matmul(bank[4 + h // 2][:, (h % 2) * T:(h % 2 + 1) * T], K["rot64"][:, :], retQ[:, h, :], start=True, stop=True)
                for h in range(RH):
                    last = pe.matmul(bank[6 + h // 2][:, (h % 2) * T:(h % 2 + 1) * T], K["rot64"][:, :], retK[:, h, :], start=True, stop=True)
                last.then_inc(c_rot, 1)
                rows2(w, "rv_1", 1)
                w = slab2("rg")
                for i in range(2):
                    pair2(w, f"rg_{i}", i, lat2)
                for nm in ("gq", "gk"):
                    pair2(slab2(nm), f"{nm}_0", 0, lat2)
                w = slab2("gv")
                for t in range(2):
                    rows2(w, f"gv_{t}", t)
                w = slab2("gr")
                for i in range(2):
                    pair2(w, f"gr_{i}", i, lat2)
                w = slab2("ga")
                b = open2("ga_0")
                for c in range(DC):
                    last = pe.matmul(b[0:GR, 0:T], w[:, c, :], hT[:, c, :], start=(c == 0), stop=(c == DC - 1))
                last.then_inc(c_lin, 1)
                pe.wait_ge(*emptied2(G2["ga_0"], L))
                pe.wait_ge(c_wa2, L * 16 + 16)
                pe.wait_ge(c_rope, L + 1)
                for m in range(2):
                    last = pe.matmul(bank[4][:, m * T:(m + 1) * T], wa2[0:GR, m * P:(m + 1) * P], glaA[0:GR, :], start=True, stop=True)
                last.then_inc(c_lg, 1)

                order = [(x, i) for x in "abc" for i in range(4)]

                def gate_group(k):
                    x, i = order[k]
                    pair2(slab2(f"g{x}{i // 2}"), f"gate{x}_{i}", i % 2, lat2)

                def attend(v, h, p):
                    d = bank[6]
                    val = lambda t: v[:, t, h * P:(h + 1) * P]
                    pe.matmul(d[:, 0:P], val(0), p[:, 0:128], start=True, stop=True)
                    pe.matmul(d[:, P:T], val(0), p[:, 128:256], start=True, stop=False)
                    pe.matmul(d[:, P:T], val(1), p[:, 256:384], start=False, stop=True).then_inc(r_o, 1)

                def ret_scores(h):
                    b = bank[4 + h % 2]
                    if h == 0:
                        pe.wait_ge(c_abs, L + 1)
                        pe.wait_ge(c_const, 32)
                    if h >= 2:
                        pe.wait_ge(r_p, L * 4 + (h - 1))
                    pe.matmul(b[:, 0:T], retK[:, h, 0:P], retQ[:, h, :], start=True, stop=True)
                    pe.matmul(b[:, T:T + P], retK[:, h, P:T], retQ[:, h, P:T], start=True, stop=True).then_inc(r_s, 1)

                ret_scores(0)
                for h in range(RH):
                    gate_group(2 * h)
                    if h + 1 < RH:
                        ret_scores(h + 1)
                    pe.wait_ge(r_p, L * 4 + (h + 1))
                    if h >= 1:
                        pe.wait_ge(r_oc, L * 8 + h)
                    attend(retV, h, retP[:, h % 2, :])
                    gate_group(2 * h + 1)
                    pe.wait_ge(r_oc, L * 8 + (h + 1))
                    if h >= 1:
                        pe.wait_ge(r_cc, L * 4 + h)
                    pe.matmul(bank[7][:, 0:T], center, headY[:, h, :], start=True, stop=True).then_inc(r_c, 1)

                def head_sums(k):
                    for h in range(4):
                        for t in range(TT):
                            last = pe.matmul(bank[7][:, 256 + 2 * h + t:257 + 2 * h + t], headSq[:, h, t * P:(t + 1) * P], ones[:, 0:1],
                                             start=True, stop=True)
                    last.then_inc(h_sum, 1)

                def head_rows(k):
                    pe.wait_ge(h_col, L * 2 + (k + 1))
                    for h in range(4):
                        for t in range(TT):
                            last = pe.matmul(bank[4 + h // 2][:, (h % 2) * T + t * P:(h % 2) * T + (t + 1) * P],
                                             hcol[:, 2 * h + t:2 * h + t + 1].to_broadcast([P, P]), K["ident"][:, :],
                                             start=True, stop=True)
                    last.then_inc(h_row, 1)

                pe.wait_ge(r_cc, L * 4 + 4)
                head_sums(0)
                head_rows(0)
                for m in range(2):
                    for b in range(4):
                        k = 4 * m + b
                        pe.wait_ge(l_q, L * 8 + (k + 1))
                        if b == 0:
                            if m == 0:
                                pe.wait_ge(h_y, L * 2 + 1)
                            else:
                                pe.wait_ge(l_p, L * 4 + 2)
                        pe.nop(nofuse=True)
                        w = T - 64 * b
                        col = 64 * b if b < 2 else T + 64 * (b - 2)
                        r = 64 * (b % 2)
                        for hh in range(2):
                            s = 64 * hh
                            last = pe.matmul(bank[4 + hh][r:r + 64, col:col + w], glaEk[s:s + 64, k % 2, :], glaEq[s:s + 64, k % 2, 0:w],
                                             start=True, stop=True, skip_group_check=True)
                        last.then_inc(l_s, 1)
                    for hh in range(2):
                        h = 2 * m + hh
                        gate_group(8 + h)
                        pe.wait_ge(l_p, L * 4 + (h + 1))
                        if h == 0:
                            pe.wait_ge(r_oc, L * 8 + 4)
                        else:
                            pe.wait_ge(r_oc, L * 8 + 4 + h)
                        attend(glaV, h, glaP[:, hh, :])
                pe.wait_ge(r_oc, L * 8 + 8)
                head_sums(1)
                head_rows(1)
                pe.wait_ge(h_y, L * 2 + 2)
                for x, y in (("a", yA), ("b", yB), ("c", yC)):
                    w = slab2(f"br{x}")
                    for i in range(4):
                        pair2(w, f"br{x}_{i}", i, lambda c, y=y: y[:, c, :], 4)
                pe.wait_ge(c_dve, L * NDVE2 + 12)
                for i in range(4):
                    pair2(slab2(f"out{i // 2}"), f"out_{i}", i % 2, lambda c: mergedC[:, c, :])
                norm(L * 4 + 4, (L * 4 + 4) * DC)
                norm(L * 4 + 5, (L * 4 + 5) * DC)
                def split2(name):
                    pe.wait_ge(w_hi, L * (2 * NSPLIT) + 2 * SPLIT.index(name) + 2)
                    return place2(name + "_hi", ringR), place2(name, ringR)

                def rest2(name):
                    pe.wait_ge(w_lo, L * (2 * NSPLIT) + 2 * SPLIT.index(name) + 2)

                pe.wait_ge(f_hi, L * (DC + NHID) + DC)
                for i in range(6):
                    for nm in ("fg", "fu"):
                        wH, wL = split2(f"{nm}{i}")
                        for k in range(2 if i < 5 else 1):
                            b = open2(f"{nm}_{2 * i + k}")
                            for part, (w, h) in enumerate(((wH, hH), (wH, hL), (wL, hH))):
                                if part == 1 and i == 0 and nm == "fg" and k == 0:
                                    pe.wait_ge(f_lo, L * (2 + NHID) + 2)
                                if part == 2 and k == 0:
                                    rest2(f"{nm}{i}")
                                for j in range(2):
                                    m = 2 * k + j
                                    for c in range(DC):
                                        last = pe.matmul(b[:, j * T:(j + 1) * T], w[:, c, m * P:(m + 1) * P], h[:, c, :],
                                                         start=(part == 0 and c == 0 and j == 0), stop=(part == 2 and c == DC - 1),
                                                         skip_group_check=True)
                            last.then_inc(c_lin, 1)
                pe.wait_ge(*emptied2(G2["fu_10"], L))
                pe.wait_ge(*emptied2(G2["fg_10"], L))
                for i, (c0, kc) in enumerate(DOWN):
                    wH, wL = split2(f"fd{i}")
                    pe.wait_ge(f_lo, L * (2 + NHID) + 2 + (c0 + kc + 1) // 2)
                    for part, (w, h) in enumerate(((wH, fH), (wH, fL), (wL, fH))):
                        if part == 2:
                            rest2(f"fd{i}")
                        for k in range(kc):
                            for m in range(DC):
                                last = pe.matmul(bank[m // 2][:, (m % 2) * T:(m % 2 + 1) * T], w[:, k, m * P:(m + 1) * P],
                                                 h[:, c0 + k, :], start=(part == 0 and c0 + k == 0 and m % 2 == 0),
                                                 stop=(part == 2 and c0 + k == FC - 1), skip_group_check=True)
                    last.then_inc(c_lin, 1)
                norm(L * 4 + 6, (L * 4 + 6) * DC)
            pe.wait_ge(x_done, 6 * DC)
            for g in range(4):
                for k in range(4):
                    c = 4 * (g % 2) + k
                    last = pe.transpose(bank[g][:, k * P:(k + 1) * P], xT[:, c, (g // 2) * P:(g // 2 + 1) * P], K["ident"][:, :])
                last.then_inc(fin_t, 1)

        @block.vector
        def _(dve):
            links = [0]

            def link(ins):
                links[0] += 1
                ins.then_inc(dve_chain, 1)
                dve.wait_ge(dve_chain, links[0])

            dve.memset(relrhs[:, :], 1.0).then_inc(ones_set, 1)
            dve.memset(ones[:, :], 1.0)
            link(dve.memset(scol[:, :, :], 0.0))
            dve.wait_ge(sig_c, 1)
            vcol = lambda n: vT[:, VECS1[n][0]:VECS1[n][0] + VECS1[n][1]]
            dve.tensor_tensor(scol[:, :, 0], vT[:, 0:8], stage[:, 0:8], ALU.mult)
            dve.tensor_tensor(scol[:, :, 1], vT[:, 8:16], stage[:, 8:16], ALU.mult).then_inc(silu_done, 1)
            for c in range(DC):
                dve.wait_ge(x_turned, c + 1)
                dve.tensor_copy(xT[:, c, :], bank[c % 4][:, 0:T]).then_inc(x_copied, 1)
                dve.tensor_copy(hAll[:, c, T:512], bank[c % 4][:, T:512]).then_inc(x_copied, 1)
            ba = VECS1["b_ada"][0]

            def modulation(i):
                g = G1[f"ada{i}"]
                ps = bank[g % 4][:, 0:8].rearrange("p (m a) -> p m a", a=2)
                vb = vT[:, ba + 4 * i:ba + 4 * i + 4]
                dve.wait_ge(lin_done, g + 1)
                if i < 4:
                    dve.tensor_tensor(modc[:, 4 * i:4 * i + 4], ps[:, :, 1], vb, ALU.add)
                dve.tensor_tensor(mod[:, 4 * i:4 * i + 4], ps[:, :, 0], vb, ALU.add).then_inc(lin_dve, 1)

            for i in range(4):
                modulation(i)
            dve.wait_ge(*emptied(G1["ada3"]))
            dve.scalar_tensor_tensor(out=gains[:, 0, :], in0=mod[:, 8:16], scalar=1.0, in1=vcol("g_mix_pre"),
                                     op0=ALU.add, op1=ALU.mult)
            dve.scalar_tensor_tensor(out=gains[:, 1, :], in0=modc[:, 8:16], scalar=1.0, in1=vcol("g_mix_pre"),
                                     op0=ALU.add, op1=ALU.mult).then_inc(gains_done, 1)
            dve.wait_ge(sum_done, 1)
            dve.tensor_scalar(colA[:, 0:4], bank[6][:, 0:4], 1.0 / D, EPS, ALU.mult, ALU.add).then_inc(ms_done, 1)
            dve.wait_ge(root_done, 1)
            dve.reciprocal(colA[:, 0:4], colA[:, 0:4]).then_inc(rstd_done, 1)
            dve.wait_ge(rstd_row, 1)
            for c in range(DC):
                dve.tensor_tensor(hAll[:, c, 0:T], xT[:, c, :], bank[5][:, 0:T], ALU.mult)
                dve.tensor_tensor(hAll[:, c, T:512], hAll[:, c, T:512], bank[5][:, T:512], ALU.mult).then_inc(xn_done, 1)
            dve.memset(mlV[:, :, 128:129], 1.0).then_inc(ones_set, 1)
            dve.wait_ge(lin_done, G1["ml_g"] + 1)
            dve.wait_ge(bg_in, 16)
            dve.tensor_tensor(gate[:, :, :], bank[G1["ml_g"] % 4][:, 0:64].rearrange("p (a b) -> p a b", a=4),
                              bg[:, None, :].to_broadcast([P, 4, 16]), ALU.add).then_inc(lin_dve, 1)
            dve.wait_ge(*emptied(G1["ml_g"]))
            dve.memset(stage[:, 61:62], 0.0).then_inc(g_pre, 1)
            dve.wait_ge(g_tanh, 1)
            link(dve.tensor_scalar(gate[:, :, :], gate[:, :, :], SOFTCAP, None, ALU.mult))
            gf = gate[:, :, :].rearrange("p t (d k h) -> p t d k h", d=2, k=2)
            for dr in range(2):
                ins = dve.scalar_tensor_tensor(out=gt1[:, :, 4 * dr:4 * dr + 4], in0=gf[:, :, dr, 1, :], scalar=-1.0,
                                               in1=gf[:, :, dr, 1, :], op0=ALU.mult, op1=ALU.max)
            ins.then_inc(g_cap, 1)
            dve.wait_ge(g_exp, 1)
            for dr in range(2):
                link(dve.scalar_tensor_tensor(out=lsg[:, :, 4 * dr:4 * dr + 4], in0=gf[:, :, dr, 1, :], scalar=0.0,
                                              in1=lsg[:, :, 4 * dr:4 * dr + 4], op0=ALU.min, op1=ALU.subtract))
            dve.memset(stage[:, 61:62], 0.0).then_inc(g_lf, 1)
            dve.wait_ge(ml_rot, 1)
            rot = lambda b: b[:, :].rearrange("p (a b) -> p a b", a=2)
            bc = lambda k: K[k][:, None, :].to_broadcast([P, 2, T])
            rt = ropeT[:, :].rearrange("p (a b) -> p a b", a=2)
            for buf, b in ((mlQ[:, :, :], bank[4]), (mlK[:, :, 0:T], bank[5])):
                link(dve.tensor_tensor(rt, rot(b), bc("sin1"), ALU.mult))
                link(dve.tensor_tensor(buf, buf, bc("cos1"), ALU.mult))
                link(dve.tensor_tensor(buf, buf, rt, ALU.add))
            dve.memset(stage[:, 61:62], 0.0).then_inc(ml_rope, 1)
            dve.wait_ge(g_cum, 1)
            cum = bank[6][:, 0:32].rearrange("p (t d h) -> p t d h", t=4, d=2)
            for dr in range(2):
                ins = dve.tensor_tensor(keyb[:, :, 4 * dr:4 * dr + 4], gf[:, :, dr, 0, :], cum[:, :, dr, :], ALU.subtract)
            link(ins)
            dve.memset(stage[:, 61:62], 0.0).then_inc(g_keyb, 1)

            for b in range(7):
                n = min(10, 64 - 10 * b)
                dve.wait_ge(rel_done, b + 1)
                dve.tensor_copy(bias[:, :, 10 * b:10 * b + n],
                                bank[4 + b % 2][:, 0:48 * n].rearrange("p (k x) -> p x k", k=n)).then_inc(rel_copied, 1)

            def front(i):
                h, qt = divmod(i, 2)
                e0 = 2 - 2 * qt
                dve.wait_ge(na_s, i + 1)
                b = bank[4 + i % 2]
                loc = b[:, 0:T].rearrange("p (a b) -> p a b", a=4)
                link(dve.tensor_tensor(loc, loc, bias[:, 6 * h + e0:6 * h + e0 + 4, :], ALU.add))
                link(dve.tensor_reduce(nst[:, 16 + i:17 + i], b[:, :], AX.X, ALU.max))
                dve.tensor_scalar(nst[:, i:i + 1], nst[:, 16 + i:17 + i], -1.0, None, ALU.mult).then_inc(na_max, 1)

            front(0)
            for i in range(2 * NA_H):
                h, qt = divmod(i, 2)
                if i + 1 < 2 * NA_H:
                    front(i + 1)
                if i >= 8:
                    modulation(i - 4)
                dve.wait_ge(na_exp, i + 1)
                link(dve.reciprocal(nst[:, 32 + i:33 + i], nst[:, 32 + i:33 + i]))
                dve.tensor_scalar(Pna[:, i % 2, :], Pna[:, i % 2, :], nst[:, 32 + i:33 + i], None, ALU.mult).then_inc(na_p, 1)
                if qt:
                    r = 64 * (h % 2)
                    dve.wait_ge(na_o, h + 1)
                    dve.tensor_copy(oNaT[r:r + 64, h // 2, :], bank[7][r:r + 64, 0:T]).then_inc(na_os, 1)

            for h in range(ML_H):
                for dr in range(2):
                    i = 2 * h + dr
                    dve.wait_ge(ml_b, h + 1)
                    if i >= 2:
                        dve.wait_ge(ml_w, i - 1)
                    mask = K["maskf" if dr == 0 else "maskb"][:, None, :].to_broadcast([P, 2, P])
                    dve.tensor_tensor(ropeT[:, dr * T:dr * T + T].rearrange("p (a b) -> p a b", a=2),
                                      bank[6][:, dr * T:dr * T + T].rearrange("p (a b) -> p a b", a=2),
                                      mask, ALU.add).then_inc(ml_bm, 1)
                g = G1[f"b_na{h}"]
                dve.wait_ge(lin_done, g + 1)
                if h == 0:
                    dve.wait_ge(lin_act, emptied(G1["gml3"])[1])
                dve.tensor_tensor(merged[:, 2 * h:2 * h + 2, :], bank[g % 4][:, :].rearrange("p (a b) -> p a b", a=2),
                                  gNA[:, 2 * h:2 * h + 2, :], ALU.mult).then_inc(lin_dve, 1)
                for dr in range(2):
                    i = 2 * h + dr
                    w = wml[:, i % 2, :]
                    dve.wait_ge(ml_w, i + 1)
                    dve.wait_ge(ml_s, h + 1)
                    S = lambda tt, a, b: bank[4 + tt // 2][:, (tt % 2) * T + a:(tt % 2) * T + b]
                    dve.tensor_tensor(w[:, 0:256], w[:, 0:256], S(2, 0, T), ALU.mult)
                    dve.tensor_tensor(w[:, 256:512], w[:, 256:512], S(3, 0, T), ALU.mult)
                    dve.tensor_tensor(w[:, 512:640], w[:, 512:640], S(0, 0, 128), ALU.mult)
                    dve.tensor_tensor(w[:, 640:768], w[:, 640:768], S(1, 128, 256), ALU.mult)
                    far = S(0, 128, 256) if dr == 0 else S(1, 0, 128)
                    dve.tensor_tensor(w[:, 768:896], w[:, 768:896], far, ALU.mult).then_inc(ml_p, 1)
                for dr in range(2):
                    i = 2 * h + dr
                    dve.wait_ge(ml_o, i + 1)
                    for qt in range(2):
                        dst = hml[:, qt, h * P:(h + 1) * P]
                        num = bank[7][:, 129 * qt:129 * qt + 128]
                        den = bank[7][:, 129 * qt + 128:129 * qt + 129]
                        q = nst[:, 48 + qt:49 + qt]
                        link(dve.tensor_scalar(q, den, 1.0, None, ALU.max))
                        link(dve.scalar_tensor_tensor(out=q, in0=den, scalar=-1.0, in1=q, op0=ALU.mult, op1=ALU.max))
                        link(dve.reciprocal(q, q))
                        if dr == 0:
                            link(dve.tensor_scalar(dst, num, q, None, ALU.mult))
                        else:
                            link(dve.scalar_tensor_tensor(out=dst, in0=num, scalar=q, in1=dst, op0=ALU.mult, op1=ALU.add))
                    dve.memset(stage[:, 61:62], 0.0).then_inc(ml_os, 1)
                for qt in range(2):
                    dst = hml[:, qt, h * P:(h + 1) * P]
                    link(dve.tensor_tensor(rstd[:, 0:P], dst, dst, ALU.mult))
                    link(dve.tensor_reduce(nst[:, 56 + 2 * h + qt:57 + 2 * h + qt], rstd[:, 0:P], AX.X, ALU.add))
            ms = nst[:, 56:64]
            dve.tensor_scalar(ms, ms, 1.0 / ML_V, EPS, ALU.mult, ALU.add).then_inc(ms_done, 1)
            dve.wait_ge(root_done, 2)
            link(dve.reciprocal(ms, ms))
            for h in range(ML_H):
                for qt in range(2):
                    dst = hml[:, qt, h * P:(h + 1) * P]
                    ins = dve.tensor_scalar(dst, dst, ms[:, 2 * h + qt:2 * h + qt + 1], None, ALU.mult)
                ins.then_inc(ml_hn, 1)
            gh = VECS1["g_mlstm_head"][0]
            for h in range(ML_H):
                dve.wait_ge(ml_ht, h + 1)
                dve.scalar_tensor_tensor(out=oMlT[:, h, :], in0=bank[4 + h % 2][:, 0:T], scalar=vT[:, gh + h:gh + h + 1],
                                         in1=mlO[:, h, :], op0=ALU.mult, op1=ALU.mult).then_inc(ml_hts, 1)
            for m in range(4):
                g = G1[f"b_ml{m}"]
                dve.wait_ge(lin_done, g + 1)
                gm = gML[:, 2 * m:2 * m + 2, :]
                link(dve.tensor_tensor(gm, bank[g % 4][:, :].rearrange("p (a b) -> p a b", a=2), gm, ALU.mult))
                dve.tensor_tensor(merged[:, 2 * m:2 * m + 2, :], merged[:, 2 * m:2 * m + 2, :], gm, ALU.add).then_inc(lin_dve, 1)
            def norm(k):
                dve.wait_ge(n_sum, k + 1)
                dve.tensor_scalar(ncol[:, :], bank[6][:, 0:2], 1.0 / D, EPS, ALU.mult, ALU.add).then_inc(n_ms, 1)
                dve.wait_ge(n_root, k + 1)
                dve.reciprocal(ncol[:, :], ncol[:, :]).then_inc(n_col, 1)
                dve.wait_ge(n_row, k + 1)

            row = bank[7][:, 0:T]

            def residual(src):
                for k in (0, 4):
                    for c in range(k, k + 4):
                        ins = dve.scalar_tensor_tensor(out=tmpx[:, c, :], in0=src[:, c, :], scalar=gpost[:, c:c + 1], in1=row,
                                                       op0=ALU.mult, op1=ALU.mult)
                    link(ins)
                    dve.tensor_tensor(xT[:, k:k + 4, :], xT[:, k:k + 4, :], tmpx[:, k:k + 4, :], ALU.add).then_inc(x_done, 4)

            dve.wait_ge(pos_in, 16)
            link(dve.tensor_copy(posf, posi.bitcast(I32)))
            link(dve.tensor_scalar(ang, posf, K["invfreq"][:, 0:1], None, ALU.mult))
            link(dve.tensor_scalar(kf, ang, float(1 / (2 * np.pi)), MAGIC, ALU.mult, ALU.add))
            link(dve.tensor_scalar(kf, kf, -MAGIC, None, ALU.add))
            for part in TURN:
                link(dve.scalar_tensor_tensor(out=ang, in0=kf, scalar=-part, in1=ang, op0=ALU.mult, op1=ALU.add))
            link(dve.tensor_scalar(ang, ang, PI_IN, -PI_IN, ALU.min, ALU.max))
            link(dve.tensor_scalar(kf, ang, float(np.pi / 2), None, ALU.add))
            link(dve.tensor_scalar(posf, kf, PI_IN, float(-2 * np.pi), ALU.is_gt, ALU.mult))
            link(dve.tensor_tensor(kf, kf, posf, ALU.add))
            dve.tensor_scalar(kf, kf, PI_IN, -PI_IN, ALU.min, ALU.max).then_inc(c_pos, 1)
            dve.tensor_tensor(gpost[:, :], mod[:, 16:24], vcol("g_mix_post"), ALU.mult)
            dve.scalar_tensor_tensor(out=gpre[:, :], in0=mod[:, 32:40], scalar=1.0, in1=vcol("g_ffn_pre"), op0=ALU.add, op1=ALU.mult)
            norm(0)
            residual(mixT)
            norm(1)
            dve.wait_ge(x_done, DC)
            for c in range(DC):
                dve.tensor_tensor(tmpx[:, c, :], xT[:, c, :], row, ALU.mult).then_inc(n_xn, 1)
            dve.wait_ge(rt_log, 1)
            dve.wait_ge(moe_const, 16 * 5)
            link(dve.tensor_tensor(logits, bank[7][:, 0:TT * E].rearrange("p (a b) -> p a b", a=TT),
                                   brow[:, None, :].to_broadcast([P, TT, E]), ALU.add))
            for t in range(TT):
                link(dve.max(top[:, t, :], logits[:, t, :]))
            for t in range(TT):
                ins = dve.tensor_scalar(rcol[:, t:t + 1], top[:, t, 0:1], -1.0, None, ALU.mult)
            ins.then_inc(rt_top, 1)
            for t in range(TT):
                link(dve.max_index(topi[:, t, :].bitcast(U32), top[:, t, :], logits[:, t, :]))
                link(dve.tensor_copy(topf[:, t, :], topi[:, t, :].bitcast(U32)))
            io = K["iota"][:, 0:E]
            for t in range(TT):
                link(dve.tensor_scalar(chosen[:, t, :], io, topf[:, t, 0:1], None, ALU.is_equal))
                for k in range(1, TOPK):
                    link(dve.scalar_tensor_tensor(out=chosen[:, t, :], in0=io, scalar=topf[:, t, k:k + 1], in1=chosen[:, t, :],
                                                  op0=ALU.is_equal, op1=ALU.add))
            dve.memset(stage[:, 61:62], 0.0).then_inc(rt_sel, 1)
            dve.wait_ge(rt_exp, 1)
            link(dve.reciprocal(rcol[:, 4:6], rcol[:, 2:4]))
            for t in range(TT):
                link(dve.tensor_scalar(topp[:, t, 0:TOPK], topp[:, t, 0:TOPK], rcol[:, 4 + t:5 + t], None, ALU.mult))
                link(dve.tensor_scalar(weight[:, t, :], io, topf[:, t, 0:1], topp[:, t, 0:1], ALU.is_equal, ALU.mult))
                for k in range(1, TOPK):
                    link(dve.tensor_scalar(tmpe[:, t, :], io, topf[:, t, k:k + 1], topp[:, t, k:k + 1], ALU.is_equal, ALU.mult))
                    link(dve.tensor_tensor(weight[:, t, :], weight[:, t, :], tmpe[:, t, :], ALU.add))
            dve.memset(stage[:, 61:62], 0.0).then_inc(rt_sel, 1)
            dve.wait_ge(rt_cnt, 1)
            cnt = bank[5][:, 0:2 * E].rearrange("p (a b) -> p a b", a=TT)
            link(dve.tensor_tensor(place0, cnt, chosen, ALU.mult))
            dve.memset(place[:, :, MAXPASS * E:], -1.0)
            for p in range(MAXPASS):
                link(dve.tensor_scalar(place[:, :, p * E:(p + 1) * E], place0, float(-1 - SLOTS * p), None, ALU.add))
            link(dve.tensor_reduce(rcol[:, 8:9], bank[5][:, 2 * E:3 * E], AX.X, ALU.max))
            link(dve.tensor_scalar(rcol[:, 9:10], rcol[:, 8:9], SLOTS + 0.5, 1.0, ALU.is_ge, ALU.add))
            for p in range(2, MAXPASS):
                link(dve.tensor_scalar(rcol[:, 10:11], rcol[:, 8:9], SLOTS * p + 0.5, None, ALU.is_ge))
                link(dve.tensor_tensor(rcol[:, 9:10], rcol[:, 9:10], rcol[:, 10:11], ALU.add))
            dve.tensor_copy(npass_sb[:, :], rcol[:, 9:10]).then_inc(npass_set, 1)
            for g in range(4):
                dve.wait_ge(acc_ps, g + 1)
                dve.tensor_copy(accT[:, 2 * g:2 * g + 2, :], two(bank[g][:, :])).then_inc(moe_add, 1)

            dve.wait_ge(npass_set, 1)
            npass = dve.value_load(npass_sb[0:1, 0:1], min_val=1, max_val=MAXPASS)
            for t in range(TT):
                ins = dve.tensor_scalar(selS[:, 0, t, :], K["iota"][:, 0:SLOTS], place[:, t, 0:1], None, ALU.is_equal)
            ins.then_inc(moe_sel, 1)
            with dve.Fori(0, npass) as p:
                with dve.Fori(0, E // 2) as j:
                    it = dve.snap(p * (E // 2) + j)
                    e2 = dve.snap(j * 2)
                    n2 = dve.snap(p * E + j * 2)
                    dve.wait_ge(moe_x, it * 2 + 1)
                    for a in range(2):
                        for t in range(TT):
                            dve.tensor_scalar(selS[:, 1 - a, t, :], K["iota"][:, 0:SLOTS], place[:, t, bass.DynSlice(n2 + (a + 1), 1)],
                                              None, ALU.is_equal)
                            dve.tensor_scalar(selW[:, t, a * SLOTS:(a + 1) * SLOTS], K["iota"][:, 0:SLOTS],
                                              place[:, t, bass.DynSlice(n2 + a, 1)],
                                              weight[:, t, bass.DynSlice(e2 + a, 1)], ALU.is_equal, ALU.mult)
                        ins = dve.tensor_copy(expertSel[0:E, a, :], K["ident"][0:E, bass.DynSlice(e2 + a, 1)].to_broadcast([E, SLOTS]))
                    ins.then_inc(moe_sel, 1)
                    for a in range(2):
                        n = it * 2 + a
                        dve.wait_ge(moe_used, n * 6 + 2)
                        dve.tensor_scalar(eg, bank[3][:, :], LIMIT, None, ALU.min).then_inc(moe_g2, 1)
                        dve.wait_ge(moe_used, n * 6 + 4)
                        dve.tensor_scalar(el, bank[4][:, :], LIMIT, -LIMIT, ALU.min, ALU.max).then_inc(moe_l2, 1)
                        dve.wait_ge(moe_l2, n + 1)
                        dve.scalar_tensor_tensor(out=el, in0=el, scalar=1.0, in1=eg, op0=ALU.add, op1=ALU.mult).then_inc(moe_l3, 1)
                        dve.wait_ge(moe_l3, n + 1)
                        dve.wait_ge(moe_sig, n + 1)
                        dve.tensor_tensor(ea, el, es, ALU.mult).then_inc(moe_a, 1)
                    dve.wait_ge(moe_add, it * 4 + 4)
                    for g in range(4):
                        dve.wait_ge(moe_sc, it * 4 + (g + 1))
                        dve.tensor_tensor(accT[:, 2 * g:2 * g + 2, :], accT[:, 2 * g:2 * g + 2, :],
                                          two(bank[6 + g % 2][:, :]), ALU.add).then_inc(moe_add, 1)
            dve.tensor_tensor(gpost[:, :], mod[:, 40:48], vcol("g_ffn_post"), ALU.mult)
            norm(2)
            residual(accT)
            dve.memset(glaP[64:128, :, :], 0.0)
            with dve.Fori(0, 2) as L:
                steps = [0]

                def link(ins):
                    steps[0] += 1
                    ins.then_inc(c_chain, 1)
                    dve.wait_ge(c_chain, L * LINKS + steps[0])

                def residual(src, n):
                    for k in (0, 4):
                        for c in range(k, k + 4):
                            ins = dve.scalar_tensor_tensor(out=tmpx[:, c, :], in0=src[:, c, :], scalar=gpost[:, c:c + 1], in1=row,
                                                           op0=ALU.mult, op1=ALU.mult)
                        link(ins)
                        dve.tensor_tensor(xT[:, k:k + 4, :], xT[:, k:k + 4, :], tmpx[:, k:k + 4, :], ALU.add).then_inc(x_done, 4)

                link(dve.tensor_copy(v2c[:, :], v2T[:, :].rearrange("p (l n) -> p l n", l=2)[:, bass.DynSlice(L, 1), :]
                                     .rearrange("p l n -> p (l n)")))
                norm(L * 4 + 3)
                dve.wait_ge(x_done, L * (2 * DC) + 2 * DC)
                for c in range(DC):
                    dve.scalar_tensor_tensor(out=hT[:, c, :], in0=xT[:, c, :], scalar=V2("norm_mix_pre_2")[:, c:c + 1], in1=row,
                                             op0=ALU.mult, op1=ALU.mult).then_inc(c_h, 1)
                dve.wait_ge(*emptied2(G2["cc_1"], L))
                cw = V2("conv_w_2")
                link(dve.tensor_tensor(convU, convU, convC, ALU.mult))
                for c in range(4):
                    link(dve.tensor_scalar(yA[:, c, :], convU[:, c, :], cw[:, 8 + c:9 + c], None, ALU.mult))
                    link(dve.scalar_tensor_tensor(out=yA[:, c, 1:T], in0=convU[:, c, 0:T - 1], scalar=cw[:, 4 + c:5 + c],
                                                  in1=yA[:, c, 1:T], op0=ALU.mult, op1=ALU.add))
                    link(dve.scalar_tensor_tensor(out=yA[:, c, 2:T], in0=convU[:, c, 0:T - 2], scalar=cw[:, c:c + 1],
                                                  in1=yA[:, c, 2:T], op0=ALU.mult, op1=ALU.add))
                dve.tensor_tensor(yA, yA, convB, ALU.mult).then_inc(c_conv, 1)
                dve.wait_ge(c_sin, 1)
                dve.wait_ge(c_rot, L + 1)
                tr = at(13840, 4, T)
                for buf, b0 in ((retQ, 4), (retK, 6)):
                    for k in range(2):
                        link(dve.tensor_tensor(tr[:, 2 * k:2 * k + 2, :], two(bank[b0 + k][:, :]), sin2[:, None, :].to_broadcast([P, 2, T]), ALU.mult))
                    link(dve.tensor_tensor(buf, buf, cos2[:, None, :].to_broadcast([P, 4, T]), ALU.mult))
                    ins = dve.tensor_tensor(buf, buf, tr, ALU.add)
                    if b0 == 4:
                        link(ins)
                ins.then_inc(c_rope, 1)
                dve.wait_ge(c_lg, L + 1)
                for m in range(2):
                    ins = dve.tensor_scalar(lgt[:, m, :], bank[4][:, m * T:(m + 1) * T], V2("gla_b_a_2")[:, m:m + 1], None, ALU.add)
                link(ins)
                dve.scalar_tensor_tensor(out=lab, in0=lgt, scalar=-1.0, in1=lgt, op0=ALU.mult, op1=ALU.max).then_inc(c_abs, 1)
                dve.wait_ge(c_ln, L + 1)
                link(dve.scalar_tensor_tensor(out=lgt, in0=lgt, scalar=0.0, in1=lln, op0=ALU.min, op1=ALU.subtract))
                for m in range(2):
                    link(dve.tensor_tensor_scan(glaCum[:, m, :], ones[:, :], lgt[:, m, :], 0.0, ALU.mult, ALU.add))
                mid = glaCum.rearrange("p m (b k) -> p m b k", k=64)[:, :, :, 31]
                dve.tensor_scalar(glaNeg, mid, -1.0 / TAU, None, ALU.mult)
                dve.tensor_scalar(glaPos, mid, 1.0 / TAU, None, ALU.mult).then_inc(c_cum, 1)
                dve.wait_ge(c_const, 32)
                for h in range(RH):
                    dve.wait_ge(r_s, L * 4 + (h + 1))
                    if h >= 2:
                        dve.wait_ge(r_o, L * 8 + (h - 1))
                    b = bank[4 + h % 2]
                    dve.tensor_tensor(retP[:, h % 2, 0:T], b[:, 0:T], retmask[:, h, :], ALU.mult)
                    dve.tensor_tensor(retP[:, h % 2, T:T + P], b[:, T:T + P], retmask[:, h, 0:P], ALU.mult).then_inc(r_p, 1)

                def heads(k, y, gain, gate_):
                    dve.wait_ge(h_sum, L * 2 + (k + 1))
                    dve.tensor_scalar(hcol, bank[7][:, 256:264], 1.0 / P, EPS, ALU.mult, ALU.add).then_inc(h_ms, 1)
                    dve.wait_ge(h_root, L * 2 + (k + 1))
                    dve.reciprocal(hcol, hcol).then_inc(h_col, 1)
                    dve.wait_ge(h_row, L * 2 + (k + 1))
                    for m in range(2):
                        link(dve.tensor_tensor(headY[:, 2 * m:2 * m + 2, :], headY[:, 2 * m:2 * m + 2, :], two(bank[4 + m][:, :]), ALU.mult))
                    for h in range(4):
                        ins = dve.scalar_tensor_tensor(out=y[:, h, :], in0=headY[:, h, :], scalar=gain[:, h:h + 1], in1=gate_[:, h, :],
                                                       op0=ALU.mult, op1=ALU.mult)
                    ins.then_inc(h_y, 1)

                heads(0, yB, V2("ret_gn_w_2"), retG)
                for m in range(2):
                    for b in range(4):
                        k = 4 * m + b
                        w = T - 64 * b
                        dve.wait_ge(l_e, L * 8 + (k + 1))
                        dve.tensor_tensor(glaEq[:, k % 2, 0:w], glaEq[:, k % 2, 0:w], glaQ[:, m, 64 * b:T], ALU.mult)
                        dve.tensor_tensor(glaEk[:, k % 2, :], glaEk[:, k % 2, :], glaK[:, m, 64 * b:64 * b + 64], ALU.mult).then_inc(l_q, 1)
                    dve.wait_ge(l_s, L * 8 + (4 * m + 4))
                    for hh in range(2):
                        if m:
                            dve.wait_ge(r_o, L * 8 + (5 + hh))
                        for b in range(4):
                            w = T - 64 * b
                            col = 64 * b if b < 2 else T + 64 * (b - 2)
                            r = 64 * (b % 2)
                            c0 = 64 * (b % 2)
                            ins = dve.tensor_tensor(glaP[r:r + 64, hh, col:col + w], bank[4 + hh][r:r + 64, col:col + w],
                                                    K["tri"][r:r + 64, c0:c0 + w], ALU.mult)
                        ins.then_inc(l_p, 1)
                heads(1, yC, V2("gla_gn_w_2"), glaR)
                for x, g_ in (("a", gateA), ("b", gateB), ("c", gateC)):
                    for i in range(4):
                        g = G2[f"br{x}_{i}"]
                        dve.wait_ge(*made2(f"br{x}_{i}", L))
                        mg = mergedC[:, 2 * i:2 * i + 2, :]
                        gg = g_[:, 2 * i:2 * i + 2, :]
                        if x == "a":
                            if i == 0:
                                dve.wait_ge(*emptied2(G2["gatec_3"], L))
                            dve.tensor_tensor(mg, two(bank[g % 4][:, :]), gg, ALU.mult).then_inc(c_dve, 1)
                        else:
                            link(dve.tensor_tensor(gg, two(bank[g % 4][:, :]), gg, ALU.mult))
                            dve.tensor_tensor(mg, mg, gg, ALU.add).then_inc(c_dve, 1)
                link(dve.tensor_copy(gpost[:, :], V2("norm_mix_post_2")))
                norm(L * 4 + 4)
                residual(mixC, 0)
                norm(L * 4 + 5)
                dve.wait_ge(x_done, L * (2 * DC) + 3 * DC)
                for c in range(DC):
                    dve.scalar_tensor_tensor(out=hLo[:, c, :], in0=xT[:, c, :], scalar=V2("norm_ffn_pre_2")[:, c:c + 1], in1=row,
                                             op0=ALU.mult, op1=ALU.mult).then_inc(c_h, 1)
                for k in (0, 4):
                    dve.wait_ge(f_hi, L * (DC + NHID) + (k + 4))
                    dve.tensor_tensor(hL[:, k:k + 4, :], hLo[:, k:k + 4, :], hH[:, k:k + 4, :].bitcast(F32), ALU.subtract)\
                        .then_inc(f_lo, 1)

                def hidden_rest(i):
                    dve.wait_ge(f_hi, L * (DC + NHID) + (DC + i + 1))
                    c = slice(2 * i, 2 * i + 2)
                    dve.tensor_tensor(fL[:, c, :], fLo[:, c, :], fH[:, c, :].bitcast(F32), ALU.subtract).then_inc(f_lo, 1)

                for i in range(11):
                    g = G2[f"fu_{i}"]
                    dve.wait_ge(*made2(f"fu_{i}", L))
                    dve.wait_ge(*emptied2(G2[f"fg_{i}"], L))
                    dve.tensor_tensor(fLo[:, 2 * i:2 * i + 2, :], two(bank[g % 4][:, :]), two(fS[:, i % 4, :]), ALU.mult).then_inc(c_dve, 1)
                    if i >= 2:
                        hidden_rest(i - 2)
                hidden_rest(9)
                hidden_rest(10)
                link(dve.tensor_copy(gpost[:, :], V2("norm_ffn_post_2")))
                norm(L * 4 + 6)
                residual(ffT, 0)
                assert steps[0] == LINKS, steps[0]
            for g in range(4):
                dve.wait_ge(fin_t, 2 + g + 1)
                dve.tensor_copy(outN[:, g // 2, (g % 2) * 512:(g % 2 + 1) * 512], bank[g][:, :]).then_inc(fin_c, 1)

        @block.gpsimd
        def _(pool):
            pool.wait_ge(ones_set, 1)
            src = A["rpb"][0].rearrange("h r d -> d h r")
            with nc.allow_non_contiguous_dma(reason="a small table turned"):
                for a in range(2):
                    for h in range(NA_H):
                        pool.dma_start(relrhs[31 * a:31 * a + 31, 6 * h:6 * h + 6], src[:, h, 5 - a:11 - a])\
                            .then_inc(relrhs_in, 16)
                pool.dma_start(bg[:, :], A["b_mlstm_gates"][0].rearrange("a b -> (a b)").partition_broadcast(P)).then_inc(bg_in, 16)
            pool.wait_ge(x_done, 2 * DC)
            for L in range(2):
                if L:
                    pool.wait_ge(c_lg, L)
                pool.dma_start(wa2[0:GR, :], A["gla_w_a2_2"][L]).then_inc(c_wa2, 16)
            with pool.Fori(0, 2) as L:
                for k, name in enumerate(SPLIT):
                    w, hi = place2(name), place2(name + "_hi", ringR).bitcast(F32)
                    n = w.shape[1]
                    for h, (a, b) in enumerate(((0, n // 2), (n // 2, n))):
                        pool.wait_ge(w_hi, L * (2 * NSPLIT) + (2 * k + h + 1))
                        pool.tensor_tensor(place2(name, ringR)[:, a:b, :], w[:, a:b, :], hi[:, a:b, :], ALU.subtract).then_inc(w_lo, 1)


def kernel(**inputs):
    import numpy as _np
    import concourse.bacc as _bacc
    from concourse.bass_utils import run_bass_kernel_spmd as _run

    nc = _bacc.Bacc("TRN2", target_bir_lowering=False, num_devices=1)
    arrays, aps = {}, {}
    for name, a in list(inputs.items()) + list(constants().items()):
        a = _np.ascontiguousarray(a)
        arrays[f"in_{name}"] = a
        aps[name] = nc.dram_tensor(f"in_{name}", a.shape, mybir.dt.from_np(a.dtype), kind="ExternalInput").ap()
    out = nc.dram_tensor("out_0", (1, T, D), F32, kind="ExternalOutput").ap()
    build(nc, aps, out)
    r = _run(nc, [arrays], core_ids=[0])
    return r.results[0]["out_0"]
```
